# Optimizing a Trainium2 kernel written in Bass

```python
import math
import jax, jax.numpy as jnp
from jax import lax
import numpy as np

D_MODEL = 1024
BATCH = 1
SEQ = 256
DEPTH = 4

CHUNK = 64
N_MIXERS = 3
ALPHA = (2.0 * DEPTH) ** 0.25
BETA = (8.0 * DEPTH) ** -0.25
LN_EPS = 1e-5
RMS_EPS = 1e-5
N_SSD_LAYERS = (DEPTH + 2) // 3
N_SWA_LAYERS = (DEPTH + 1) // 3
N_CA_LAYERS = DEPTH // 3

SSD_D_INNER = 2 * D_MODEL
SSD_HEAD_DIM = 64
SSD_N_HEADS = SSD_D_INNER // SSD_HEAD_DIM
SSD_N_GROUPS = 4
SSD_HEADS_PER_GROUP = SSD_N_HEADS // SSD_N_GROUPS
SSD_D_STATE = 128
SSD_CONV = 4
SSD_CONV_DIM = SSD_D_INNER + 2 * SSD_N_GROUPS * SSD_D_STATE
SSD_IN_DIM = SSD_D_INNER + SSD_CONV_DIM + SSD_N_HEADS

SWA_N_HEADS = 16
SWA_N_KV_HEADS = 4
SWA_HEAD_DIM = D_MODEL // SWA_N_HEADS
SWA_GROUP = SWA_N_HEADS // SWA_N_KV_HEADS
SWA_WINDOW = 128
SWA_BAND_CHUNKS = SWA_WINDOW // CHUNK
SWA_IN_DIM = (SWA_N_HEADS + 2 * SWA_N_KV_HEADS) * SWA_HEAD_DIM

CA_N_HEADS = 16
CA_HEAD_DIM = D_MODEL // CA_N_HEADS
CA_PREV_CHUNKS = 8
CA_BAND = (CA_PREV_CHUNKS + 1) * CHUNK
CA_REL_CLIP = 128
CA_N_REL = (CHUNK - 1) + CA_REL_CLIP + 1

MOE_N_EXPERTS = 16
MOE_N_GROUPS = 4
MOE_EXPERTS_PER_GROUP = MOE_N_EXPERTS // MOE_N_GROUPS
MOE_TOP_K = 2
MOE_D_FF = D_MODEL // 4

kernel_name = "hybrid_ssd_swa_chunkattn_moe_deepnorm"

def layer_norm(x, g, b):
    xf = x.astype(jnp.float32)
    mu = jnp.mean(xf, axis=-1, keepdims=True)
    xc = xf - mu
    var = jnp.mean(xc * xc, axis=-1, keepdims=True)
    return (xc * lax.rsqrt(var + LN_EPS) * g + b).astype(x.dtype)

def alibi_slopes(n_heads):
    return jnp.exp2(-8.0 * jnp.arange(1, n_heads + 1, dtype=jnp.float32) / n_heads)

def ssd_mixer(x, w_in, conv_w, conv_b, dt_bias, a_log, d_skip, norm_w, w_out):
    b, s, _ = x.shape
    nc = s // CHUNK
    G, R, P, N = SSD_N_GROUPS, SSD_HEADS_PER_GROUP, SSD_HEAD_DIM, SSD_D_STATE
    f32 = jnp.float32
    proj = x @ w_in
    z, xbc, dt_raw = jnp.split(proj, [SSD_D_INNER, SSD_D_INNER + SSD_CONV_DIM], axis=-1)
    xbc = lax.conv_general_dilated(
        xbc, conv_w[:, None, :], window_strides=(1,), padding=[(SSD_CONV - 1, 0)],
        dimension_numbers=("NWC", "WIO", "NWC"), feature_group_count=SSD_CONV_DIM)
    xbc = jax.nn.silu(xbc + conv_b)
    xs, bs, cs = jnp.split(xbc, [SSD_D_INNER, SSD_D_INNER + G * N], axis=-1)
    xs = xs.reshape(b, s, G, R, P)
    bs = bs.reshape(b, s, G, N).astype(f32)
    cs = cs.reshape(b, s, G, N).astype(f32)
    dt = jax.nn.softplus(dt_raw.astype(f32) + dt_bias.astype(f32))
    a = -jnp.exp(a_log.astype(f32))
    da = (dt * a).reshape(b, nc, CHUNK, G, R)
    acs = jnp.transpose(jnp.cumsum(da, axis=2), (1, 0, 3, 4, 2))
    xdt = xs.astype(f32) * dt.reshape(b, s, G, R)[..., None]

    def to_chunks(t):
        return jnp.moveaxis(t.reshape((b, nc, CHUNK) + t.shape[2:]), 1, 0)

    causal = jnp.tril(jnp.ones((CHUNK, CHUNK), dtype=bool))

    def step(h, inp):
        xc, bc, cc, ac = inp
        seg = ac[..., :, None] - ac[..., None, :]
        decay_in = jnp.exp(jnp.where(causal, seg, -jnp.inf))
        cb = jnp.einsum("blgn,bsgn->bgls", cc, bc)
        y_diag = jnp.einsum("bgls,bgrls,bsgrp->blgrp", cb, decay_in, xc)
        y_off = jnp.einsum("blgn,bgrpn,bgrl->blgrp", cc, h, jnp.exp(ac))
        decay_out = jnp.exp(ac[..., -1:] - ac)
        h_new = h * jnp.exp(ac[..., -1])[..., None, None] + jnp.einsum(
            "blgn,bgrl,blgrp->bgrpn", bc, decay_out, xc)
        return h_new, y_diag + y_off

    h0 = jnp.zeros((b, G, R, P, N), f32)
    _, ys = lax.scan(step, h0, (to_chunks(xdt), to_chunks(bs), to_chunks(cs), acs))
    y = jnp.moveaxis(ys, 0, 1).reshape(b, s, G, R, P)
    y = y + xs.astype(f32) * d_skip.astype(f32).reshape(G, R)[:, :, None]
    y = y.reshape(b, s, SSD_D_INNER) * jax.nn.silu(z.astype(f32))
    yg = y.reshape(b, s, G, SSD_D_INNER // G)
    yg = yg * lax.rsqrt(jnp.mean(yg * yg, axis=-1, keepdims=True) + RMS_EPS)
    y = (yg.reshape(b, s, SSD_D_INNER) * norm_w).astype(x.dtype)
    return y @ w_out

def swa_mixer(x, w_in, sinks, w_out):
    b, s, _ = x.shape
    nc = s // CHUNK
    H, KV, GRP, Dh = SWA_N_HEADS, SWA_N_KV_HEADS, SWA_GROUP, SWA_HEAD_DIM
    BC = SWA_BAND_CHUNKS
    f32 = jnp.float32
    q, k, v = jnp.split(x @ w_in, [H * Dh, (H + KV) * Dh], axis=-1)
    q = q.reshape(b, nc, CHUNK, KV, GRP, Dh)
    k = k.reshape(b, nc, CHUNK, KV, Dh)
    v = v.reshape(b, nc, CHUNK, KV, Dh)

    def band(t):
        parts = [jnp.pad(t, ((0, 0), (n, 0), (0, 0), (0, 0), (0, 0)))[:, :nc]
                 for n in range(BC - 1, -1, -1)]
        return jnp.concatenate(parts, axis=2)

    kb, vb = band(k), band(v)
    scores = jnp.einsum("bcqhgd,bckhd->bchgqk", q, kb).astype(f32) * (Dh ** -0.5)
    qi = jnp.arange(CHUNK)[:, None]
    kj = jnp.arange(BC * CHUNK)[None, :]
    dist = jnp.abs((BC - 1) * CHUNK + qi - kj).astype(f32)
    slopes = alibi_slopes(H).reshape(KV, GRP)
    scores = scores - slopes[:, :, None, None] * dist
    src_chunk = jnp.arange(nc)[:, None] - (BC - 1) + jnp.arange(BC * CHUNK)[None, :] // CHUNK
    valid = src_chunk >= 0
    scores = jnp.where(valid[None, :, None, None, None, :], scores, -jnp.inf)
    sink = jnp.broadcast_to(sinks.astype(f32).reshape(KV, GRP)[:, :, None, None],
                            scores.shape[:-1] + (1,))
    probs = jax.nn.softmax(jnp.concatenate([scores, sink], axis=-1), axis=-1)[..., :-1]
    out = jnp.einsum("bchgqk,bckhd->bcqhgd", probs.astype(v.dtype), vb)
    return out.reshape(b, s, H * Dh) @ w_out

def chunk_attn_mixer(x, w_in, rel_bias, w_out):
    b, s, _ = x.shape
    nc = s // CHUNK
    H, Dh = CA_N_HEADS, CA_HEAD_DIM
    f32 = jnp.float32
    q, k, v = jnp.split(x @ w_in, 3, axis=-1)
    q = q.reshape(b, s, H, Dh)
    k = k.reshape(b, s, H, Dh)
    v = v.reshape(b, s, H, Dh)
    pad = CA_PREV_CHUNKS * CHUNK
    k_pad = jnp.pad(k, ((0, 0), (pad, 0), (0, 0), (0, 0)))
    v_pad = jnp.pad(v, ((0, 0), (pad, 0), (0, 0), (0, 0)))
    qi = jnp.arange(CHUNK)[:, None]
    kj = jnp.arange(CA_BAND)[None, :]
    rel = jnp.clip(pad + qi - kj, -(CHUNK - 1), CA_REL_CLIP) + (CHUNK - 1)
    bias = rel_bias[:, rel].astype(f32)
    scale = Dh ** -0.5

    def one_chunk(c):
        start = c * CHUNK
        qc = lax.dynamic_slice_in_dim(q, start, CHUNK, axis=1)
        kc = lax.dynamic_slice_in_dim(k_pad, start, CA_BAND, axis=1)
        vc = lax.dynamic_slice_in_dim(v_pad, start, CA_BAND, axis=1)
        sc = jnp.einsum("bqhd,bkhd->bhqk", qc, kc).astype(f32) * scale + bias
        valid = jnp.arange(CA_BAND) >= (CA_PREV_CHUNKS - c) * CHUNK
        p = jax.nn.softmax(jnp.where(valid, sc, -jnp.inf), axis=-1)
        return jnp.einsum("bhqk,bkhd->bqhd", p.astype(vc.dtype), vc)

    out = lax.map(one_chunk, jnp.arange(nc))
    return jnp.moveaxis(out, 0, 1).reshape(b, s, H * Dh) @ w_out

def moe_ffn(x, router_w, router_bias, w_gate, w_up, w_down):
    b, s, d = x.shape
    f32 = jnp.float32
    t = x.reshape(b * s, d)
    scores = jax.nn.sigmoid((t @ router_w).astype(f32))
    sel = scores + router_bias.astype(f32)
    grp = sel.reshape(-1, MOE_N_GROUPS, MOE_EXPERTS_PER_GROUP)
    grp_score = jnp.sum(lax.top_k(grp, MOE_TOP_K)[0], axis=-1)
    best = jnp.argmax(grp_score, axis=-1)
    in_group = (jnp.arange(MOE_N_EXPERTS) // MOE_EXPERTS_PER_GROUP)[None, :] == best[:, None]
    _, idx = lax.top_k(jnp.where(in_group, sel, -jnp.inf), MOE_TOP_K)
    w = jnp.take_along_axis(scores, idx, axis=-1)
    w = w / jnp.sum(w, axis=-1, keepdims=True)
    gates = jnp.einsum("tk,tke->te", w, jax.nn.one_hot(idx, MOE_N_EXPERTS, dtype=f32)).astype(x.dtype)
    y = jnp.zeros_like(t)
    for e in range(MOE_N_EXPERTS):
        h = jax.nn.silu(t @ w_gate[e]) * (t @ w_up[e])
        y = y + gates[:, e:e + 1] * (h @ w_down[e])
    return y.reshape(b, s, d)

def setup_inputs(seed: int = 0) -> dict:
    key = jax.random.key(seed)
    ks = jax.random.split(key, 24)
    f32 = jnp.float32

    def nrm(k, shape, scale):
        return jax.random.normal(k, shape, f32) * scale

    dt = jnp.exp(jax.random.uniform(ks[4], (N_SSD_LAYERS, SSD_N_HEADS), f32,
                                    math.log(1e-3), math.log(1e-1)))
    return {
        "x": nrm(ks[0], (BATCH, SEQ, D_MODEL), 1.0),
        "ssd_w_in": nrm(ks[1], (N_SSD_LAYERS, D_MODEL, SSD_IN_DIM), D_MODEL ** -0.5),
        "ssd_conv_w": nrm(ks[2], (N_SSD_LAYERS, SSD_CONV, SSD_CONV_DIM), SSD_CONV ** -0.5),
        "ssd_conv_b": nrm(ks[3], (N_SSD_LAYERS, SSD_CONV_DIM), 0.02),
        "ssd_dt_bias": dt + jnp.log(-jnp.expm1(-dt)),
        "ssd_a_log": jnp.log(jax.random.uniform(ks[5], (N_SSD_LAYERS, SSD_N_HEADS), f32, 1.0, 16.0)),
        "ssd_d_skip": 1.0 + nrm(ks[6], (N_SSD_LAYERS, SSD_N_HEADS), 0.02),
        "ssd_norm_w": 1.0 + nrm(ks[7], (N_SSD_LAYERS, SSD_D_INNER), 0.02),
        "ssd_w_out": nrm(ks[8], (N_SSD_LAYERS, SSD_D_INNER, D_MODEL), SSD_D_INNER ** -0.5 * BETA),
        "swa_w_in": nrm(ks[9], (N_SWA_LAYERS, D_MODEL, SWA_IN_DIM), D_MODEL ** -0.5),
        "swa_sinks": nrm(ks[10], (N_SWA_LAYERS, SWA_N_HEADS), 0.5),
        "swa_w_out": nrm(ks[11], (N_SWA_LAYERS, SWA_N_HEADS * SWA_HEAD_DIM, D_MODEL),
                          (SWA_N_HEADS * SWA_HEAD_DIM) ** -0.5 * BETA),
        "ca_w_in": nrm(ks[12], (N_CA_LAYERS, D_MODEL, 3 * CA_N_HEADS * CA_HEAD_DIM), D_MODEL ** -0.5),
        "ca_rel_bias": nrm(ks[13], (N_CA_LAYERS, CA_N_HEADS, CA_N_REL), 0.5),
        "ca_w_out": nrm(ks[14], (N_CA_LAYERS, CA_N_HEADS * CA_HEAD_DIM, D_MODEL),
                         (CA_N_HEADS * CA_HEAD_DIM) ** -0.5 * BETA),
        "router_w": nrm(ks[15], (D_MODEL, MOE_N_EXPERTS), D_MODEL ** -0.5),
        "router_bias": nrm(ks[16], (MOE_N_EXPERTS,), 0.01),
        "moe_w_gate": nrm(ks[17], (DEPTH, MOE_N_EXPERTS, D_MODEL, MOE_D_FF), D_MODEL ** -0.5),
        "moe_w_up": nrm(ks[18], (DEPTH, MOE_N_EXPERTS, D_MODEL, MOE_D_FF), D_MODEL ** -0.5),
        "moe_w_down": nrm(ks[19], (DEPTH, MOE_N_EXPERTS, MOE_D_FF, D_MODEL), MOE_D_FF ** -0.5 * BETA),
        "ln_mix_g": 1.0 + nrm(ks[20], (DEPTH, D_MODEL), 0.02),
        "ln_mix_b": nrm(ks[21], (DEPTH, D_MODEL), 0.02),
        "ln_ffn_g": 1.0 + nrm(ks[22], (DEPTH, D_MODEL), 0.02),
        "ln_ffn_b": nrm(ks[23], (DEPTH, D_MODEL), 0.02),
    }

def reference(x, ssd_w_in, ssd_conv_w, ssd_conv_b, ssd_dt_bias, ssd_a_log, ssd_d_skip,
              ssd_norm_w, ssd_w_out, swa_w_in, swa_sinks, swa_w_out, ca_w_in, ca_rel_bias,
              ca_w_out, router_w, router_bias, moe_w_gate, moe_w_up, moe_w_down,
              ln_mix_g, ln_mix_b, ln_ffn_g, ln_ffn_b):
    for i in range(DEPTH):
        kind = i % N_MIXERS
        j = i // N_MIXERS
        if kind == 0:
            mix = ssd_mixer(x, ssd_w_in[j], ssd_conv_w[j], ssd_conv_b[j], ssd_dt_bias[j],
                            ssd_a_log[j], ssd_d_skip[j], ssd_norm_w[j], ssd_w_out[j])
        elif kind == 1:
            mix = swa_mixer(x, swa_w_in[j], swa_sinks[j], swa_w_out[j])
        else:
            mix = chunk_attn_mixer(x, ca_w_in[j], ca_rel_bias[j], ca_w_out[j])
        x = layer_norm(ALPHA * x + mix, ln_mix_g[i], ln_mix_b[i])
        ffn = moe_ffn(x, router_w, router_bias, moe_w_gate[i], moe_w_up[i], moe_w_down[i])
        x = layer_norm(ALPHA * x + ffn, ln_ffn_g[i], ln_ffn_b[i])
    return x


_drawn_inputs = setup_inputs


def setup_inputs(seed=0):
    import zlib

    import numpy as np

    out = dict(_drawn_inputs(seed))
    spreads = {}
    factors = {'swa_sinks': 5.064}
    for name, (base, spread) in spreads.items():
        noise = np.random.default_rng([zlib.crc32(name.encode()), seed]).standard_normal(out[name].shape)
        drawn = base * np.exp(spread * noise) if base else spread * noise
        out[name] = __import__('jax').numpy.asarray(drawn.astype(out[name].dtype))
    for name, factor in factors.items():
        out[name] = (out[name] * factor).astype(out[name].dtype)
    return out
```

```python
from contextlib import ExitStack

import concourse.bass as bass
from concourse import mybir

F32 = mybir.dt.float32
ALU = mybir.AluOpType
ACT = mybir.ActivationFunctionType
AX = mybir.AxisListType

P = 128
D = 1024
T = 256
TT = T // P
KT = D // P
DEPTH = 4
CH = 64
ALPHA = (2.0 * DEPTH) ** 0.25
EPS = 1e-5
DI = 2 * D
NH = 32
NG = 4
HPG = NH // NG
XBC = DI + 2 * NG * 128
CT_X = DI // P
CT_BC = XBC // P
CONV = 4
AH = 16
DH = 64
KVH = 4
REL_CLIP = 128
N_REL = CH - 1 + REL_CLIP + 1
NEG = -1.0e30
NE = 16
FF = D // 4
FT = FF // P
UW = 2048
RING = 6
UPE = 3
BODY = RING // UPE
SC = P + T

SSD, SWA, CA = 0, 1, 2
KINDS = [i % 3 for i in range(DEPTH)]
N_IN = {SSD: (DI + XBC) // 256, SWA: 6, CA: 12}
N_OUT = {SSD: 8, SWA: 4, CA: 4}
UNIT0 = []
PROJ0 = []
_u = _p = 0
for _k in KINDS:
    UNIT0.append(_u)
    PROJ0.append(_p)
    _u += N_IN[_k] + N_OUT[_k] + UPE * NE
    _p += N_IN[_k]
N_UNITS = _u


def moe_unit0(layer):
    k = KINDS[layer]
    return UNIT0[layer] + N_IN[k] + N_OUT[k]


def trunk(nc, a, out):
    ctx = ExitStack()
    with ctx:
        def sb(name, shape, dt=F32):
            return ctx.enter_context(nc.sbuf_tensor(name, shape, dt))

        def sem(name):
            return ctx.enter_context(nc.semaphore(name))

        ring = sb("ring", [P, RING, UW])
        x = sb("x", [P, TT, D])
        res = sb("res", [P, TT, D])
        xT = sb("xT", [P, KT, T])
        ln_gb = sb("ln_gb", [P, 2, D])
        ident = sb("ident", [P, P])
        ones = sb("ones", [P, P])
        triu = sb("triu", [P, T])
        rank = sb("rank", [P, NE])
        par = sb("par", [P, 2, 176])
        par_rows = sb("par_rows", [P, 2, 2, P])
        d_rows = sb("d_rows", [CT_X, 2, 2])
        w_dt = sb("w_dt", [P, 2, KT, NH])
        dtb = sb("dtb", [1, 2, NH])
        a_row = sb("a_row", [1, 2, NH])
        a_bc = sb("a_bc", [P, 2, NH])
        w_rt = sb("w_rt", [P, KT, NE])
        rt_bias = sb("rt_bias", [P, NE])
        sinks = sb("sinks", [P, AH])
        st = sb("st", [P, TT, 2, 6])
        mv = sb("mv", [P, TT, 2])
        rs = sb("rs", [P, TT])
        arena = sb("arena", [P, 24000])
        top = [0]

        def take(n, reset=None):
            if reset is not None:
                top[0] = reset
            top[0] += n
            assert top[0] <= 24000
            return arena[:, top[0] - n:top[0]]

        xbc = take(8 * 259, 0).rearrange("p (c t) -> p c t", t=259)
        cacc = take(4 * T).rearrange("p (c t) -> p c t", t=T)
        cv = take(CT_BC * T).rearrange("p (c t) -> p c t", t=T)
        sz = take(CT_X * T).rearrange("p (c t) -> p c t", t=T)
        xdt = take(TT * DI).rearrange("p (a c) -> p a c", a=TT)
        cbm = take(NG * SC).rearrange("p (g c) -> p g c", g=NG)
        seg = take(2 * SC).rearrange("p (g c) -> p g c", g=2)
        dec = take(2 * SC).rearrange("p (g c) -> p g c", g=2)
        mm_ = take(2 * SC).rearrange("p (g c) -> p g c", g=2)
        dts = take(8 * TT * NH).rearrange("p (n c) -> p n c", n=8)
        acT = take(T)
        gsum = take(NG * T, 0).rearrange("p (g t) -> p g t", g=NG)
        ytmp = take(2 * T).rearrange("p (g t) -> p g t", g=2)
        sq = take(4 * T).rearrange("p (g t) -> p g t", g=4)
        assert top[0] <= 8 * 259 + 4 * T
        qT = take(8 * T, 0).rearrange("p (c t) -> p c t", t=T)
        kT = take(8 * T).rearrange("p (c t) -> p c t", t=T)
        v = take(TT * D).rearrange("p (a c) -> p a c", a=TT)
        oT = take(8 * T).rearrange("p (c t) -> p c t", t=T)
        bias = take(2 * SC).rearrange("p (g c) -> p g c", g=2)
        lg = take(2 * SC).rearrange("p (g c) -> p g c", g=2)
        pT = take(2 * SC).rearrange("p (g c) -> p g c", g=2)
        hst = take(2 * 16).rearrange("p (g c) -> p g c", g=2)
        revx = take(384)
        rel = take(N_REL)
        gate_bc = take(NE * T, 0).rearrange("p (e t) -> p e t", t=T)
        sg = take(2 * 512).rearrange("p (b c) -> p b c", b=2)
        hb = take(2 * 512).rearrange("p (b c) -> p b c", b=2)
        gT = take(T)
        rt = take(20 * TT * NE).rearrange("p (n a e) -> p n a e", n=20, a=TT)

        ps = [ctx.enter_context(nc.psum_tensor(f"ps{i}", [P, 512], F32)) for i in range(8)]
        rev_dram = nc.dram_tensor("rev_dram", (AH, CH, 384), F32, kind="Internal").ap()

        loaded = [sem(f"loaded{s}") for s in range(RING)]
        S = {n: sem(n) for n in (
            "consts", "par_in", "par_rows_d", "par_ps", "par_sb", "a_exp", "a_ps", "a_sb", "rt_in", "x_in",
            "xt_ps", "xt_sb", "proj_ready", "proj_free", "lngb_in", "out_used", "gate_used", "down_used", "res_done", "ln_stats", "ln_sqrt",
            "ln_done", "dve_step", "act_step",
            "dt_ps", "dt_abs", "dt_exp", "dt_u", "dt_ln", "dt_sb", "cum_ps", "cum_sb", "conv_acc", "conv_done",
            "cb_ps", "cb_sb", "xs_ps", "xdt_sb", "bc_ps", "seg_sb", "dec_sb", "m_sb", "y_ps", "y2_sb", "sq_sb",
            "ss_ps", "ss_sb", "ss_sqrt", "yn_sb",
            "bias_sb", "rel_in", "rev_sb", "rev_out", "bias_in0", "bias_in1", "s_ps", "max_sb", "exp_sb", "p_sb", "pt_ps", "pt_sb", "o_ps", "o_sb",
            "rt_ps", "rt_exp", "gates_sb", "gt_ps", "gt_sb", "gb_ps", "gb_sb", "gu_ps", "sg_sb", "h_sb", "store", "pool_step")}

        def par_cw(j, tile, k):
            return par[:, j, k * CT_BC + tile:k * CT_BC + tile + 1]

        def par_d(j, t):
            return par[:, j, 96 + t:97 + t]

        def par_cb(j, tile):
            return par[:, j, 96 + 32 + tile:97 + 32 + tile]

        def par_nw(j, t):
            return par[:, j, 96 + 64 + t:97 + 64 + t]

        occ = {0: 0, 3: 1}
        att = {1: 0, 2: 1}
        order = [("xbc", n) for n in (8, 9, 10, 11, 0, 1, 2, 3, 4, 5, 6, 7)] + [("z", n) for n in range(8)]

        def used(u):
            L = max(n for n in range(DEPTH) if UNIT0[n] <= u)
            n = u - UNIT0[L]
            if n < N_IN[KINDS[L]]:
                return S["proj_ready"], PROJ0[L] + n + 1
            n -= N_IN[KINDS[L]]
            if n < N_OUT[KINDS[L]]:
                return S["out_used"], sum(N_OUT[k] for k in KINDS[:L]) + n + 1
            n -= N_OUT[KINDS[L]]
            return S[("gate_used", "gu_ps", "down_used")[n % UPE]], NE * L + n // UPE + 1

        block = ctx.enter_context(nc.Block())

        @block.sync
        def _(sp):
            def put(u, src):
                if u >= RING:
                    sp.wait_ge(*used(u - RING))
                dst = ring[:, u % RING, :]
                if len(src.shape) == 3:
                    dst = dst.rearrange("p (a b) -> p a b", a=src.shape[1])
                sp.dma_start(dst, src).then_inc(loaded[u % RING], 16)

            def w_in_unit(w, c):
                return w.rearrange("(p k) n -> p k n", k=KT)[:, :, c:c + 256]

            def w_out_unit(w, n):
                return w[256 * n:256 * n + 256, :].rearrange("(r p) n -> p r n", r=2)

            for L in range(DEPTH):
                kind = KINDS[L]
                u = UNIT0[L]
                if kind == SSD:
                    j = occ[L]
                    for n, (what, i) in enumerate(order):
                        c = 256 * i + (DI if what == "xbc" else 0)
                        put(u + n, w_in_unit(a["ssd_w_in"][j], c))
                    wo = a["ssd_w_out"][j]
                elif kind == SWA:
                    for n in range(N_IN[SWA]):
                        put(u + n, w_in_unit(a["swa_w_in"][0], 256 * n))
                    wo = a["swa_w_out"][0]
                else:
                    for n in range(N_IN[CA]):
                        put(u + n, w_in_unit(a["ca_w_in"][0], 256 * n))
                    wo = a["ca_w_out"][0]
                u += N_IN[kind]
                for n in range(N_OUT[kind]):
                    put(u + n, w_out_unit(wo, n))
                u = moe_unit0(L)
                gate_v = a["moe_w_gate"][L].rearrange("e (p k) f -> e p (k f)", k=KT)
                up_v = a["moe_w_up"][L].rearrange("e (p k) f -> e p (k f)", k=KT)
                down_v = a["moe_w_down"][L].rearrange("e (r p) n -> e p r n", r=FT)
                for b in range(BODY):
                    for n, view in enumerate((gate_v, up_v, down_v)):
                        put(u + b * UPE + n, view[b])
                with sp.Fori(1, NE // BODY) as i:
                    for b in range(BODY):
                        for n, view in enumerate((gate_v, up_v, down_v)):
                            k = u + b * UPE + n
                            s_used, at = used(k)
                            sp.wait_ge(s_used, i * BODY + (at - BODY))
                            dst = ring[:, k % RING, :]
                            if n == 2:
                                dst = dst.rearrange("p (r n) -> p r n", r=FT)
                            sp.dma_start(dst, view[i * BODY + b]).then_inc(loaded[k % RING], 16)
            sp.wait_ge(S["ln_done"], 2 * DEPTH * TT)
            sp.dma_start(out.rearrange("(a p) d -> p a d", p=P), x[:]).then_inc(S["store"], 16)
            sp.wait_ge(S["store"], 16)

        @block.tensor
        def _(pe):
            def unit_wait(u):
                pe.wait_ge(loaded[u % RING], 16 * (u // RING + 1))

            def unit(u, r):
                return ring[:, u % RING, :].rearrange("p (a b) -> p a b", a=r)

            def turn_x(n):
                if n == 0:
                    pe.wait_ge(S["x_in"], 16)
                    pe.wait_ge(S["consts"], 6)
                else:
                    pe.wait_ge(S["ln_done"], TT * n)
                for kp in range(4):
                    for k in (2 * kp, 2 * kp + 1):
                        for tt in range(TT):
                            c = (k % 2) * T + tt * P
                            t = pe.transpose(ps[kp][:, c:c + P], x[:, tt, k:D:KT], ident[:])
                    t.then_inc(S["xt_ps"], 1)

            def project_in(u, pg):
                unit_wait(u)
                if pg >= 4:
                    pe.wait_ge(S["proj_free"], pg - 3)
                w = unit(u, KT)
                for c in range(2):
                    for k in range(KT):
                        t = pe.matmul(ps[pg % 4][:, c * T:c * T + T], w[:, k, c * P:c * P + P], xT[:, k, :],
                                      start=k == 0, stop=k == KT - 1)
                return t

            def project_out(L, lhs, n_ct, ready):
                u0 = UNIT0[L] + N_IN[KINDS[L]]
                for n in range(n_ct // 2):
                    unit_wait(u0 + n)
                    w = unit(u0 + n, 2)
                    for r in range(2):
                        ct = 2 * n + r
                        ready(ct)
                        for tt in range(TT):
                            for half in range(2):
                                t = pe.matmul(ps[4 + 2 * tt + half][:, :], lhs[:, ct, tt * P:tt * P + P],
                                              w[:, r, half * 512:half * 512 + 512],
                                              start=ct == 0, stop=ct == n_ct - 1)
                    t.then_inc(S["out_used"], 1)

            def xt_wait(n):
                pe.wait_ge(S["xt_sb"], 4 * (n + 1))

            def ssd(L):
                j = occ[L]
                pg0 = PROJ0[L]
                u0 = UNIT0[L]
                xt_wait(2 * L)
                for tt in range(TT):
                    o = ps[4][:, tt * NH:tt * NH + NH]
                    for k in range(KT):
                        pe.matmul(o, xT[:, k, tt * P:tt * P + P], w_dt[:, j, k, :], start=k == 0, stop=False)
                    t = pe.matmul(o, ones[0:1, :], dtb[0:1, j, :], start=False, stop=True)
                t.then_inc(S["dt_ps"], 1)
                for n in range(4):
                    project_in(u0 + n, pg0 + n).then_inc(S["proj_ready"], 1)
                pe.wait_ge(S["dt_sb"], 2 * (j + 1))
                da = dts[:, 1, :].rearrange("p (a h) -> p a h", a=TT)
                pe.matmul(ps[5][:, 0:NH], triu[:, 0:P], da[:, 0, :], start=True, stop=True)
                pe.matmul(ps[5][:, NH:2 * NH], ones[:, :], da[:, 0, :], start=True, stop=False)
                pe.matmul(ps[5][:, NH:2 * NH], triu[:, 0:P], da[:, 1, :], start=False, stop=True)
                pe.matmul(ps[6][0:NH, 0:T], da[:, 0, :], triu[:, :], start=True, stop=False)
                pe.matmul(ps[6][0:NH, P:T], da[:, 1, :], triu[:, 0:P], start=False, stop=True)\
                    .then_inc(S["cum_ps"], 1)
                for n in range(4, 12):
                    project_in(u0 + n, pg0 + n).then_inc(S["proj_ready"], 1)
                pe.wait_ge(S["conv_done"], j * CT_BC + 8)
                pe.wait_ge(S["cum_sb"], 2 * (j + 1))
                for g in range(NG):
                    bt, c_t = cv[:, CT_X + g, :], cv[:, CT_X + NG + g, :]
                    pe.matmul(ps[4 + g][:, 0:T], bt[:, 0:P], c_t[:, :], start=True, stop=True)
                    pe.matmul(ps[4 + g][:, T:SC], bt[:, P:T], c_t[:, P:T], start=True, stop=True)\
                        .then_inc(S["cb_ps"], 1)
                for n in range(12, 20):
                    project_in(u0 + n, pg0 + n).then_inc(S["proj_ready"], 1)
                pe.wait_ge(S["conv_done"], j * CT_BC + 24)
                for q in range(8):
                    tt, c4 = q % 2, q // 2
                    if q < 4:
                        pe.wait_ge(S["cb_sb"], NG * j + q + 1)
                    else:
                        pe.wait_ge(S["xdt_sb"], 8 * j + q - 3)
                    for c in range(4):
                        t = pe.transpose(ps[4 + q % 4][:, c * P:c * P + P], cv[:, 4 * c4 + c, tt * P:tt * P + P], ident[:])
                    t.then_inc(S["xs_ps"], 1)

                def bc(h):
                    if h == 0:
                        pe.wait_ge(S["proj_free"], pg0 + 20)
                    if h >= 3:
                        pe.wait_ge(S["seg_sb"], 2 * (j * NH + h - 2))
                    pe.matmul(ps[h % 3][:, 0:T], ident[0:NH, h:h + 1].to_broadcast([NH, P]), acT[0:NH, 0:T],
                              start=True, stop=True)
                    pe.matmul(ps[h % 3][:, T:SC], ident[0:NH, h:h + 1].to_broadcast([NH, P]), acT[0:NH, P:T],
                              start=True, stop=True).then_inc(S["bc_ps"], 1)

                def yh(h):
                    b = 4 + (h // 4) % 4
                    if h == 0:
                        pe.wait_ge(S["xdt_sb"], 8 * (j + 1))
                    if h % 4 == 0 and h >= 16:
                        pe.wait_ge(S["y2_sb"], j * CT_X + 2 * (h // 4 - 3))
                    pe.wait_ge(S["m_sb"], j * NH + h + 1)
                    lo = DH * (h % 2)
                    c = T * ((h % 4) // 2)
                    o = ps[b][lo:lo + DH, :]
                    pe.matmul(o[:, c:c + T], xdt[:, 0, h * DH:h * DH + DH], mm_[:, h % 2, 0:T], start=True, stop=False)
                    t = pe.matmul(o[:, c + P:c + T], xdt[:, 1, h * DH:h * DH + DH], mm_[:, h % 2, T:SC],
                                  start=False, stop=True)
                    t.then_inc(S["y_ps"], 1)

                def sumsq(g):
                    if g >= 1:
                        pe.wait_ge(S["ss_sb"], j * NG + g)
                    for c in range(4):
                        pe.wait_ge(S["sq_sb"], j * CT_X + 4 * g + c + 1)
                        t = pe.matmul(ps[3][:, (g % 2) * T:(g % 2) * T + T], ones[:, :], sq[:, c, :],
                                      start=c == 0, stop=c == 3)
                    t.then_inc(S["ss_ps"], 1)

                bc(0)
                bc(1)
                for h in range(NH):
                    if h + 2 < NH:
                        bc(h + 2)
                    yh(h)
                    if h % 8 == 3 and h >= 8:
                        sumsq(h // 8 - 1)
                sumsq(NG - 1)
                project_out(L, sz, CT_X, lambda ct: pe.wait_ge(S["yn_sb"], j * CT_X + ct + 1))

            def attention(L):
                m = att[L]
                kind = KINDS[L]
                pg0, u0 = PROJ0[L], UNIT0[L]
                xt_wait(2 * L)
                nqk = 5 if kind == SWA else 8
                for n in range(nqk):
                    project_in(u0 + n, pg0 + n).then_inc(S["proj_ready"], 1)
                for n in range(nqk, N_IN[kind]):
                    pg = pg0 + n
                    unit_wait(u0 + n)
                    pe.wait_ge(S["proj_free"], pg - 3)
                    w = unit(u0 + n, KT)
                    for tt in range(TT):
                        for k in range(KT):
                            t = pe.matmul(ps[pg % 4][:, tt * T:tt * T + T], xT[:, k, tt * P:tt * P + P], w[:, k, :],
                                          start=k == 0, stop=k == KT - 1)
                    t.then_inc(S["proj_ready"], 1)
                pe.wait_ge(S["proj_free"], pg0 + N_IN[kind])

                def heads(h):
                    kvh = h // (AH // KVH) if kind == SWA else h
                    lo = DH * (h % 2)
                    kc = kvh if kind == SWA else h // 2
                    return lo, kvh, kc

                def scores(h):
                    lo, kvh, kc = heads(h)
                    b = h % 2
                    if h >= 2:
                        pe.wait_ge(S["max_sb"], AH * m + h - 1)
                    q = qT[lo:lo + DH, h // 2, :]
                    k = kT[lo:lo + DH, kc, :]
                    pe.matmul(ps[b][:, 0:P], q[:, 0:P], k[:, 0:P], start=True, stop=True)
                    pe.matmul(ps[b][:, P:SC], q[:, P:T], k[:, :], start=True, stop=True).then_inc(S["s_ps"], 1)

                def turn_p(h):
                    b = 2 + h % 2
                    pe.wait_ge(S["p_sb"], AH * m + h + 1)
                    if h >= 2:
                        pe.wait_ge(S["pt_sb"], AH * m + h - 1)
                    pe.transpose(ps[b][:, 0:P], lg[:, h % 2, 0:P], ident[:])
                    pe.transpose(ps[b][:, P:2 * P], lg[:, h % 2, P:2 * P], ident[:])
                    pe.transpose(ps[b][:, 2 * P:SC], lg[:, h % 2, 2 * P:SC], ident[:]).then_inc(S["pt_ps"], 1)

                def pv(h):
                    lo, kvh, kc = heads(h)
                    b = 4 + (h // 4) % 4
                    pe.wait_ge(S["pt_sb"], AH * m + h + 1)
                    c = T * ((h % 4) // 2)
                    o = ps[b][lo:lo + DH, :]
                    pe.matmul(o[:, c:c + T], v[:, 0, kvh * DH:kvh * DH + DH], pT[:, h % 2, 0:T], start=True, stop=False)
                    pe.matmul(o[:, c + P:c + T], v[:, 1, kvh * DH:kvh * DH + DH], pT[:, h % 2, T:SC],
                              start=False, stop=True).then_inc(S["o_ps"], 1)

                scores(0)
                scores(1)
                for h in range(AH):
                    turn_p(h)
                    if h + 2 < AH:
                        scores(h + 2)
                    pv(h)
                pe.wait_ge(S["o_sb"], 4 * (m + 1))
                project_out(L, oT, 8, lambda ct: None)

            def moe(L):
                xt_wait(2 * L + 1)
                for tt in range(TT):
                    for k in range(KT):
                        t = pe.matmul(ps[4][:, tt * NE:tt * NE + NE], xT[:, k, tt * P:tt * P + P], w_rt[:, k, :],
                                      start=k == 0, stop=k == KT - 1)
                t.then_inc(S["rt_ps"], 1)
                pe.wait_ge(S["gates_sb"], L + 1)
                for tt in range(TT):
                    t = pe.transpose(ps[5][0:NE, tt * P:tt * P + P], rt[:, 0, tt, :], ident[:])
                t.then_inc(S["gt_ps"], 1)
                pe.wait_ge(S["gt_sb"], L + 1)
                for e2 in range(NE // 2):
                    b = 4 + e2 % 4
                    if e2 >= 4:
                        pe.wait_ge(S["gb_sb"], 8 * L + e2 - 3)
                    for e in (2 * e2, 2 * e2 + 1):
                        t = pe.matmul(ps[b][:, (e % 2) * T:(e % 2) * T + T], ident[0:NE, e:e + 1].to_broadcast([NE, P]),
                                      gT[0:NE, :], start=True, stop=True)
                    t.then_inc(S["gb_ps"], 1)
                pe.wait_ge(S["gb_sb"], 8 * (L + 1))
                u0 = moe_unit0(L)

                def gate_up(i, b):
                    for n in range(2):
                        u = u0 + b * UPE + n
                        pe.wait_ge(loaded[u % RING], 16 * (u // RING + 1) + 16 * i)
                        w = unit(u, KT)
                        bank = ps[2 * (b % 2) + n]
                        for f in range(FT):
                            for k in range(KT):
                                t = pe.matmul(bank[:, f * T:f * T + T], w[:, k, f * P:f * P + P], xT[:, k, :],
                                              start=k == 0, stop=k == KT - 1)
                        t.then_inc(S["gate_used" if n == 0 else "gu_ps"], 1)

                def down(i, b, first, last):
                    u = u0 + b * UPE + 2
                    pe.wait_ge(loaded[u % RING], 16 * (u // RING + 1) + 16 * i)
                    w = unit(u, FT)
                    pe.wait_ge(S["h_sb"], NE * L + b + 1 + BODY * i)
                    for f in range(FT):
                        for tt in range(TT):
                            for half in range(2):
                                t = pe.matmul(ps[4 + 2 * tt + half][:, :],
                                              hb[:, b % 2, f * T + tt * P:f * T + tt * P + P],
                                              w[:, f, half * 512:half * 512 + 512],
                                              start=first and f == 0, stop=last and f == FT - 1, skip_group_check=True)
                    t.then_inc(S["down_used"], 1)

                for b in range(BODY):
                    gate_up(0, b)
                    down(0, b, b == 0, False)
                with pe.Fori(1, NE // BODY) as i:
                    for b in range(BODY):
                        gate_up(i, b)
                        down(i, b, False, False)

            pe.wait_ge(S["consts"], 6)
            pe.wait_ge(S["par_in"], 16 * 11)
            pe.wait_ge(S["par_rows_d"], 2)
            for j in range(2):
                pe.transpose(ps[4 + j][:, 0:96], par_rows[0:96, j, 0, :], ident[0:96, 0:96])
                pe.transpose(ps[4 + j][:, 96:176], par_rows[0:80, j, 1, :], ident[0:80, 0:80]).then_inc(S["par_ps"], 1)
            pe.wait_ge(S["a_exp"], 1)
            pe.matmul(ps[6][:, 0:2 * NH], ones[0:1, :], a_row[0:1, :, :].rearrange("p a b -> p (a b)"),
                      start=True, stop=True).then_inc(S["a_ps"], 1)
            pe.wait_ge(S["par_sb"], 2)
            pe.wait_ge(S["a_sb"], 1)
            turn_x(0)
            for L in range(DEPTH):
                if KINDS[L] == SSD:
                    ssd(L)
                else:
                    attention(L)
                turn_x(2 * L + 1)
                moe(L)
                if L < DEPTH - 1:
                    turn_x(2 * L + 2)

        @block.scalar
        def _(act):
            steps = [0]

            def link(ins):
                steps[0] += 1
                ins.then_inc(S["act_step"], 1)
                act.wait_ge(S["act_step"], steps[0])

            act.wait_ge(S["pool_step"], 1)
            for j in range(2):
                act.dma_start(par_rows[0:96, j, 0, :], a["ssd_conv_w"][j].rearrange("k (c p) -> (k c) p", p=P)).then_inc(S["par_in"], 16)
                act.dma_start(par_rows[32:56, j, 1, :], a["ssd_conv_b"][j].rearrange("(c p) -> c p", p=P)).then_inc(S["par_in"], 16)
                act.dma_start(par_rows[64:80, j, 1, :], a["ssd_norm_w"][j].rearrange("(c p) -> c p", p=P)).then_inc(S["par_in"], 16)
            act.dma_start(d_rows[:, :, :], a["ssd_d_skip"].rearrange("j (c r) -> c j r", r=2)).then_inc(S["par_in"], 16)
            act.dma_start(a_row[0:1, :, :], a["ssd_a_log"].rearrange("(o j) h -> o j h", o=1)).then_inc(S["par_in"], 16)
            act.dma_start(dtb[0:1, :, :], a["ssd_dt_bias"].rearrange("(o j) h -> o j h", o=1)).then_inc(S["par_in"], 16)
            for j in range(2):
                act.dma_start(w_dt[:, j, :, :], a["ssd_w_in"][j].rearrange("(p k) n -> p k n", k=KT)[:, :, DI + XBC:DI + XBC + NH]).then_inc(S["par_in"], 16)
            act.wait_ge(S["par_in"], 16 * 11)
            act.activation(a_row[0:1, :, :], a_row[0:1, :, :], ACT.Exp).then_inc(S["a_exp"], 1)

            def xt_evac(n):
                for kp in range(4):
                    act.wait_ge(S["xt_ps"], 4 * n + kp + 1)
                    act.activation(xT[:, 2 * kp:2 * kp + 2, :], ps[kp][:, :].rearrange("p (a t) -> p a t", a=2), ACT.Copy)\
                        .then_inc(S["xt_sb"], 1)

            def norm(n):
                for tt in range(TT):
                    act.wait_ge(S["ln_stats"], TT * n + tt + 1)
                    act.activation(rs[:, tt:tt + 1], mv[:, tt, 1:2], ACT.Sqrt).then_inc(S["ln_sqrt"], 1)

            def ssd(L):
                j = occ[L]
                pg0 = PROJ0[L]

                def silu_conv(n):
                    t0 = 2 * order[n][1]
                    act.wait_ge(S["conv_acc"], j * 12 + n + 1)
                    for c in range(2):
                        act.activation(cv[:, t0 + c, :], cacc[:, 2 * (n % 2) + c, :], ACT.Silu, bias=par_cb(j, t0 + c))\
                            .then_inc(S["conv_done"], 1)

                def softplus_exp():
                    act.wait_ge(S["dt_abs"], 2 * j + 2)
                    act.activation(dts[:, 2, :], dts[:, 3, :], ACT.Exp).then_inc(S["dt_exp"], 1)

                def softplus_ln():
                    act.wait_ge(S["dt_u"], j + 1)
                    act.activation(dts[:, 5, :], dts[:, 4, :], ACT.Ln).then_inc(S["dt_ln"], 1)

                softplus_exp()
                softplus_ln()
                for n in range(12):
                    act.wait_ge(S["proj_ready"], pg0 + n + 1)
                    if n >= 4:
                        act.wait_ge(S["conv_acc"], j * 12 + n - 3)
                    s = 2 * (n % 4)
                    act.activation(xbc[:, s:s + 2, 3:259], ps[(pg0 + n) % 4][:, :].rearrange("p (a t) -> p a t", a=2),
                                   ACT.Copy).then_inc(S["proj_free"], 1)
                    if n >= 1:
                        silu_conv(n - 1)
                silu_conv(11)
                for n in range(12, 20):
                    act.wait_ge(S["proj_ready"], pg0 + n + 1)
                    t0 = 2 * order[n][1]
                    act.activation(sz[:, t0:t0 + 2, :], ps[(pg0 + n) % 4][:, :].rearrange("p (a t) -> p a t", a=2),
                                   ACT.Silu).then_inc(S["proj_free"], 1)
                for h in range(NH):
                    act.wait_ge(S["seg_sb"], 2 * (j * NH + h + 1))
                    if h >= 2:
                        act.wait_ge(S["m_sb"], j * NH + h - 1)
                    act.activation(dec[:, h % 2, :], seg[:, h % 2, :], ACT.Exp).then_inc(S["dec_sb"], 1)
                    if h % 4 == 1 and h >= 4:
                        square(j, h // 4 - 1)
                square(j, 7)
                act.wait_ge(S["ss_sb"], NG * (j + 1))
                act.activation(gsum[:, :, :], gsum[:, :, :], ACT.Sqrt).then_inc(S["ss_sqrt"], 1)

            def square(j, q):
                for c in (2 * q, 2 * q + 1):
                    act.wait_ge(S["y2_sb"], j * CT_X + c + 1)
                    if c >= 4:
                        act.wait_ge(S["ss_ps"], j * NG + c // 4)
                    act.activation(sq[:, c % 4, :], sz[:, c, :], ACT.Square).then_inc(S["sq_sb"], 1)

            def attention(L):
                m = att[L]
                kind = KINDS[L]
                pg0 = PROJ0[L]
                scale = float(DH) ** -0.5
                for n in range(4):
                    act.wait_ge(S["proj_ready"], pg0 + n + 1)
                    act.activation(qT[:, 2 * n:2 * n + 2, :], ps[(pg0 + n) % 4][:, :].rearrange("p (a t) -> p a t", a=2),
                                   ACT.Copy, scale=scale).then_inc(S["proj_free"], 1)
                if kind == SWA:
                    act.wait_ge(S["proj_ready"], pg0 + 5)
                    bank = ps[(pg0 + 4) % 4]
                    for g in range(KVH):
                        src = bank[DH * (g % 2):DH * (g % 2) + DH, (g // 2) * T:(g // 2) * T + T]
                        for half in range(2):
                            ins = act.activation(kT[DH * half:DH * half + DH, g, :], src, ACT.Copy)
                            if g == KVH - 1 and half == 1:
                                ins.then_inc(S["proj_free"], 1)
                    nv = 5
                else:
                    for n in range(4, 8):
                        act.wait_ge(S["proj_ready"], pg0 + n + 1)
                        act.activation(kT[:, 2 * n - 8:2 * n - 6, :],
                                       ps[(pg0 + n) % 4][:, :].rearrange("p (a t) -> p a t", a=2),
                                       ACT.Copy).then_inc(S["proj_free"], 1)
                    nv = 8
                for n in range(nv, N_IN[kind]):
                    act.wait_ge(S["proj_ready"], pg0 + n + 1)
                    c = 256 * (n - nv)
                    act.activation(v[:, :, c:c + 256], ps[(pg0 + n) % 4][:, :].rearrange("p (a t) -> p a t", a=2),
                                   ACT.Copy).then_inc(S["proj_free"], 1)
                for h in range(AH):
                    act.wait_ge(S["max_sb"], AH * m + h + 1)
                    b = h % 2
                    act.activation(lg[:, b, 0:P], lg[:, b, 0:P], ACT.Exp, bias=hst[:, b, 0:1],
                                   accum_out=hst[:, b, 2:3])
                    if kind == SWA:
                        act.activation(hst[:, b, 4:6], hst[:, b, 0:2], ACT.Exp, bias=sinks[:, h:h + 1])
                    act.activation(lg[:, b, P:SC], lg[:, b, P:SC], ACT.Exp, bias=hst[:, b, 1:2],
                                   accum_out=hst[:, b, 3:4]).then_inc(S["exp_sb"], 1)
                    act.wait_ge(S["pt_ps"], AH * m + h + 1)
                    if h >= 2:
                        act.wait_ge(S["o_ps"], AH * m + h - 1)
                    act.activation(pT[:, b, :], ps[2 + b][:, 0:SC], ACT.Copy).then_inc(S["pt_sb"], 1)
                    if h % 4 == 3:
                        act.wait_ge(S["o_ps"], AH * m + h + 1)
                        c = h // 4
                        act.activation(oT[:, 2 * c:2 * c + 2, :], ps[4 + c][:, :].rearrange("p (a t) -> p a t", a=2),
                                       ACT.Copy).then_inc(S["o_sb"], 1)

            def moe(L):
                act.wait_ge(S["rt_ps"], L + 1)
                act.activation(rt[:, 1, :, :], ps[4][:, 0:TT * NE].rearrange("p (a e) -> p a e", a=TT), ACT.Exp,
                               scale=-1.0).then_inc(S["rt_exp"], 1)
                act.wait_ge(S["gt_ps"], L + 1)
                act.activation(gT[0:NE, :], ps[5][0:NE, 0:T], ACT.Copy).then_inc(S["gt_sb"], 1)
                for e2 in range(NE // 2):
                    act.wait_ge(S["gb_ps"], 8 * L + e2 + 1)
                    act.activation(gate_bc[:, 2 * e2:2 * e2 + 2, :], ps[4 + e2 % 4][:, :].rearrange("p (a t) -> p a t", a=2),
                                   ACT.Copy).then_inc(S["gb_sb"], 1)
                with act.Fori(0, NE // BODY) as i:
                    for b in range(BODY):
                        act.wait_ge(S["gu_ps"], NE * L + b + 1 + BODY * i)
                        act.activation(sg[:, b % 2, :], ps[2 * (b % 2)][:, :], ACT.Silu).then_inc(S["sg_sb"], 1)

            xt_evac(0)
            for L in range(DEPTH):
                if KINDS[L] == SSD:
                    ssd(L)
                else:
                    attention(L)
                norm(2 * L)
                xt_evac(2 * L + 1)
                moe(L)
                norm(2 * L + 1)
                if L < DEPTH - 1:
                    xt_evac(2 * L + 2)

        @block.vector
        def _(dve):
            steps = [0]

            def link(ins):
                steps[0] += 1
                ins.then_inc(S["dve_step"], 1)
                dve.wait_ge(S["dve_step"], steps[0])

            link(dve.memset(xbc[:, :, 0:3], 0.0))
            dve.wait_ge(S["par_in"], 16 * 11)
            dve.wait_ge(S["pool_step"], 1)
            for j in range(2):
                dve.tensor_copy(par_rows[0:CT_X, j, 1, :].rearrange("c (r q) -> c r q", r=2),
                                d_rows[:, j, :].unsqueeze(2).to_broadcast([CT_X, 2, DH])).then_inc(S["par_rows_d"], 1)
            for j in range(2):
                dve.wait_ge(S["par_ps"], j + 1)
                dve.tensor_copy(par[:, j, :], ps[4 + j][:, 0:176]).then_inc(S["par_sb"], 1)
            dve.wait_ge(S["a_ps"], 1)
            dve.tensor_copy(a_bc[:, :, :].rearrange("p a b -> p (a b)"), ps[6][:, 0:2 * NH]).then_inc(S["a_sb"], 1)

            def norm(n):
                if n == 0:
                    dve.wait_ge(S["x_in"], 16)
                for tt in range(TT):
                    for half in range(2):
                        c = slice(half * 512, half * 512 + 512)
                        dve.scalar_tensor_tensor(res[:, tt, c], x[:, tt, c], ALPHA, ps[4 + 2 * tt + half][:, :],
                                                 ALU.mult, ALU.add).then_inc(S["res_done"], 1)
                for tt in range(TT):
                    for half in range(2):
                        c = slice(half * 512, half * 512 + 512)
                        dve.wait_ge(S["res_done"], 4 * n + 2 * tt + half + 1)
                        ins = dve.bn_stats(st[:, tt, half, :], res[:, tt, c])
                    link(ins)
                    link(dve.bn_aggr(mv[:, tt, :], st[:, tt, :, :]))
                    dve.tensor_scalar(mv[:, tt, 1:2], mv[:, tt, 1:2], EPS, None, ALU.add).then_inc(S["ln_stats"], 1)
                for tt in range(TT):
                    dve.wait_ge(S["ln_sqrt"], TT * n + tt + 1)
                    link(dve.reciprocal(rs[:, tt:tt + 1], rs[:, tt:tt + 1]))
                    link(dve.tensor_scalar(res[:, tt, :], res[:, tt, :], mv[:, tt, 0:1], rs[:, tt:tt + 1],
                                           ALU.subtract, ALU.mult))
                    dve.wait_ge(S["lngb_in"], 32 * (n + 1))
                    link(dve.tensor_tensor(res[:, tt, :], res[:, tt, :], ln_gb[:, 0, :], ALU.mult))
                    dve.tensor_tensor(x[:, tt, :], res[:, tt, :], ln_gb[:, 1, :], ALU.add).then_inc(S["ln_done"], 1)

            def ssd(L):
                j = occ[L]
                if j > 0:
                    link(dve.memset(xbc[:, :, 0:3], 0.0))
                dve.wait_ge(S["dt_ps"], j + 1)
                pre = ps[4][:, 0:TT * NH]
                dve.tensor_scalar(dts[:, 6, :], pre, 0.0, None, ALU.max).then_inc(S["dt_abs"], 1)
                dve.wait_ge(S["dt_abs"], 2 * j + 1)
                dve.scalar_tensor_tensor(dts[:, 3, :], dts[:, 6, :], -2.0, pre, ALU.mult, ALU.add).then_inc(S["dt_abs"], 1)
                dve.wait_ge(S["dt_exp"], j + 1)
                dve.tensor_scalar(dts[:, 4, :], dts[:, 2, :], 1.0, None, ALU.add).then_inc(S["dt_u"], 1)
                dve.wait_ge(S["dt_u"], j + 1)
                link(dve.scalar_tensor_tensor(dts[:, 7, :], dts[:, 4, :], 1.0, dts[:, 2, :], ALU.subtract, ALU.subtract))
                link(dve.reciprocal(dts[:, 2, :], dts[:, 4, :]))
                link(dve.tensor_tensor(dts[:, 7, :], dts[:, 7, :], dts[:, 2, :], ALU.mult))
                link(dve.tensor_tensor(dts[:, 6, :], dts[:, 6, :], dts[:, 7, :], ALU.subtract))
                dve.wait_ge(S["dt_ln"], j + 1)
                dve.tensor_tensor(dts[:, 0, :], dts[:, 6, :], dts[:, 5, :], ALU.add).then_inc(S["dt_sb"], 1)
                dve.wait_ge(S["dt_sb"], 2 * j + 1)
                dve.scalar_tensor_tensor(dts[:, 1, :].rearrange("p (a h) -> p a h", a=TT),
                                         dts[:, 0, :].rearrange("p (a h) -> p a h", a=TT), -1.0,
                                         a_bc[:, j, :].unsqueeze(1).to_broadcast([P, TT, NH]), ALU.mult, ALU.mult)\
                    .then_inc(S["dt_sb"], 1)

                def conv(n):
                    dve.wait_ge(S["proj_free"], PROJ0[L] + n + 1)
                    if n >= 2:
                        dve.wait_ge(S["conv_done"], j * CT_BC + 2 * (n - 1))
                    t0 = 2 * order[n][1]
                    for k in range(CONV):
                        for c in range(2):
                            src = xbc[:, 2 * (n % 4) + c, k:k + T]
                            dst = cacc[:, 2 * (n % 2) + c, :]
                            w = par_cw(j, t0 + c, k)
                            if k == 0:
                                ins = dve.tensor_scalar(dst, src, w, None, ALU.mult)
                            else:
                                ins = dve.scalar_tensor_tensor(dst, src, w, dst, ALU.mult, ALU.add)
                            if k == CONV - 1 and c == 1:
                                ins.then_inc(S["conv_acc"], 1)
                            elif c == 1:
                                link(ins)
                for n in range(2):
                    conv(n)
                dve.wait_ge(S["cum_ps"], j + 1)
                dve.tensor_copy(dts[:, 7, :], ps[5][:, 0:TT * NH]).then_inc(S["cum_sb"], 1)
                dve.tensor_copy(acT[0:NH, :], ps[6][0:NH, 0:T]).then_inc(S["cum_sb"], 1)
                for n in range(2, 12):
                    conv(n)
                for g in range(NG):
                    dve.wait_ge(S["cb_ps"], NG * j + g + 1)
                    dve.tensor_tensor(cbm[:, g, 0:T], ps[4 + g][:, 0:T], triu[:, :], ALU.mult)
                    dve.tensor_tensor(cbm[:, g, T:SC], ps[4 + g][:, T:SC], triu[:, 0:P], ALU.mult).then_inc(S["cb_sb"], 1)
                dt_v = dts[:, 0, :].rearrange("p (a h) -> p a h", a=TT)
                for q in range(8):
                    tt, c4 = q % 2, q // 2
                    dve.wait_ge(S["xs_ps"], 8 * j + q + 1)
                    dve.tensor_tensor(xdt[:, tt, 512 * c4:512 * c4 + 512].rearrange("p (h c) -> p h c", c=DH),
                                      ps[4 + q % 4][:, :].rearrange("p (h c) -> p h c", c=DH),
                                      dt_v[:, tt, 8 * c4:8 * c4 + 8].unsqueeze(2).to_broadcast([P, 8, DH]), ALU.mult)\
                        .then_inc(S["xdt_sb"], 1)

                def gating(c):
                    dve.wait_ge(S["y_ps"], j * NH + 4 * (c // 2) + 4)
                    link(dve.scalar_tensor_tensor(ytmp[:, c % 2, :], cv[:, c, :], par_d(j, c),
                                                  ps[4 + (c // 2) % 4][:, (c % 2) * T:(c % 2) * T + T], ALU.mult, ALU.add))
                    dve.tensor_tensor(sz[:, c, :], ytmp[:, c % 2, :], sz[:, c, :], ALU.mult).then_inc(S["y2_sb"], 1)

                def sumsq_evac(g):
                    dve.wait_ge(S["ss_ps"], NG * j + g + 1)
                    dve.tensor_scalar(gsum[:, g, :], ps[3][:, (g % 2) * T:(g % 2) * T + T], 1.0 / (DI // NG), EPS,
                                      ALU.mult, ALU.add).then_inc(S["ss_sb"], 1)

                acs = dts[:, 7, :].rearrange("p (a h) -> p a h", a=TT)
                dve.wait_ge(S["cum_sb"], 2 * (j + 1))
                for h in range(NH):
                    dve.wait_ge(S["bc_ps"], j * NH + h + 1)
                    if h >= 2:
                        dve.wait_ge(S["dec_sb"], j * NH + h - 1)
                    dve.tensor_scalar(seg[:, h % 2, 0:T], ps[h % 3][:, 0:T], acs[:, 0, h:h + 1], 0.0,
                                      ALU.subtract, ALU.min).then_inc(S["seg_sb"], 1)
                    dve.tensor_scalar(seg[:, h % 2, T:SC], ps[h % 3][:, T:SC], acs[:, 1, h:h + 1], 0.0,
                                      ALU.subtract, ALU.min).then_inc(S["seg_sb"], 1)
                    if h % 4 == 1 and h >= 4:
                        gating(2 * (h // 4) - 2)
                        gating(2 * (h // 4) - 1)
                    if h % 8 == 7 and h >= 15:
                        sumsq_evac(h // 8 - 1)
                gating(14)
                gating(15)
                sumsq_evac(NG - 1)
                dve.wait_ge(S["ss_sqrt"], j + 1)
                link(dve.reciprocal(gsum[:, :, :], gsum[:, :, :]))
                for c in range(CT_X):
                    dve.scalar_tensor_tensor(sz[:, c, :], sz[:, c, :], par_nw(j, c), gsum[:, c // 4, :],
                                             ALU.mult, ALU.mult).then_inc(S["yn_sb"], 1)

            def attention(L):
                m = att[L]
                kind = KINDS[L]
                if kind == CA:
                    dve.wait_ge(S["rel_in"], 16)
                    dve.tensor_copy(revx[0:AH, 0:127], rel[0:AH, N_REL - 1:N_REL].to_broadcast([AH, 127]))
                    dve.tensor_copy(revx[0:AH, 127:127 + N_REL], rel[0:AH, ::-1])
                    dve.tensor_copy(revx[0:AH, 127 + N_REL:384], rel[0:AH, 0:1].to_broadcast([AH, 384 - 127 - N_REL]))\
                        .then_inc(S["rev_sb"], 1)
                for h in range(AH):
                    b = h % 2
                    dve.wait_ge(S["s_ps"], AH * m + h + 1)
                    if kind == SWA:
                        dve.wait_ge(S["bias_sb"], 4)
                        slope = 2.0 ** (-8.0 * (h + 1) / AH)
                        bsrc, mul = bias[:, 0, :], slope
                    else:
                        dve.wait_ge(S[f"bias_in{b}"], 16 * 4 * (h // 2 + 1))
                        bsrc, mul = bias[:, b, :], 1.0
                    if kind == CA and h == 0:
                        dve.wait_ge(S["bias_sb"], 8)
                    if h >= 2:
                        dve.wait_ge(S["pt_ps"], AH * m + h - 1)
                    link(dve.scalar_tensor_tensor(lg[:, b, :], bsrc, mul, ps[b][:, 0:SC], ALU.mult, ALU.add))
                    dve.tensor_reduce(hst[:, b, 6:7], lg[:, b, 0:P], AX.X, ALU.max)
                    link(dve.tensor_reduce(hst[:, b, 7:8], lg[:, b, P:SC], AX.X, ALU.max))
                    if kind == SWA:
                        dve.tensor_scalar(hst[:, b, 0:2], hst[:, b, 6:8], sinks[:, h:h + 1], -1.0, ALU.max, ALU.mult)\
                            .then_inc(S["max_sb"], 1)
                    else:
                        dve.tensor_scalar(hst[:, b, 0:2], hst[:, b, 6:8], -1.0, None, ALU.mult).then_inc(S["max_sb"], 1)
                    dve.wait_ge(S["exp_sb"], AH * m + h + 1)
                    if kind == SWA:
                        link(dve.tensor_tensor(hst[:, b, 2:4], hst[:, b, 2:4], hst[:, b, 4:6], ALU.add))
                    link(dve.reciprocal(hst[:, b, 8:10], hst[:, b, 2:4]))
                    dve.tensor_scalar(lg[:, b, 0:P], lg[:, b, 0:P], hst[:, b, 8:9], None, ALU.mult)
                    dve.tensor_scalar(lg[:, b, P:SC], lg[:, b, P:SC], hst[:, b, 9:10], None, ALU.mult)\
                        .then_inc(S["p_sb"], 1)

            def moe(L):
                R = lambda n: rt[:, n, :, :]
                small = lambda n, w: rt[:, n, :, :].rearrange("p a e -> p (a e)")[:, 0:TT * w].rearrange("p (a e) -> p a e", e=w)
                dve.wait_ge(S["rt_exp"], L + 1)
                link(dve.tensor_scalar(R(1), R(1), 1.0, None, ALU.add))
                link(dve.reciprocal(R(2), R(1)))
                link(dve.tensor_tensor(R(3), R(2), rt_bias[:, :].unsqueeze(1).to_broadcast([P, TT, NE]), ALU.add))
                g4 = rt[:, 3, :, :].rearrange("p a (g e) -> p (a g) e", e=4)
                pairs = rt[:, 4:7, :, :].rearrange("p n a e -> p (n a e)")[:, 0:48].rearrange("p (g e) -> p g e", e=6)
                dve.tensor_tensor(pairs[:, :, 0:2], g4[:, :, 0:2], g4[:, :, 2:4], ALU.add)
                dve.tensor_tensor(pairs[:, :, 2:4], g4[:, :, 0:2], g4[:, :, 3:1:-1], ALU.add)
                link(dve.tensor_tensor(pairs[:, :, 4:6], g4[:, :, 0:4:2], g4[:, :, 1:4:2], ALU.add))
                gs = small(7, 4)
                link(dve.tensor_reduce(gs.rearrange("p a g -> p (a g)"), pairs, AX.X, ALU.max))
                m1 = rt[:, 8, 0, :]

                def one_hot(dst, src, w, tmp, c):
                    rk = rank[:, NE - w:NE].unsqueeze(1).to_broadcast([P, TT, w])
                    link(dve.tensor_reduce(m1[:, c:c + TT], src, AX.X, ALU.max))
                    link(dve.tensor_tensor(dst, src, m1[:, c:c + TT].unsqueeze(2).to_broadcast([P, TT, w]), ALU.is_equal))
                    link(dve.tensor_tensor(tmp, dst, rk, ALU.mult))
                    link(dve.tensor_reduce(m1[:, c + TT:c + 2 * TT], tmp, AX.X, ALU.max))
                    link(dve.tensor_tensor(dst, tmp, m1[:, c + TT:c + 2 * TT].unsqueeze(2).to_broadcast([P, TT, w]), ALU.is_equal))

                best = small(9, 4)
                one_hot(best, gs, 4, small(10, 4), 0)
                link(dve.tensor_scalar(small(11, 4), best, 1.0, -NEG, ALU.subtract, ALU.mult))
                selm = R(12)
                link(dve.tensor_tensor(selm.rearrange("p a (g e) -> p (a g) e", e=4), g4,
                                       small(11, 4).rearrange("p a g -> p (a g)").unsqueeze(2).to_broadcast([P, TT * 4, 4]), ALU.add))
                one_hot(R(13), selm, NE, R(14), 4)
                link(dve.scalar_tensor_tensor(R(15), R(13), 4.0 * NEG, selm, ALU.mult, ALU.add))
                one_hot(R(16), R(15), NE, R(14), 8)
                link(dve.tensor_tensor(R(13), R(13), R(16), ALU.add))
                link(dve.tensor_tensor(R(17), R(13), R(2), ALU.mult))
                link(dve.tensor_reduce(m1[:, 12:12 + TT], R(17), AX.X, ALU.add))
                link(dve.reciprocal(m1[:, 14:14 + TT], m1[:, 12:12 + TT]))
                dve.tensor_tensor(R(0), R(17), m1[:, 14:14 + TT].unsqueeze(2).to_broadcast([P, TT, NE]), ALU.mult)\
                    .then_inc(S["gates_sb"], 1)
                dve.wait_ge(S["gb_sb"], 8 * (L + 1))
                base = steps[0]
                with dve.Fori(0, NE // BODY) as i:
                    for b in range(BODY):
                        dve.wait_ge(S["sg_sb"], NE * L + b + 1 + BODY * i)
                        s, h = sg[:, b % 2, :], hb[:, b % 2, :]
                        dve.tensor_tensor(s, s, ps[2 * (b % 2) + 1][:, :], ALU.mult).then_inc(S["dve_step"], 1)
                        dve.wait_ge(S["dve_step"], base + b + 1 + BODY * i)
                        dve.tensor_tensor(h.rearrange("p (f t) -> p f t", f=FT), s.rearrange("p (f t) -> p f t", f=FT),
                                          gate_bc[:, bass.ds(i * BODY + b, 1), :].to_broadcast([P, FT, T]), ALU.mult)\
                            .then_inc(S["h_sb"], 1)
                steps[0] = base + NE

            for L in range(DEPTH):
                if KINDS[L] == SSD:
                    ssd(L)
                else:
                    attention(L)
                dve.wait_ge(S["out_used"], sum(N_OUT[k] for k in KINDS[:L + 1]))
                norm(2 * L)
                moe(L)
                dve.wait_ge(S["down_used"], NE * (L + 1))
                norm(2 * L + 1)

        @block.gpsimd
        def _(pool):
            pool.dma_start(x[:], a["x"][0].rearrange("(t p) d -> p t d", p=P)).then_inc(S["x_in"], 16)
            pool.dma_start(w_rt[:, :, :], a["router_w"].rearrange("(p k) e -> p k e", k=KT)).then_inc(S["rt_in"], 16)
            pool.dma_start(rt_bias[:, :], a["router_bias"].rearrange("(o e) -> o e", o=1).to_broadcast([P, NE])).then_inc(S["rt_in"], 16)
            pool.dma_start(sinks[:, :], a["swa_sinks"].to_broadcast([P, AH])).then_inc(S["rt_in"], 16)
            pool.memset(par_rows[:, :, 1, :], 0.0).then_inc(S["pool_step"], 1)
            pool.memset(ident[:, :], 0.0).then_inc(S["consts"], 1)
            pool.memset(ones[:, :], 1.0).then_inc(S["consts"], 1)
            pool.memset(triu[:, :], 1.0).then_inc(S["consts"], 1)
            pool.wait_ge(S["consts"], 3)
            pool.affine_select(out=ident[:, :], in_=ident[:, :], compare_op=ALU.not_equal, fill=1.0, base=0,
                               pattern=[[-1, P]], channel_multiplier=1).then_inc(S["consts"], 1)
            pool.affine_select(out=triu[:, :], in_=triu[:, :], compare_op=ALU.is_ge, fill=0.0, base=0,
                               pattern=[[1, T]], channel_multiplier=-1).then_inc(S["consts"], 1)
            pool.iota(rank[:, :], pattern=[[-1, NE]], base=NE, channel_multiplier=0, allow_small_or_imprecise_dtypes=True).then_inc(S["consts"], 1)

            def gains(n):
                if n > 0:
                    pool.wait_ge(S["ln_done"], TT * n)
                g, b = ("ln_mix_g", "ln_mix_b") if n % 2 == 0 else ("ln_ffn_g", "ln_ffn_b")
                for i, w in enumerate((g, b)):
                    pool.dma_start(ln_gb[:, i, :], a[w][n // 2:n // 2 + 1, :].to_broadcast([P, D])).then_inc(S["lngb_in"], 16)

            def ssd(L):
                j = occ[L]
                for h in range(NH):
                    pool.wait_ge(S["dec_sb"], j * NH + h + 1)
                    pool.wait_ge(S["cb_sb"], NG * (j + 1))
                    if h >= 2:
                        pool.wait_ge(S["y_ps"], j * NH + h - 1)
                    pool.tensor_tensor(mm_[:, h % 2, :], dec[:, h % 2, :], cbm[:, h // HPG, :], ALU.mult)\
                        .then_inc(S["m_sb"], 1)

            def mask(rows, b, cols, at):
                pool.memset(bias[rows, b, cols], NEG).then_inc(S["bias_sb"], 1)
                pool.wait_ge(S["bias_sb"], at)

            def swa():
                pool.wait_ge(S["ln_done"], TT * 2)
                pool.iota(lg[:, 0, 0:P], pattern=[[-1, P]], base=0, channel_multiplier=1, allow_small_or_imprecise_dtypes=True)
                pool.iota(lg[:, 0, P:SC], pattern=[[-1, T]], base=P, channel_multiplier=1, allow_small_or_imprecise_dtypes=True).then_inc(S["pool_step"], 1)
                pool.wait_ge(S["pool_step"], 2)
                pool.tensor_scalar(lg[:, 1, :], lg[:, 0, :], 0.0, -2.0, ALU.max, ALU.mult).then_inc(S["pool_step"], 1)
                pool.wait_ge(S["pool_step"], 3)
                pool.tensor_tensor(bias[:, 0, :], lg[:, 0, :], lg[:, 1, :], ALU.add).then_inc(S["pool_step"], 1)
                pool.wait_ge(S["pool_step"], 4)
                mask(slice(0, CH), 0, slice(CH, P), 1)
                mask(slice(0, CH), 0, slice(P + 3 * CH, SC), 2)
                mask(slice(0, P), 0, slice(P, P + CH), 3)
                mask(slice(CH, P), 0, slice(P + CH, P + 2 * CH), 4)

            def ca():
                pool.wait_ge(S["ln_done"], TT * 4)
                pool.dma_start(rel[0:AH, :], a["ca_rel_bias"][0]).then_inc(S["rel_in"], 16)
                for b in range(2):
                    mask(slice(0, CH), b, slice(CH, P), 5 + 2 * b)
                    mask(slice(0, CH), b, slice(P + 3 * CH, SC), 6 + 2 * b)
                pool.wait_ge(S["rev_sb"], 1)
                pool.dma_start(rev_dram, revx[0:AH, :].unsqueeze(1).to_broadcast([AH, CH, 384])).then_inc(S["rev_out"], 16)
                pool.wait_ge(S["rev_out"], 16)
                for h in range(AH):
                    if h >= 2:
                        pool.wait_ge(S["max_sb"], AH + h - 1)
                    b = h % 2

                    def toeplitz(q0, width, col):
                        src = bass.AP(rev_dram.tensor, h * CH * 384 + 255 - q0, [[383, CH], [1, width]])
                        pool.dma_start(bias[q0 % P:q0 % P + CH, b, col:col + width], src)\
                            .then_inc(S[f"bias_in{b}"], 16)

                    toeplitz(0, CH, 0)
                    toeplitz(CH, P, 0)
                    toeplitz(P, 3 * CH, P)
                    toeplitz(3 * CH, T, P)

            gains(0)
            for L in range(DEPTH):
                if KINDS[L] == SSD:
                    ssd(L)
                elif KINDS[L] == SWA:
                    swa()
                else:
                    ca()
                gains(2 * L + 1)
                if L < DEPTH - 1:
                    gains(2 * L + 2)


_INS = ["x", "ssd_w_in", "ssd_conv_w", "ssd_conv_b", "ssd_dt_bias", "ssd_a_log", "ssd_d_skip", "ssd_norm_w", "ssd_w_out",
        "swa_w_in", "swa_sinks", "swa_w_out", "ca_w_in", "ca_rel_bias", "ca_w_out", "router_w", "router_bias",
        "moe_w_gate", "moe_w_up", "moe_w_down", "ln_mix_g", "ln_mix_b", "ln_ffn_g", "ln_ffn_b"]


def kernel(**inputs):
    import numpy as _np
    import concourse.bacc as _bacc
    from concourse import mybir as _mybir
    from concourse.bass_utils import run_bass_kernel_spmd as _run

    nc = _bacc.Bacc("TRN2", target_bir_lowering=False, num_devices=1)
    arrays, aps = {}, {}
    for name in _INS:
        arr = _np.ascontiguousarray(inputs[name])
        arrays[f"in_{name}"] = arr
        aps[name] = nc.dram_tensor(f"in_{name}", arr.shape, _mybir.dt.from_np(arr.dtype), kind="ExternalInput").ap()
    out = nc.dram_tensor("out", (T, D), _mybir.dt.float32, kind="ExternalOutput").ap()
    trunk(nc, aps, out)
    r = _run(nc, [arrays], core_ids=[0])
    return r.results[0]["out"].reshape(1, T, D)
```

```python
from contextlib import ExitStack

import concourse.bass as bass
from concourse import mybir

F32 = mybir.dt.float32
BF16 = mybir.dt.bfloat16
F32R = mybir.dt.float32r
I32 = mybir.dt.int32
ALU = mybir.AluOpType
ACT = mybir.ActivationFunctionType
AX = mybir.AxisListType

P = 128
D = 1024
T = 256
TT = T // P
KT = D // P
DEPTH = 4
CH = 64
ALPHA = (2.0 * DEPTH) ** 0.25
EPS = 1e-5
DI = 2 * D
NH = 32
NG = 4
HPG = NH // NG
XBC = DI + 2 * NG * 128
CT_X = DI // P
CT_BC = XBC // P
CONV = 4
AH = 16
DH = 64
KVH = 4
REL_CLIP = 128
N_REL = CH - 1 + REL_CLIP + 1
NEG = -1.0e30
NE = 16
FF = D // 4
FT = FF // P
UW = 2048
RING = 6
UPE = 3
BODY = 4
PEEL = 2
CAP = CH
PAIR = 2
E0 = 2
FILLS = 4 * NE // PAIR
SC = P + T

SSD, SWA, CA = 0, 1, 2
KINDS = [i % 3 for i in range(DEPTH)]
N_IN = {SSD: (DI + XBC) // 256, SWA: 6, CA: 12}
N_OUT = {SSD: 8, SWA: 4, CA: 4}
UNIT0 = []
PROJ0 = []
_u = _p = 0
for _k in KINDS:
    UNIT0.append(_u)
    PROJ0.append(_p)
    _u += N_IN[_k] + N_OUT[_k]
    _p += N_IN[_k]
N_UNITS = _u


def trunk(nc, a, out):
    ctx = ExitStack()
    with ctx:
        def sb(name, shape, dt=F32):
            return ctx.enter_context(nc.sbuf_tensor(name, shape, dt))

        def sem(name):
            return ctx.enter_context(nc.semaphore(name))

        ring = sb("ring", [P, RING, UW])
        x = sb("x", [P, TT, D])
        ln_gb = sb("ln_gb", [P, 2, D])
        ident = sb("ident", [P, P])
        ones = sb("ones", [P, P])
        triu = sb("triu", [P, T])
        rank = sb("rank", [P, NE])
        par = sb("par", [P, 2, 176])
        d_rows = sb("d_rows", [CT_X, 2, 2])
        w_dt = sb("w_dt", [P, 2, KT, NH])
        dtb = sb("dtb", [1, 2, NH])
        a_row = sb("a_row", [1, 2, NH])
        a_bc = sb("a_bc", [P, 2, NH])
        w_rt = sb("w_rt", [P, KT, NE])
        rt_bias = sb("rt_bias", [P, NE])
        sinks = sb("sinks", [P, AH])
        st = sb("st", [P, TT, 2, 6])
        mv = sb("mv", [P, TT, 2])
        rs = sb("rs", [P, TT])
        eps = None
        iota_c = sb("iota_c", [P, 2 * CAP])
        ident_r = sb("ident_r", [P, P], F32R)
        zero = sb("zero", [1, 512], F32R)
        nwin = sb("nwin", [1, 1], I32)

        mix_ctx = ExitStack()
        xT = mix_ctx.enter_context(nc.sbuf_tensor("xT", [P, KT, T], F32))
        arena = mix_ctx.enter_context(nc.sbuf_tensor("arena", [P, 24000], F32))
        mix_ctx.close()
        moe_ctx = ExitStack()

        def mb(name, shape, dt=F32):
            return moe_ctx.enter_context(nc.sbuf_tensor(name, shape, dt))

        slot_tok = mb("slot_tok", [P, NE, T], BF16)
        x_hi = mb("x_hi", [P, TT, D], F32R)
        x_lo = mb("x_lo", [P, TT, D], F32R)
        w_hi = [mb(f"{n}_hi", [P, UW], F32R) for n in ("gate", "up")]
        w_lo = [mb(f"{n}_lo", [P, UW], F32R) for n in ("gate", "up")]
        w_hi.append(mb("down_hi", [P, UW], F32R))
        w_lo.append(mb("down_lo", [P, UW], F32R))
        xg = mb("xg", [P, 2, KT, PAIR, 2 * CAP], F32R)
        disp = mb("disp", [P, TT, NE, 2 * CAP], F32R)
        gates = mb("gates", [P, TT, NE, 2], F32R)
        hi_lo_h = mb("hi_lo_h", [P, FT, 2, CAP], F32R)
        sel = mb("sel", [P, 2, T], F32R)
        fold = mb("fold", [CAP, 512])
        gu = mb("gu", [CAP, 512])
        sil = mb("sil", [CAP, FF])
        hbuf = mb("hbuf", [CAP, FF])
        gate_slot = mb("gate_slot", [P, NE])
        posm = mb("posm", [P, TT, NE])
        rt = mb("rt", [P, 20, TT, NE])
        y_hi = mb("y_hi", [P, 2, D], F32R)
        y_lo = mb("y_lo", [P, 2, D], F32R)
        moe_ctx.close()
        top = [0]

        def take(n, reset=None):
            if reset is not None:
                top[0] = reset
            top[0] += n
            assert top[0] <= 24000
            return arena[:, top[0] - n:top[0]]

        xbc = take(8 * 259, 0).rearrange("p (c t) -> p c t", t=259)
        cacc = take(4 * T).rearrange("p (c t) -> p c t", t=T)
        cv = take(CT_BC * T).rearrange("p (c t) -> p c t", t=T)
        sz = take(CT_X * T).rearrange("p (c t) -> p c t", t=T)
        xdt = take(TT * DI).rearrange("p (a c) -> p a c", a=TT)
        cbm = take(NG * SC).rearrange("p (g c) -> p g c", g=NG)
        seg = take(2 * SC).rearrange("p (g c) -> p g c", g=2)
        dec = take(2 * SC).rearrange("p (g c) -> p g c", g=2)
        mm_ = take(2 * SC).rearrange("p (g c) -> p g c", g=2)
        dts = take(8 * TT * NH).rearrange("p (n c) -> p n c", n=8)
        acT = take(T)
        par_rows = take(4 * P, 0).rearrange("p (j n c) -> p j n c", j=2, n=2)
        gsum = take(NG * T, 0).rearrange("p (g t) -> p g t", g=NG)
        ytmp = take(2 * T).rearrange("p (g t) -> p g t", g=2)
        sq = take(4 * T).rearrange("p (g t) -> p g t", g=4)
        assert top[0] <= 8 * 259 + 4 * T
        qT = take(8 * T, 0).rearrange("p (c t) -> p c t", t=T)
        kT = take(8 * T).rearrange("p (c t) -> p c t", t=T)
        v = take(TT * D).rearrange("p (a c) -> p a c", a=TT)
        oT = take(8 * T).rearrange("p (c t) -> p c t", t=T)
        bias = take(2 * SC).rearrange("p (g c) -> p g c", g=2)
        lg = take(2 * SC).rearrange("p (g c) -> p g c", g=2)
        pT = take(2 * SC).rearrange("p (g c) -> p g c", g=2)
        hst = take(2 * 16).rearrange("p (g c) -> p g c", g=2)
        revx = take(384)
        rel = take(N_REL)
        ps = [ctx.enter_context(nc.psum_tensor(f"ps{i}", [P, 512], F32)) for i in range(8)]
        rev_dram = nc.dram_tensor("rev_dram", (AH, CH, 384), F32, kind="Internal").ap()

        loaded = [sem(f"loaded{s}") for s in range(RING)]
        loaded_moe = [sem(f"loaded_moe{s}") for s in range(RING)]
        S = {n: sem(n) for n in (
            "consts", "par_in", "par_rows_d", "par_ps", "par_sb", "a_exp", "a_ps", "a_sb", "rt_in", "x_in",
            "xt_ps", "xt_sb", "proj_ready", "proj_free", "lngb_in", "out_used", "pos_ps", "nwin_sb", "disp_sb", "xhi_sb", "xlo_sb", "pro_ps", "fill_ps", "fill_sb", "tok_a", "tok_v", "gates_ps", "gates_hl", "gs_sb", "win_done", "posm_sb", "zeroed",
            "gate_used", "up_used", "ht_ps", "yp_ps", "comb_ps", "gate_hi", "down_hi", "fold_sb", "sil_sb", "hth_sb", "yhi_sb", "sel_sb", "sel_tok",
            "up_hi", "gate_lo", "up_lo", "sum_sb", "h_sb", "htl_sb", "ylo_sb", "down_lo", "res_done", "ln_stats", "ln_sqrt",
            "ln_rs", "ln_done", "dve_step", "act_step",
            "dt_ps", "dt_abs", "dt_exp", "dt_u", "dt_ln", "dt_sb", "cum_ps", "cum_sb", "conv_acc", "conv_done",
            "cb_ps", "cb_sb", "xs_ps", "xdt_sb", "bc_ps", "seg_sb", "dec_sb", "m_sb", "y_ps", "y2_sb", "sq_sb",
            "ss_ps", "ss_sb", "ss_sqrt", "yn_sb",
            "bias_sb", "rel_in", "rev_sb", "rev_out", "bias_in0", "bias_in1", "s_ps", "max_sb", "exp_sb", "p_sb", "pt_ps", "pt_sb", "o_ps", "o_sb",
            "rt_ps", "rt_exp", "gates_sb", "store", "pool_step")}

        def par_cw(j, tile, k):
            return par[:, j, k * CT_BC + tile:k * CT_BC + tile + 1]

        def par_d(j, t):
            return par[:, j, 96 + t:97 + t]

        def par_cb(j, tile):
            return par[:, j, 96 + 32 + tile:97 + 32 + tile]

        def par_nw(j, t):
            return par[:, j, 96 + 64 + t:97 + 64 + t]

        occ = {0: 0, 3: 1}
        att = {1: 0, 2: 1}
        order = [("xbc", n) for n in (8, 9, 10, 11, 0, 1, 2, 3, 4, 5, 6, 7)] + [("z", n) for n in range(8)]

        def used(u):
            L = max(n for n in range(DEPTH) if UNIT0[n] <= u)
            n = u - UNIT0[L]
            if n < N_IN[KINDS[L]]:
                return S["proj_ready"], PROJ0[L] + n + 1
            n -= N_IN[KINDS[L]]
            return S["out_used"], sum(N_OUT[k] for k in KINDS[:L]) + n + 1

        def slot(u):
            L = max(n for n in range(DEPTH) if UNIT0[n] <= u)
            return (u - UNIT0[L]) % RING

        def landed(u):
            return sum(slot(n) == slot(u) for n in range(u + 1))

        def landed_moe(gw, o, e, n):
            return (gw * NE + o) * (16 * UPE // RING) + 16 * ((e * UPE + n) // RING + 1)

        lo_sems = ("gate_lo", "up_lo", "down_lo")

        block = ctx.enter_context(nc.Block())

        @block.sync
        def _(sp):
            def put(u, src, g):
                L = max(n for n in range(DEPTH) if UNIT0[n] <= u)
                n = u - UNIT0[L]
                if n >= RING:
                    sp.wait_ge(*used(u - RING))
                elif L > 0:
                    sp.wait_ge(S[lo_sems[n % UPE]], g * NE + (E0 - 1 + n // UPE))
                dst = ring[:, slot(u), :].rearrange("p (a b) -> p a b", a=src.shape[1])
                sp.dma_start(dst, src).then_inc(loaded[slot(u)], 16)

            def w_in_unit(w, c):
                return w.rearrange("(p k) n -> p k n", k=KT)[:, :, c:c + 256]

            def w_out_unit(w, n):
                return w[256 * n:256 * n + 256, :].rearrange("(r p) n -> p r n", r=2)

            g = 0
            for L in range(DEPTH):
                kind = KINDS[L]
                u = UNIT0[L]
                if kind == SSD:
                    j = occ[L]
                    for n, (what, i) in enumerate(order):
                        c = 256 * i + (DI if what == "xbc" else 0)
                        put(u + n, w_in_unit(a["ssd_w_in"][j], c), g)
                    wo = a["ssd_w_out"][j]
                elif kind == SWA:
                    for n in range(N_IN[SWA]):
                        put(u + n, w_in_unit(a["swa_w_in"][0], 256 * n), g)
                    wo = a["swa_w_out"][0]
                else:
                    for n in range(N_IN[CA]):
                        put(u + n, w_in_unit(a["ca_w_in"][0], 256 * n), g)
                    wo = a["ca_w_out"][0]
                u += N_IN[kind]
                for n in range(N_OUT[kind]):
                    put(u + n, w_out_unit(wo, n), g)
                gate_v = a["moe_w_gate"][L].rearrange("e (p k) f -> e p (k f)", k=KT)
                up_v = a["moe_w_up"][L].rearrange("e (p k) f -> e p (k f)", k=KT)
                down_v = a["moe_w_down"][L].rearrange("e (r p) n -> e p r n", r=FT)
                last = UNIT0[L] + N_IN[kind] + N_OUT[kind]

                def experts(gw):
                    with sp.Fori(0, NE // BODY) as i:
                        eb = gw * NE + i * BODY
                        for b in range(BODY):
                            for n, view in enumerate((gate_v, up_v, down_v)):
                                k = b * UPE + n
                                if k < RING:
                                    sp.wait_ge(*used(max(u for u in range(last - RING, last) if slot(u) == k)))
                                sp.wait_ge(S[lo_sems[n]], eb + (E0 + b - RING // UPE + 1))
                                dst = ring[:, k % RING, :]
                                if n == 2:
                                    dst = dst.rearrange("p (r n) -> p r n", r=FT)
                                sp.dma_start(dst, view[i * BODY + b]).then_inc(loaded_moe[k % RING], 16)

                experts(g)
                sp.wait_ge(S["nwin_sb"], L + 1)
                g1 = sp.snap(g + sp.value_load(nwin[0:1, 0:1], min_val=1, max_val=T // CAP))
                with sp.If(g1 > g + 1):
                    with sp.Fori(g + 1, g1) as gw:
                        experts(gw)
                g = g1
            sp.wait_ge(S["ln_done"], 2 * DEPTH * TT)
            sp.dma_start(out.rearrange("(a p) d -> p a d", p=P), x[:]).then_inc(S["store"], 16)
            sp.wait_ge(S["store"], 16)

        @block.tensor
        def _(pe):
            def unit_wait(u):
                pe.wait_ge(loaded[slot(u)], 16 * landed(u))

            def unit(u, r):
                return ring[:, slot(u), :].rearrange("p (a b) -> p a b", a=r)

            def turn_x(n):
                if n == 0:
                    pe.wait_ge(S["x_in"], 16)
                    pe.wait_ge(S["consts"], 7)
                else:
                    pe.wait_ge(S["ln_done"], TT * n)
                for kp in range(4):
                    for k in (2 * kp, 2 * kp + 1):
                        for tt in range(TT):
                            c = (k % 2) * T + tt * P
                            t = pe.transpose(ps[kp][:, c:c + P], x[:, tt, k:D:KT], ident[:])
                    t.then_inc(S["xt_ps"], 1)

            def project_in(u, pg):
                unit_wait(u)
                if pg >= 4:
                    pe.wait_ge(S["proj_free"], pg - 3)
                w = unit(u, KT)
                for c in range(2):
                    for k in range(KT):
                        t = pe.matmul(ps[pg % 4][:, c * T:c * T + T], w[:, k, c * P:c * P + P], xT[:, k, :],
                                      start=k == 0, stop=k == KT - 1)
                return t

            def project_out(L, lhs, n_ct, ready):
                u0 = UNIT0[L] + N_IN[KINDS[L]]
                for n in range(n_ct // 2):
                    unit_wait(u0 + n)
                    w = unit(u0 + n, 2)
                    for r in range(2):
                        ct = 2 * n + r
                        ready(ct)
                        for tt in range(TT):
                            for half in range(2):
                                t = pe.matmul(ps[4 + 2 * tt + half][:, :], lhs[:, ct, tt * P:tt * P + P],
                                              w[:, r, half * 512:half * 512 + 512],
                                              start=ct == 0, stop=ct == n_ct - 1)
                    t.then_inc(S["out_used"], 1)

            def xt_wait(n):
                pe.wait_ge(S["xt_sb"], 4 * (n + 1))

            def ssd(L):
                j = occ[L]
                pg0 = PROJ0[L]
                u0 = UNIT0[L]
                xt_wait(2 * L)
                for tt in range(TT):
                    o = ps[4][:, tt * NH:tt * NH + NH]
                    for k in range(KT):
                        pe.matmul(o, xT[:, k, tt * P:tt * P + P], w_dt[:, j, k, :], start=k == 0, stop=False)
                    t = pe.matmul(o, ones[0:1, :], dtb[0:1, j, :], start=False, stop=True)
                t.then_inc(S["dt_ps"], 1)
                for n in range(4):
                    project_in(u0 + n, pg0 + n).then_inc(S["proj_ready"], 1)
                pe.wait_ge(S["dt_sb"], 2 * (j + 1))
                da = dts[:, 1, :].rearrange("p (a h) -> p a h", a=TT)
                pe.matmul(ps[5][:, 0:NH], triu[:, 0:P], da[:, 0, :], start=True, stop=True)
                pe.matmul(ps[5][:, NH:2 * NH], ones[:, :], da[:, 0, :], start=True, stop=False)
                pe.matmul(ps[5][:, NH:2 * NH], triu[:, 0:P], da[:, 1, :], start=False, stop=True)
                pe.matmul(ps[6][0:NH, 0:T], da[:, 0, :], triu[:, :], start=True, stop=False)
                pe.matmul(ps[6][0:NH, P:T], da[:, 1, :], triu[:, 0:P], start=False, stop=True)\
                    .then_inc(S["cum_ps"], 1)
                for n in range(4, 12):
                    project_in(u0 + n, pg0 + n).then_inc(S["proj_ready"], 1)
                pe.wait_ge(S["conv_done"], j * CT_BC + 8)
                pe.wait_ge(S["cum_sb"], 2 * (j + 1))
                for g in range(NG):
                    bt, c_t = cv[:, CT_X + g, :], cv[:, CT_X + NG + g, :]
                    pe.matmul(ps[4 + g][:, 0:T], bt[:, 0:P], c_t[:, :], start=True, stop=True)
                    pe.matmul(ps[4 + g][:, T:SC], bt[:, P:T], c_t[:, P:T], start=True, stop=True)\
                        .then_inc(S["cb_ps"], 1)
                for n in range(12, 20):
                    project_in(u0 + n, pg0 + n).then_inc(S["proj_ready"], 1)
                pe.wait_ge(S["conv_done"], j * CT_BC + 24)
                for q in range(8):
                    tt, c4 = q % 2, q // 2
                    if q < 4:
                        pe.wait_ge(S["cb_sb"], NG * j + q + 1)
                    else:
                        pe.wait_ge(S["xdt_sb"], 8 * j + q - 3)
                    for c in range(4):
                        t = pe.transpose(ps[4 + q % 4][:, c * P:c * P + P], cv[:, 4 * c4 + c, tt * P:tt * P + P], ident[:])
                    t.then_inc(S["xs_ps"], 1)

                def bc(h):
                    if h == 0:
                        pe.wait_ge(S["proj_free"], pg0 + 20)
                    if h >= 3:
                        pe.wait_ge(S["seg_sb"], 2 * (j * NH + h - 2))
                    pe.matmul(ps[h % 3][:, 0:T], ident[0:NH, h:h + 1].to_broadcast([NH, P]), acT[0:NH, 0:T],
                              start=True, stop=True)
                    pe.matmul(ps[h % 3][:, T:SC], ident[0:NH, h:h + 1].to_broadcast([NH, P]), acT[0:NH, P:T],
                              start=True, stop=True).then_inc(S["bc_ps"], 1)

                def yh(h):
                    b = 4 + (h // 4) % 4
                    if h == 0:
                        pe.wait_ge(S["xdt_sb"], 8 * (j + 1))
                    if h % 4 == 0 and h >= 16:
                        pe.wait_ge(S["y2_sb"], j * CT_X + 2 * (h // 4 - 3))
                    pe.wait_ge(S["m_sb"], j * NH + h + 1)
                    lo = DH * (h % 2)
                    c = T * ((h % 4) // 2)
                    o = ps[b][lo:lo + DH, :]
                    pe.matmul(o[:, c:c + T], xdt[:, 0, h * DH:h * DH + DH], mm_[:, h % 2, 0:T], start=True, stop=False)
                    t = pe.matmul(o[:, c + P:c + T], xdt[:, 1, h * DH:h * DH + DH], mm_[:, h % 2, T:SC],
                                  start=False, stop=True)
                    t.then_inc(S["y_ps"], 1)

                def sumsq(g):
                    if g >= 1:
                        pe.wait_ge(S["ss_sb"], j * NG + g)
                    for c in range(4):
                        pe.wait_ge(S["sq_sb"], j * CT_X + 4 * g + c + 1)
                        t = pe.matmul(ps[3][:, (g % 2) * T:(g % 2) * T + T], ones[:, :], sq[:, c, :],
                                      start=c == 0, stop=c == 3)
                    t.then_inc(S["ss_ps"], 1)

                bc(0)
                bc(1)
                for h in range(NH):
                    if h + 2 < NH:
                        bc(h + 2)
                    yh(h)
                    if h % 8 == 3 and h >= 8:
                        sumsq(h // 8 - 1)
                sumsq(NG - 1)
                project_out(L, sz, CT_X, lambda ct: pe.wait_ge(S["yn_sb"], j * CT_X + ct + 1))

            def attention(L):
                m = att[L]
                kind = KINDS[L]
                pg0, u0 = PROJ0[L], UNIT0[L]
                xt_wait(2 * L)
                nqk = 5 if kind == SWA else 8
                for n in range(nqk):
                    project_in(u0 + n, pg0 + n).then_inc(S["proj_ready"], 1)
                for n in range(nqk, N_IN[kind]):
                    pg = pg0 + n
                    unit_wait(u0 + n)
                    pe.wait_ge(S["proj_free"], pg - 3)
                    w = unit(u0 + n, KT)
                    for tt in range(TT):
                        for k in range(KT):
                            t = pe.matmul(ps[pg % 4][:, tt * T:tt * T + T], xT[:, k, tt * P:tt * P + P], w[:, k, :],
                                          start=k == 0, stop=k == KT - 1)
                    t.then_inc(S["proj_ready"], 1)
                pe.wait_ge(S["proj_free"], pg0 + N_IN[kind])

                def heads(h):
                    kvh = h // (AH // KVH) if kind == SWA else h
                    lo = DH * (h % 2)
                    kc = kvh if kind == SWA else h // 2
                    return lo, kvh, kc

                def scores(h):
                    lo, kvh, kc = heads(h)
                    b = h % 2
                    if h >= 2:
                        pe.wait_ge(S["max_sb"], AH * m + h - 1)
                    q = qT[lo:lo + DH, h // 2, :]
                    k = kT[lo:lo + DH, kc, :]
                    pe.matmul(ps[b][:, 0:P], q[:, 0:P], k[:, 0:P], start=True, stop=True)
                    pe.matmul(ps[b][:, P:SC], q[:, P:T], k[:, :], start=True, stop=True).then_inc(S["s_ps"], 1)

                def turn_p(h):
                    b = 2 + h % 2
                    pe.wait_ge(S["p_sb"], AH * m + h + 1)
                    if h >= 2:
                        pe.wait_ge(S["pt_sb"], AH * m + h - 1)
                    pe.transpose(ps[b][:, 0:P], lg[:, h % 2, 0:P], ident[:])
                    pe.transpose(ps[b][:, P:2 * P], lg[:, h % 2, P:2 * P], ident[:])
                    pe.transpose(ps[b][:, 2 * P:SC], lg[:, h % 2, 2 * P:SC], ident[:]).then_inc(S["pt_ps"], 1)

                def pv(h):
                    lo, kvh, kc = heads(h)
                    b = 4 + (h // 4) % 4
                    pe.wait_ge(S["pt_sb"], AH * m + h + 1)
                    c = T * ((h % 4) // 2)
                    o = ps[b][lo:lo + DH, :]
                    pe.matmul(o[:, c:c + T], v[:, 0, kvh * DH:kvh * DH + DH], pT[:, h % 2, 0:T], start=True, stop=False)
                    pe.matmul(o[:, c + P:c + T], v[:, 1, kvh * DH:kvh * DH + DH], pT[:, h % 2, T:SC],
                              start=False, stop=True).then_inc(S["o_ps"], 1)

                scores(0)
                scores(1)
                for h in range(AH):
                    turn_p(h)
                    if h + 2 < AH:
                        scores(h + 2)
                    pv(h)
                pe.wait_ge(S["o_sb"], 4 * (m + 1))
                project_out(L, oT, 8, lambda ct: None)

            def moe(L, g):
                xt_wait(2 * L + 1)
                for tt in range(TT):
                    for k in range(KT):
                        t = pe.matmul(ps[4][:, tt * NE:tt * NE + NE], xT[:, k, tt * P:tt * P + P], w_rt[:, k, :],
                                      start=k == 0, stop=k == KT - 1)
                t.then_inc(S["rt_ps"], 1)
                pe.wait_ge(S["sel_sb"], L + 1)
                chosen = rt[:, 13, :, :]
                pe.matmul(ps[5][:, 0:NE], triu[:, 0:P], chosen[:, 0, :], start=True, stop=True)
                pe.matmul(ps[5][:, NE:2 * NE], ones[:, :], chosen[:, 0, :], start=True, stop=False)
                pe.matmul(ps[5][:, NE:2 * NE], triu[:, 0:P], chosen[:, 1, :], start=False, stop=True)
                pe.matmul(ps[5][:, 2 * NE:3 * NE], ones[:, :], chosen[:, 0, :], start=True, stop=False)
                pe.matmul(ps[5][:, 2 * NE:3 * NE], ones[:, :], chosen[:, 1, :], start=False, stop=True)\
                    .then_inc(S["pos_ps"], 1)
                if L == 0:
                    pe.wait_ge(S["zeroed"], 2)
                pe.wait_ge(S["nwin_sb"], L + 1)
                for bank in range(4, 8):
                    pe.matmul(ps[bank][:, :], zero[0:1, 0:P], zero[0:1, :], start=True, stop=False,
                              skip_group_check=True)
                g1 = pe.snap(g + pe.value_load(nwin[0:1, 0:1], min_val=1, max_val=T // CAP))
                pe.wait_ge(S["xlo_sb"], L + 1)

                def gather(bank, kp, pair):
                    for k in (2 * kp, 2 * kp + 1):
                        o = ps[bank][:, (k % 2) * T:(k % 2) * T + T].rearrange("p (e m c) -> p e m c", e=PAIR, m=2)
                        for part, src in enumerate((x_hi, x_lo)):
                            for tt in range(TT):
                                t = pe.matmul(o[:, :, part, :], src[:, tt, k:D:KT], disp[:, tt, pair, 0:CAP],
                                              start=tt == 0, stop=tt == TT - 1)
                    t.then_inc(S["fill_ps"], 1)

                def gate_up(gw, o, e):
                    E = gw * NE + o + (E0 + e)
                    pe.wait_ge(S["fill_sb"], gw * FILLS + o * 2 + (4 + 4 * (e // PAIR)))
                    pe.wait_ge(S["htl_sb"], E)
                    for n, (hi_ready, lo_ready, done) in enumerate((("gate_hi", "gate_lo", "gate_used"),
                                                                    ("up_hi", "up_lo", "up_used"))):
                        pe.wait_ge(S[hi_ready], E + 1)
                        pe.wait_ge(S[lo_ready], E + 1)
                        for k in range(KT):
                            for m, w in enumerate((w_hi[n], w_lo[n])):
                                t = pe.matmul(ps[0][:, n * FF:n * FF + FF], xg[:, (e // PAIR) % 2, k, e % PAIR, :],
                                              w[:, k * FF:k * FF + FF],
                                              start=k == 0 and m == 0, stop=k == KT - 1 and m == 1)
                        t.then_inc(S[done], 1)

                def turn_h(gw, o, e):
                    pe.wait_ge(S["consts"], 7)
                    pe.wait_ge(S["h_sb"], gw * NE + o + (E0 + e + 1))
                    for f in range(FT):
                        t = pe.transpose(ps[0][:, f * CAP:f * CAP + CAP], hbuf[:, f * P:f * P + P], ident[0:CAP, 0:CAP])
                    t.then_inc(S["ht_ps"], 1)

                def down(gw, o, e):
                    E = gw * NE + o + (E0 + e)
                    pe.wait_ge(S["htl_sb"], E + 1)
                    pe.wait_ge(S["down_hi"], E + 1)
                    pe.wait_ge(S["down_lo"], E + 1)
                    pe.wait_ge(S["ylo_sb"], 2 * E)
                    for half in range(2):
                        for f in range(FT):
                            for m, w in enumerate((w_hi[2], w_lo[2])):
                                c = f * D + half * 512
                                t = pe.matmul(ps[1 + half][:, :], hi_lo_h[:, f, :, :].rearrange("p m c -> p (m c)"), w[:, c:c + 512],
                                              start=f == 0 and m == 0, stop=f == FT - 1 and m == 1)
                        t.then_inc(S["yp_ps"], 1)

                def combine(gw, o, e):
                    E = gw * NE + o + (E0 + e)
                    pe.wait_ge(S["sel_tok"], E + 1)
                    for half in range(2):
                        pe.wait_ge(S["ylo_sb"], 2 * E + half + 1)
                        for tt in range(TT):
                            for y in (y_hi, y_lo):
                                t = pe.matmul(ps[4 + 2 * tt + half][:, :], sel[:, e % 2, tt * P:tt * P + P],
                                              y[:, e % 2, half * 512:half * 512 + 512], start=False, stop=False,
                                              skip_group_check=True)
                    t.then_inc(S["comb_ps"], 1)

                def step(gw, o, e):
                    if e < NE:
                        gate_up(gw, o, e)
                    if 1 <= e <= NE:
                        down(gw, o, e - 1)
                    for r in range(2):
                        if e < NE - PAIR:
                            n = 2 * (e % PAIR) + r
                            pair = bass.ds(o + (e // PAIR + 1) * PAIR, PAIR)
                            pe.wait_ge(S["fill_sb"], gw * FILLS + o * 2 + (4 + 4 * (e // PAIR) + n))
                            gather(3, n, pair)
                        if r == 0:
                            if e >= 2:
                                combine(gw, o, e - 2)
                            if e < NE:
                                turn_h(gw, o, e)

                with pe.Fori(g, g1) as gw:
                    pe.wait_ge(S["disp_sb"], gw * 2 + 1)
                    for kp in range(4):
                        gather(kp, kp, slice(0, PAIR))
                    pe.wait_ge(S["fill_sb"], gw * FILLS + 4)
                    pe.wait_ge(S["gates_hl"], L + 1)
                    pe.wait_ge(S["disp_sb"], gw * 2 + 2)
                    for e in range(NE):
                        for tt in range(TT):
                            t = pe.matmul(ps[0][:, 2 * e:2 * e + 2], disp[:, tt, e, :], gates[:, tt, e, :],
                                          start=tt == 0, stop=tt == TT - 1)
                    t.then_inc(S["gates_ps"], 1)
                    for q in range(NE // 2):
                        if q >= 3:
                            pe.wait_ge(S["tok_v" if (q - 3) % 2 else "tok_a"], gw * 4 + ((q - 3) // 2 + 1))
                        for r in range(2):
                            for tt in range(TT):
                                t = pe.matmul(ps[1 + q % 3][:, r * T + tt * P:r * T + tt * P + P], disp[:, tt, 2 * q + r, :],
                                              ident_r[:, :], start=True, stop=True)
                        t.then_inc(S["pro_ps"], 1)
                    pe.wait_ge(S["gs_sb"], gw + 1)
                    pe.wait_ge(S["tok_a"], gw * 4 + 4)
                    pe.wait_ge(S["tok_v"], gw * 4 + 4)
                    for e in range(PEEL):
                        step(gw, 0, e)
                    with pe.Fori(0, (NE - 2 * PEEL) // BODY) as i:
                        o = i * BODY
                        for e in range(PEEL, PEEL + BODY):
                            step(gw, o, e)
                    for e in range(NE - PEEL, NE + 2):
                        step(gw, 0, e)
                return g1

            pe.wait_ge(S["consts"], 7)
            pe.wait_ge(S["par_in"], 16 * 11)
            pe.wait_ge(S["par_rows_d"], 2)
            for j in range(2):
                pe.transpose(ps[4 + j][:, 0:96], par_rows[0:96, j, 0, :], ident[0:96, 0:96])
                pe.transpose(ps[4 + j][:, 96:176], par_rows[0:80, j, 1, :], ident[0:80, 0:80]).then_inc(S["par_ps"], 1)
            pe.wait_ge(S["a_exp"], 1)
            pe.matmul(ps[6][:, 0:2 * NH], ones[0:1, :], a_row[0:1, :, :].rearrange("p a b -> p (a b)"),
                      start=True, stop=True).then_inc(S["a_ps"], 1)
            pe.wait_ge(S["par_sb"], 2)
            pe.wait_ge(S["a_sb"], 1)
            for name, n in (("gate_used", 1), ("up_used", 1), ("ht_ps", 1), ("yp_ps", 2), ("comb_ps", 1)):
                pe.nop().then_inc(S[name], E0 * n)
            turn_x(0)
            g = 0
            for L in range(DEPTH):
                if KINDS[L] == SSD:
                    ssd(L)
                else:
                    attention(L)
                turn_x(2 * L + 1)
                g = moe(L, g)
                if L < DEPTH - 1:
                    turn_x(2 * L + 2)

        @block.scalar
        def _(act):
            steps = [0]

            def link(ins):
                steps[0] += 1
                ins.then_inc(S["act_step"], 1)
                act.wait_ge(S["act_step"], steps[0])

            act.wait_ge(S["pool_step"], 1)
            for j in range(2):
                act.dma_start(par_rows[0:96, j, 0, :], a["ssd_conv_w"][j].rearrange("k (c p) -> (k c) p", p=P)).then_inc(S["par_in"], 16)
                act.dma_start(par_rows[32:56, j, 1, :], a["ssd_conv_b"][j].rearrange("(c p) -> c p", p=P)).then_inc(S["par_in"], 16)
                act.dma_start(par_rows[64:80, j, 1, :], a["ssd_norm_w"][j].rearrange("(c p) -> c p", p=P)).then_inc(S["par_in"], 16)
            act.dma_start(d_rows[:, :, :], a["ssd_d_skip"].rearrange("j (c r) -> c j r", r=2)).then_inc(S["par_in"], 16)
            act.dma_start(a_row[0:1, :, :], a["ssd_a_log"].rearrange("(o j) h -> o j h", o=1)).then_inc(S["par_in"], 16)
            act.dma_start(dtb[0:1, :, :], a["ssd_dt_bias"].rearrange("(o j) h -> o j h", o=1)).then_inc(S["par_in"], 16)
            for j in range(2):
                act.dma_start(w_dt[:, j, :, :], a["ssd_w_in"][j].rearrange("(p k) n -> p k n", k=KT)[:, :, DI + XBC:DI + XBC + NH]).then_inc(S["par_in"], 16)
            act.wait_ge(S["par_in"], 16 * 11)
            act.activation(a_row[0:1, :, :], a_row[0:1, :, :], ACT.Exp).then_inc(S["a_exp"], 1)

            def xt_evac(n):
                for kp in range(4):
                    act.wait_ge(S["xt_ps"], 4 * n + kp + 1)
                    act.activation(xT[:, 2 * kp:2 * kp + 2, :], ps[kp][:, :].rearrange("p (a t) -> p a t", a=2), ACT.Copy)\
                        .then_inc(S["xt_sb"], 1)

            def norm(n):
                for tt in range(TT):
                    act.wait_ge(S["ln_stats"], TT * n + tt + 1)
                    act.activation(rs[:, tt:tt + 1], mv[:, tt, 1:2], ACT.Sqrt).then_inc(S["ln_sqrt"], 1)

            def ssd(L):
                j = occ[L]
                pg0 = PROJ0[L]

                def silu_conv(n):
                    t0 = 2 * order[n][1]
                    act.wait_ge(S["conv_acc"], j * 12 + n + 1)
                    for c in range(2):
                        act.activation(cv[:, t0 + c, :], cacc[:, 2 * (n % 2) + c, :], ACT.Silu, bias=par_cb(j, t0 + c))\
                            .then_inc(S["conv_done"], 1)

                def softplus_exp():
                    act.wait_ge(S["dt_abs"], 2 * j + 2)
                    act.activation(dts[:, 2, :], dts[:, 3, :], ACT.Exp).then_inc(S["dt_exp"], 1)

                def softplus_ln():
                    act.wait_ge(S["dt_u"], j + 1)
                    act.activation(dts[:, 5, :], dts[:, 4, :], ACT.Ln).then_inc(S["dt_ln"], 1)

                softplus_exp()
                softplus_ln()
                for n in range(12):
                    act.wait_ge(S["proj_ready"], pg0 + n + 1)
                    if n >= 4:
                        act.wait_ge(S["conv_acc"], j * 12 + n - 3)
                    s = 2 * (n % 4)
                    act.activation(xbc[:, s:s + 2, 3:259], ps[(pg0 + n) % 4][:, :].rearrange("p (a t) -> p a t", a=2),
                                   ACT.Copy).then_inc(S["proj_free"], 1)
                    if n >= 1:
                        silu_conv(n - 1)
                silu_conv(11)
                for n in range(12, 20):
                    act.wait_ge(S["proj_ready"], pg0 + n + 1)
                    t0 = 2 * order[n][1]
                    act.activation(sz[:, t0:t0 + 2, :], ps[(pg0 + n) % 4][:, :].rearrange("p (a t) -> p a t", a=2),
                                   ACT.Silu).then_inc(S["proj_free"], 1)
                for h in range(NH):
                    act.wait_ge(S["seg_sb"], 2 * (j * NH + h + 1))
                    if h >= 2:
                        act.wait_ge(S["m_sb"], j * NH + h - 1)
                    act.activation(dec[:, h % 2, :], seg[:, h % 2, :], ACT.Exp).then_inc(S["dec_sb"], 1)
                    if h % 4 == 1 and h >= 4:
                        square(j, h // 4 - 1)
                square(j, 7)
                act.wait_ge(S["ss_sb"], NG * (j + 1))
                act.activation(gsum[:, :, :], gsum[:, :, :], ACT.Sqrt).then_inc(S["ss_sqrt"], 1)

            def square(j, q):
                for c in (2 * q, 2 * q + 1):
                    act.wait_ge(S["y2_sb"], j * CT_X + c + 1)
                    if c >= 4:
                        act.wait_ge(S["ss_ps"], j * NG + c // 4)
                    act.activation(sq[:, c % 4, :], sz[:, c, :], ACT.Square).then_inc(S["sq_sb"], 1)

            def attention(L):
                m = att[L]
                kind = KINDS[L]
                pg0 = PROJ0[L]
                scale = float(DH) ** -0.5
                for n in range(4):
                    act.wait_ge(S["proj_ready"], pg0 + n + 1)
                    act.activation(qT[:, 2 * n:2 * n + 2, :], ps[(pg0 + n) % 4][:, :].rearrange("p (a t) -> p a t", a=2),
                                   ACT.Copy, scale=scale).then_inc(S["proj_free"], 1)
                if kind == SWA:
                    act.wait_ge(S["proj_ready"], pg0 + 5)
                    bank = ps[(pg0 + 4) % 4]
                    for g in range(KVH):
                        src = bank[DH * (g % 2):DH * (g % 2) + DH, (g // 2) * T:(g // 2) * T + T]
                        for half in range(2):
                            ins = act.activation(kT[DH * half:DH * half + DH, g, :], src, ACT.Copy)
                            if g == KVH - 1 and half == 1:
                                ins.then_inc(S["proj_free"], 1)
                    nv = 5
                else:
                    for n in range(4, 8):
                        act.wait_ge(S["proj_ready"], pg0 + n + 1)
                        act.activation(kT[:, 2 * n - 8:2 * n - 6, :],
                                       ps[(pg0 + n) % 4][:, :].rearrange("p (a t) -> p a t", a=2),
                                       ACT.Copy).then_inc(S["proj_free"], 1)
                    nv = 8
                for n in range(nv, N_IN[kind]):
                    act.wait_ge(S["proj_ready"], pg0 + n + 1)
                    c = 256 * (n - nv)
                    act.activation(v[:, :, c:c + 256], ps[(pg0 + n) % 4][:, :].rearrange("p (a t) -> p a t", a=2),
                                   ACT.Copy).then_inc(S["proj_free"], 1)
                for h in range(AH):
                    act.wait_ge(S["max_sb"], AH * m + h + 1)
                    b = h % 2
                    act.activation(lg[:, b, 0:P], lg[:, b, 0:P], ACT.Exp, bias=hst[:, b, 0:1],
                                   accum_out=hst[:, b, 2:3])
                    if kind == SWA:
                        act.activation(hst[:, b, 4:6], hst[:, b, 0:2], ACT.Exp, bias=sinks[:, h:h + 1])
                    act.activation(lg[:, b, P:SC], lg[:, b, P:SC], ACT.Exp, bias=hst[:, b, 1:2],
                                   accum_out=hst[:, b, 3:4]).then_inc(S["exp_sb"], 1)
                    act.wait_ge(S["pt_ps"], AH * m + h + 1)
                    if h >= 2:
                        act.wait_ge(S["o_ps"], AH * m + h - 1)
                    act.activation(pT[:, b, :], ps[2 + b][:, 0:SC], ACT.Copy).then_inc(S["pt_sb"], 1)
                    if h % 4 == 3:
                        act.wait_ge(S["o_ps"], AH * m + h + 1)
                        c = h // 4
                        act.activation(oT[:, 2 * c:2 * c + 2, :], ps[4 + c][:, :].rearrange("p (a t) -> p a t", a=2),
                                       ACT.Copy).then_inc(S["o_sb"], 1)

            def hi(gw, o, e, n, name, used_name, used_per):
                act.wait_ge(loaded_moe[(e * UPE + n) % RING], landed_moe(gw, o, e, n))
                act.wait_ge(S[used_name], (gw * NE + o + (E0 + e)) * used_per)
                act.activation(w_hi[n][:, :], ring[:, (e * UPE + n) % RING, :], ACT.Copy).then_inc(S[name], 1)

            def moe(L, g):
                act.activation(x_hi[:, :, :], x[:, :, :], ACT.Copy).then_inc(S["xhi_sb"], 1)
                act.wait_ge(S["rt_ps"], L + 1)
                act.activation(rt[:, 1, :, :], ps[4][:, 0:TT * NE].rearrange("p (a e) -> p a e", a=TT), ACT.Exp,
                               scale=-1.0).then_inc(S["rt_exp"], 1)
                act.wait_ge(S["nwin_sb"], L + 1)
                g1 = act.snap(g + act.value_load(nwin[0:1, 0:1], min_val=1, max_val=T // CAP))

                def fill_evac(gw, o, n, buf, kp, bank):
                    act.wait_ge(S["fill_ps"], gw * FILLS + o * 2 + (n + 1))
                    act.activation(xg[:, buf, 2 * kp:2 * kp + 2, :, :].rearrange("p k e c -> p (k e c)"),
                                   ps[bank][:, :], ACT.Copy).then_inc(S["fill_sb"], 1)

                def step(gw, o, e):
                    E = gw * NE + o + (E0 + e)
                    if e + 1 < NE:
                        hi(gw, o, e + 1, 0, "gate_hi", "gate_used", 1)
                    if e < NE:
                        act.wait_ge(S["up_used"], E + 1)
                        act.activation(fold[:, :], ps[0][CAP:P, :], ACT.Copy).then_inc(S["fold_sb"], 1)
                    if 1 <= e <= NE:
                        act.wait_ge(S["comb_ps"], E - 2)
                        act.activation(sel[:, (e - 1) % 2, :].unsqueeze(1), slot_tok[:, bass.ds(o + (e - 1), 1), :], ACT.Copy)\
                            .then_inc(S["sel_tok"], 1)
                        for half in range(2):
                            c = slice(half * 512, half * 512 + 512)
                            act.wait_ge(S["yp_ps"], 2 * E + (half - 1))
                            act.activation(y_hi[:, (e - 1) % 2, c], ps[1 + half][:, :], ACT.Copy).then_inc(S["yhi_sb"], 1)
                    if e < NE:
                        hi(gw, o, e, 2, "down_hi", "yp_ps", 2)
                        act.wait_ge(S["sum_sb"], E + 1)
                        act.activation(sil[:, :], gu[:, 0:FF], ACT.Silu).then_inc(S["sil_sb"], 1)
                    for r in range(2):
                        if e < NE - PAIR:
                            fill_evac(gw, o, 4 + 2 * e + r, (e // PAIR + 1) % 2, 2 * (e % PAIR) + r, 3)
                        if r == 0 and e < NE:
                            act.wait_ge(S["ht_ps"], E + 1)
                            act.activation(hi_lo_h[:, :, 0, :], ps[0][:, 0:FT * CAP].rearrange("p (f c) -> p f c", f=FT),
                                           ACT.Copy).then_inc(S["hth_sb"], 1)

                with act.Fori(g, g1) as gw:
                    with act.If(gw > g):
                        hi(gw, 0, 0, 0, "gate_hi", "gate_used", 1)
                    for kp in range(4):
                        fill_evac(gw, 0, kp, 0, kp, kp)
                    for q in range(0, NE // 2, 2):
                        act.wait_ge(S["pro_ps"], gw * (NE // 2) + (q + 1))
                        act.activation(slot_tok[:, 2 * q:2 * q + 2, :], ps[1 + q % 3][:, :].rearrange("p (e t) -> p e t", e=2),
                                       ACT.Copy).then_inc(S["tok_a"], 1)
                    act.wait_ge(S["tok_v"], gw * 4 + 4)
                    for e in range(PEEL):
                        step(gw, 0, e)
                    with act.Fori(0, (NE - 2 * PEEL) // BODY) as i:
                        o = i * BODY
                        for e in range(PEEL, PEEL + BODY):
                            step(gw, o, e)
                    for e in range(NE - PEEL, NE + 1):
                        step(gw, 0, e)
                return g1

            for name, n in (("gate_hi", 1), ("down_hi", 1), ("fold_sb", 1), ("sil_sb", 1), ("hth_sb", 1), ("yhi_sb", 2),
                            ("sel_tok", 1)):
                act.nop().then_inc(S[name], E0 * n)
            xt_evac(0)
            g = 0
            for L in range(DEPTH):
                if KINDS[L] == SSD:
                    ssd(L)
                else:
                    attention(L)
                norm(2 * L)
                hi(g, 0, 0, 0, "gate_hi", "gate_used", 1)
                xt_evac(2 * L + 1)
                g = moe(L, g)
                norm(2 * L + 1)
                if L < DEPTH - 1:
                    xt_evac(2 * L + 2)

        @block.vector
        def _(dve):
            steps = [0]

            def link(ins):
                steps[0] += 1
                ins.then_inc(S["dve_step"], 1)
                dve.wait_ge(S["dve_step"], steps[0])

            dve.wait_ge(S["consts"], 7)
            dve.tensor_copy(ident_r[:, :], ident[:, :]).then_inc(S["zeroed"], 1)
            dve.memset(zero[:, :].bitcast(F32), 0.0).then_inc(S["zeroed"], 1)
            dve.wait_ge(S["par_in"], 16 * 11)
            dve.wait_ge(S["pool_step"], 1)
            for j in range(2):
                dve.tensor_copy(par_rows[0:CT_X, j, 1, :].rearrange("c (r q) -> c r q", r=2),
                                d_rows[:, j, :].unsqueeze(2).to_broadcast([CT_X, 2, DH])).then_inc(S["par_rows_d"], 1)
            for j in range(2):
                dve.wait_ge(S["par_ps"], j + 1)
                dve.tensor_copy(par[:, j, :], ps[4 + j][:, 0:176]).then_inc(S["par_sb"], 1)
            dve.wait_ge(S["a_ps"], 1)
            dve.tensor_copy(a_bc[:, :, :].rearrange("p a b -> p (a b)"), ps[6][:, 0:2 * NH]).then_inc(S["a_sb"], 1)

            def norm(n):
                if n == 0:
                    dve.wait_ge(S["x_in"], 16)
                for tt in range(TT):
                    for half in range(2):
                        c = slice(half * 512, half * 512 + 512)
                        dve.scalar_tensor_tensor(x[:, tt, c], x[:, tt, c], ALPHA, ps[4 + 2 * tt + half][:, :],
                                                 ALU.mult, ALU.add).then_inc(S["res_done"], 1)
                for tt in range(TT):
                    for half in range(2):
                        c = slice(half * 512, half * 512 + 512)
                        dve.wait_ge(S["res_done"], 4 * n + 2 * tt + half + 1)
                        ins = dve.bn_stats(st[:, tt, half, :], x[:, tt, c])
                    link(ins)
                    link(dve.bn_aggr(mv[:, tt, :], st[:, tt, :, :]))
                    dve.tensor_scalar(mv[:, tt, 1:2], mv[:, tt, 1:2], EPS, None, ALU.add).then_inc(S["ln_stats"], 1)
                dve.wait_ge(S["lngb_in"], 32 * (n + 1))
                for tt in range(TT):
                    dve.wait_ge(S["ln_sqrt"], TT * n + tt + 1)
                    dve.reciprocal(rs[:, tt:tt + 1], rs[:, tt:tt + 1]).then_inc(S["ln_rs"], 1)
                    link(dve.scalar_tensor_tensor(x[:, tt, :], x[:, tt, :], mv[:, tt, 0:1], ln_gb[:, 0, :],
                                                  ALU.subtract, ALU.mult))
                    dve.wait_ge(S["ln_rs"], TT * n + tt + 1)
                    dve.scalar_tensor_tensor(x[:, tt, :], x[:, tt, :], rs[:, tt:tt + 1], ln_gb[:, 1, :],
                                             ALU.mult, ALU.add).then_inc(S["ln_done"], 1)

            def ssd(L):
                j = occ[L]
                link(dve.memset(xbc[:, :, 0:3], 0.0))
                dve.wait_ge(S["dt_ps"], j + 1)
                pre = ps[4][:, 0:TT * NH]
                dve.tensor_scalar(dts[:, 6, :], pre, 0.0, None, ALU.max).then_inc(S["dt_abs"], 1)
                dve.wait_ge(S["dt_abs"], 2 * j + 1)
                dve.scalar_tensor_tensor(dts[:, 3, :], dts[:, 6, :], -2.0, pre, ALU.mult, ALU.add).then_inc(S["dt_abs"], 1)
                dve.wait_ge(S["dt_exp"], j + 1)
                dve.tensor_scalar(dts[:, 4, :], dts[:, 2, :], 1.0, None, ALU.add).then_inc(S["dt_u"], 1)
                dve.wait_ge(S["dt_u"], j + 1)
                link(dve.scalar_tensor_tensor(dts[:, 7, :], dts[:, 4, :], 1.0, dts[:, 2, :], ALU.subtract, ALU.subtract))
                link(dve.reciprocal(dts[:, 2, :], dts[:, 4, :]))
                link(dve.tensor_tensor(dts[:, 7, :], dts[:, 7, :], dts[:, 2, :], ALU.mult))
                link(dve.tensor_tensor(dts[:, 6, :], dts[:, 6, :], dts[:, 7, :], ALU.subtract))
                dve.wait_ge(S["dt_ln"], j + 1)
                dve.tensor_tensor(dts[:, 0, :], dts[:, 6, :], dts[:, 5, :], ALU.add).then_inc(S["dt_sb"], 1)
                dve.wait_ge(S["dt_sb"], 2 * j + 1)
                dve.scalar_tensor_tensor(dts[:, 1, :].rearrange("p (a h) -> p a h", a=TT),
                                         dts[:, 0, :].rearrange("p (a h) -> p a h", a=TT), -1.0,
                                         a_bc[:, j, :].unsqueeze(1).to_broadcast([P, TT, NH]), ALU.mult, ALU.mult)\
                    .then_inc(S["dt_sb"], 1)

                def conv(n):
                    dve.wait_ge(S["proj_free"], PROJ0[L] + n + 1)
                    if n >= 2:
                        dve.wait_ge(S["conv_done"], j * CT_BC + 2 * (n - 1))
                    t0 = 2 * order[n][1]
                    for k in range(CONV):
                        for c in range(2):
                            src = xbc[:, 2 * (n % 4) + c, k:k + T]
                            dst = cacc[:, 2 * (n % 2) + c, :]
                            w = par_cw(j, t0 + c, k)
                            if k == 0:
                                ins = dve.tensor_scalar(dst, src, w, None, ALU.mult)
                            else:
                                ins = dve.scalar_tensor_tensor(dst, src, w, dst, ALU.mult, ALU.add)
                            if k == CONV - 1 and c == 1:
                                ins.then_inc(S["conv_acc"], 1)
                            elif c == 1:
                                link(ins)
                for n in range(2):
                    conv(n)
                dve.wait_ge(S["cum_ps"], j + 1)
                dve.tensor_copy(dts[:, 7, :], ps[5][:, 0:TT * NH]).then_inc(S["cum_sb"], 1)
                dve.tensor_copy(acT[0:NH, :], ps[6][0:NH, 0:T]).then_inc(S["cum_sb"], 1)
                for n in range(2, 12):
                    conv(n)
                for g in range(NG):
                    dve.wait_ge(S["cb_ps"], NG * j + g + 1)
                    dve.tensor_tensor(cbm[:, g, 0:T], ps[4 + g][:, 0:T], triu[:, :], ALU.mult)
                    dve.tensor_tensor(cbm[:, g, T:SC], ps[4 + g][:, T:SC], triu[:, 0:P], ALU.mult).then_inc(S["cb_sb"], 1)
                dt_v = dts[:, 0, :].rearrange("p (a h) -> p a h", a=TT)
                for q in range(8):
                    tt, c4 = q % 2, q // 2
                    dve.wait_ge(S["xs_ps"], 8 * j + q + 1)
                    dve.tensor_tensor(xdt[:, tt, 512 * c4:512 * c4 + 512].rearrange("p (h c) -> p h c", c=DH),
                                      ps[4 + q % 4][:, :].rearrange("p (h c) -> p h c", c=DH),
                                      dt_v[:, tt, 8 * c4:8 * c4 + 8].unsqueeze(2).to_broadcast([P, 8, DH]), ALU.mult)\
                        .then_inc(S["xdt_sb"], 1)

                def gating(c):
                    dve.wait_ge(S["y_ps"], j * NH + 4 * (c // 2) + 4)
                    link(dve.scalar_tensor_tensor(ytmp[:, c % 2, :], cv[:, c, :], par_d(j, c),
                                                  ps[4 + (c // 2) % 4][:, (c % 2) * T:(c % 2) * T + T], ALU.mult, ALU.add))
                    dve.tensor_tensor(sz[:, c, :], ytmp[:, c % 2, :], sz[:, c, :], ALU.mult).then_inc(S["y2_sb"], 1)

                def sumsq_evac(g):
                    dve.wait_ge(S["ss_ps"], NG * j + g + 1)
                    dve.tensor_scalar(gsum[:, g, :], ps[3][:, (g % 2) * T:(g % 2) * T + T], 1.0 / (DI // NG), EPS,
                                      ALU.mult, ALU.add).then_inc(S["ss_sb"], 1)

                acs = dts[:, 7, :].rearrange("p (a h) -> p a h", a=TT)
                dve.wait_ge(S["cum_sb"], 2 * (j + 1))
                for h in range(NH):
                    dve.wait_ge(S["bc_ps"], j * NH + h + 1)
                    if h >= 2:
                        dve.wait_ge(S["dec_sb"], j * NH + h - 1)
                    dve.tensor_scalar(seg[:, h % 2, 0:T], ps[h % 3][:, 0:T], acs[:, 0, h:h + 1], 0.0,
                                      ALU.subtract, ALU.min).then_inc(S["seg_sb"], 1)
                    dve.tensor_scalar(seg[:, h % 2, T:SC], ps[h % 3][:, T:SC], acs[:, 1, h:h + 1], 0.0,
                                      ALU.subtract, ALU.min).then_inc(S["seg_sb"], 1)
                    if h % 4 == 1 and h >= 4:
                        gating(2 * (h // 4) - 2)
                        gating(2 * (h // 4) - 1)
                    if h % 8 == 7 and h >= 15:
                        sumsq_evac(h // 8 - 1)
                gating(14)
                gating(15)
                sumsq_evac(NG - 1)
                dve.wait_ge(S["ss_sqrt"], j + 1)
                link(dve.reciprocal(gsum[:, :, :], gsum[:, :, :]))
                for c in range(CT_X):
                    dve.scalar_tensor_tensor(sz[:, c, :], sz[:, c, :], par_nw(j, c), gsum[:, c // 4, :],
                                             ALU.mult, ALU.mult).then_inc(S["yn_sb"], 1)

            def attention(L):
                m = att[L]
                kind = KINDS[L]
                if kind == CA:
                    dve.wait_ge(S["rel_in"], 16)
                    dve.tensor_copy(revx[0:AH, 0:127], rel[0:AH, N_REL - 1:N_REL].to_broadcast([AH, 127]))
                    dve.tensor_copy(revx[0:AH, 127:127 + N_REL], rel[0:AH, ::-1])
                    dve.tensor_copy(revx[0:AH, 127 + N_REL:384], rel[0:AH, 0:1].to_broadcast([AH, 384 - 127 - N_REL]))\
                        .then_inc(S["rev_sb"], 1)
                for h in range(AH):
                    b = h % 2
                    dve.wait_ge(S["s_ps"], AH * m + h + 1)
                    if kind == SWA:
                        dve.wait_ge(S["bias_sb"], 4)
                        slope = 2.0 ** (-8.0 * (h + 1) / AH)
                        bsrc, mul = bias[:, 0, :], slope
                    else:
                        dve.wait_ge(S[f"bias_in{b}"], 16 * 4 * (h // 2 + 1))
                        bsrc, mul = bias[:, b, :], 1.0
                    if kind == CA and h == 0:
                        dve.wait_ge(S["bias_sb"], 8)
                    if h >= 2:
                        dve.wait_ge(S["pt_ps"], AH * m + h - 1)
                    link(dve.scalar_tensor_tensor(lg[:, b, :], bsrc, mul, ps[b][:, 0:SC], ALU.mult, ALU.add))
                    dve.tensor_reduce(hst[:, b, 6:7], lg[:, b, 0:P], AX.X, ALU.max)
                    link(dve.tensor_reduce(hst[:, b, 7:8], lg[:, b, P:SC], AX.X, ALU.max))
                    if kind == SWA:
                        dve.tensor_scalar(hst[:, b, 0:2], hst[:, b, 6:8], sinks[:, h:h + 1], -1.0, ALU.max, ALU.mult)\
                            .then_inc(S["max_sb"], 1)
                    else:
                        dve.tensor_scalar(hst[:, b, 0:2], hst[:, b, 6:8], -1.0, None, ALU.mult).then_inc(S["max_sb"], 1)
                    dve.wait_ge(S["exp_sb"], AH * m + h + 1)
                    if kind == SWA:
                        link(dve.tensor_tensor(hst[:, b, 2:4], hst[:, b, 2:4], hst[:, b, 4:6], ALU.add))
                    link(dve.reciprocal(hst[:, b, 8:10], hst[:, b, 2:4]))
                    dve.tensor_scalar(lg[:, b, 0:P], lg[:, b, 0:P], hst[:, b, 8:9], None, ALU.mult)
                    dve.tensor_scalar(lg[:, b, P:SC], lg[:, b, P:SC], hst[:, b, 9:10], None, ALU.mult)\
                        .then_inc(S["p_sb"], 1)

            def lo(gw, o, e, n, hi_name, name):
                dve.wait_ge(S[hi_name], gw * NE + o + (E0 + e + 1))
                dve.tensor_tensor(w_lo[n][:, :], ring[:, (e * UPE + n) % RING, :], w_hi[n][:, :].bitcast(F32),
                                  ALU.subtract).then_inc(S[name], 1)

            def up_high(gw, o, e):
                dve.wait_ge(loaded_moe[(e * UPE + 1) % RING], landed_moe(gw, o, e, 1))
                dve.wait_ge(S["up_used"], gw * NE + o + (E0 + e))
                dve.tensor_copy(w_hi[1][:, :], ring[:, (e * UPE + 1) % RING, :]).then_inc(S["up_hi"], 1)

            def moe(L, g):
                R = lambda n: rt[:, n, :, :]
                small = lambda n, w: rt[:, n, :, :].rearrange("p a e -> p (a e)")[:, 0:TT * w].rearrange("p (a e) -> p a e", e=w)
                lo(g, 0, 0, 0, "gate_hi", "gate_lo")
                up_high(g, 0, 0)
                lo(g, 0, 0, 1, "up_hi", "up_lo")
                dve.wait_ge(S["xhi_sb"], L + 1)
                dve.tensor_tensor(x_lo[:, :, :], x[:, :, :], x_hi[:, :, :].bitcast(F32), ALU.subtract).then_inc(S["xlo_sb"], 1)
                dve.wait_ge(S["rt_exp"], L + 1)
                link(dve.tensor_scalar(R(1), R(1), 1.0, None, ALU.add))
                link(dve.reciprocal(R(2), R(1)))
                link(dve.tensor_tensor(R(3), R(2), rt_bias[:, :].unsqueeze(1).to_broadcast([P, TT, NE]), ALU.add))
                g4 = rt[:, 3, :, :].rearrange("p a (g e) -> p (a g) e", e=4)
                pairs = rt[:, 4:7, :, :].rearrange("p n a e -> p (n a e)")[:, 0:48].rearrange("p (g e) -> p g e", e=6)
                dve.tensor_tensor(pairs[:, :, 0:2], g4[:, :, 0:2], g4[:, :, 2:4], ALU.add)
                dve.tensor_tensor(pairs[:, :, 2:4], g4[:, :, 0:2], g4[:, :, 3:1:-1], ALU.add)
                link(dve.tensor_tensor(pairs[:, :, 4:6], g4[:, :, 0:4:2], g4[:, :, 1:4:2], ALU.add))
                gs = small(7, 4)
                link(dve.tensor_reduce(gs.rearrange("p a g -> p (a g)"), pairs, AX.X, ALU.max))
                m1 = rt[:, 8, 0, :]

                def one_hot(dst, src, w, tmp, c):
                    rk = rank[:, NE - w:NE].unsqueeze(1).to_broadcast([P, TT, w])
                    link(dve.tensor_reduce(m1[:, c:c + TT], src, AX.X, ALU.max))
                    link(dve.tensor_tensor(dst, src, m1[:, c:c + TT].unsqueeze(2).to_broadcast([P, TT, w]), ALU.is_equal))
                    link(dve.tensor_tensor(tmp, dst, rk, ALU.mult))
                    link(dve.tensor_reduce(m1[:, c + TT:c + 2 * TT], tmp, AX.X, ALU.max))
                    link(dve.tensor_tensor(dst, tmp, m1[:, c + TT:c + 2 * TT].unsqueeze(2).to_broadcast([P, TT, w]), ALU.is_equal))

                best = small(9, 4)
                one_hot(best, gs, 4, small(10, 4), 0)
                link(dve.tensor_scalar(small(11, 4), best, 1.0, -NEG, ALU.subtract, ALU.mult))
                selm = R(12)
                link(dve.tensor_tensor(selm.rearrange("p a (g e) -> p (a g) e", e=4), g4,
                                       small(11, 4).rearrange("p a g -> p (a g)").unsqueeze(2).to_broadcast([P, TT * 4, 4]), ALU.add))
                one_hot(R(13), selm, NE, R(14), 4)
                link(dve.scalar_tensor_tensor(R(15), R(13), 4.0 * NEG, selm, ALU.mult, ALU.add))
                one_hot(R(16), R(15), NE, R(14), 8)
                dve.tensor_tensor(R(13), R(13), R(16), ALU.add).then_inc(S["sel_sb"], 1)
                dve.wait_ge(S["sel_sb"], L + 1)
                dve.wait_ge(S["pos_ps"], L + 1)
                link(dve.tensor_tensor(posm[:, :, :], ps[5][:, 0:TT * NE].rearrange("p (a e) -> p a e", a=TT), R(13), ALU.mult))
                link(dve.tensor_reduce(m1[0:1, 12:13], ps[5][0:1, 2 * NE:3 * NE], AX.X, ALU.max))
                dve.tensor_scalar(posm[:, :, :], posm[:, :, :], -1.0, None, ALU.add).then_inc(S["posm_sb"], 1)
                link(dve.tensor_scalar(m1[0:1, 13:14], m1[0:1, 12:13], CAP + 0.5, 1.0, ALU.is_gt, ALU.add))
                for n in range(2, T // CAP):
                    link(dve.scalar_tensor_tensor(m1[0:1, 13:14], m1[0:1, 12:13], n * CAP + 0.5, m1[0:1, 13:14],
                                                  ALU.is_gt, ALU.add))
                dve.tensor_copy(nwin[0:1, 0:1], m1[0:1, 13:14]).then_inc(S["nwin_sb"], 1)
                dve.wait_ge(S["nwin_sb"], L + 1)
                dve.wait_ge(S["posm_sb"], L + 1)
                g1 = dve.snap(g + dve.value_load(nwin[0:1, 0:1], min_val=1, max_val=T // CAP))

                link(dve.tensor_tensor(R(17), R(13), R(2), ALU.mult))
                link(dve.tensor_reduce(m1[:, 12:12 + TT], R(17), AX.X, ALU.add))
                link(dve.reciprocal(m1[:, 14:14 + TT], m1[:, 12:12 + TT]))
                link(dve.tensor_tensor(R(0), R(17), m1[:, 14:14 + TT].unsqueeze(2).to_broadcast([P, TT, NE]), ALU.mult))
                link(dve.tensor_copy(gates[:, :, :, 0], R(0)))
                dve.tensor_tensor(gates[:, :, :, 1], R(0), gates[:, :, :, 0].bitcast(F32), ALU.subtract).then_inc(S["gates_hl"], 1)

                def y_low(gw, o, e, half):
                    E = gw * NE + o + (E0 + e)
                    c = slice(half * 512, half * 512 + 512)
                    dve.wait_ge(S["yhi_sb"], 2 * E + half + 1)
                    dve.tensor_tensor(y_lo[:, e % 2, c], ps[1 + half][:, :], y_hi[:, e % 2, c].bitcast(F32), ALU.subtract)\
                        .then_inc(S["ylo_sb"], 1)

                def step(gw, o, e):
                    E = gw * NE + o + (E0 + e)
                    if e + 1 < NE:
                        lo(gw, o, e + 1, 0, "gate_hi", "gate_lo")
                    if e < NE:
                        dve.wait_ge(S["fold_sb"], E + 1)
                        dve.tensor_tensor(gu[:, :], ps[0][0:CAP, :], fold[:, :], ALU.add).then_inc(S["sum_sb"], 1)
                    if e + 1 < NE:
                        up_high(gw, o, e + 1)
                    if e < NE:
                        dve.wait_ge(S["sil_sb"], E + 1)
                        dve.scalar_tensor_tensor(hbuf[:, :], sil[:, :], gate_slot[0:CAP, bass.ds(o + e, 1)],
                                                 gu[:, FF:2 * FF], ALU.mult, ALU.mult).then_inc(S["h_sb"], 1)
                    if e >= 1:
                        y_low(gw, o, e - 1, 0)
                    if e < NE:
                        dve.wait_ge(S["hth_sb"], E + 1)
                        dve.tensor_tensor(hi_lo_h[:, :, 1, :], ps[0][:, 0:FT * CAP].rearrange("p (f c) -> p f c", f=FT),
                                          hi_lo_h[:, :, 0, :].bitcast(F32), ALU.subtract).then_inc(S["htl_sb"], 1)
                    if e + 1 < NE:
                        lo(gw, o, e + 1, 1, "up_hi", "up_lo")
                    if e >= 1:
                        y_low(gw, o, e - 1, 1)

                def one_hot_slots(experts):
                    n = experts.stop - experts.start
                    dve.tensor_tensor(disp[:, :, experts, :],
                                      posm[:, :, experts].unsqueeze(3).to_broadcast([P, TT, n, 2 * CAP]),
                                      iota_c[:, :].unsqueeze(1).unsqueeze(1).to_broadcast([P, TT, n, 2 * CAP]), ALU.is_equal)\
                        .then_inc(S["disp_sb"], 1)

                with dve.Fori(g, g1) as gw:
                    dve.wait_ge(S["comb_ps"], gw * NE + E0)
                    one_hot_slots(slice(0, PAIR))
                    one_hot_slots(slice(PAIR, NE))
                    with dve.If(gw > g):
                        lo(gw, 0, 0, 0, "gate_hi", "gate_lo")
                        up_high(gw, 0, 0)
                        lo(gw, 0, 0, 1, "up_hi", "up_lo")
                    dve.wait_ge(S["disp_sb"], gw * 2 + 2)
                    dve.tensor_scalar(posm[:, :, :], posm[:, :, :], -float(CAP), None, ALU.add).then_inc(S["win_done"], 1)
                    dve.wait_ge(S["win_done"], gw + 1)
                    dve.wait_ge(S["gates_ps"], gw + 1)
                    dve.tensor_reduce(gate_slot[:, :], ps[0][:, 0:2 * NE].rearrange("p (e m) -> p e m", m=2), AX.X, ALU.add)\
                        .then_inc(S["gs_sb"], 1)
                    for q in range(1, NE // 2, 2):
                        dve.wait_ge(S["pro_ps"], gw * (NE // 2) + (q + 1))
                        dve.tensor_copy(slot_tok[:, 2 * q:2 * q + 2, :], ps[1 + q % 3][:, :].rearrange("p (e t) -> p e t", e=2))\
                            .then_inc(S["tok_v"], 1)
                    dve.wait_ge(S["gs_sb"], gw + 1)
                    for e in range(PEEL):
                        step(gw, 0, e)
                    with dve.Fori(0, (NE - 2 * PEEL) // BODY) as i:
                        o = i * BODY
                        for e in range(PEEL, PEEL + BODY):
                            step(gw, o, e)
                    for e in range(NE - PEEL, NE + 1):
                        step(gw, 0, e)
                return g1

            for name, n in (("up_hi", 1), ("gate_lo", 1), ("up_lo", 1), ("sum_sb", 1), ("h_sb", 1), ("htl_sb", 1), ("ylo_sb", 2)):
                dve.nop().then_inc(S[name], E0 * n)
            g = 0
            for L in range(DEPTH):
                if KINDS[L] == SSD:
                    ssd(L)
                else:
                    attention(L)
                dve.wait_ge(S["out_used"], sum(N_OUT[k] for k in KINDS[:L + 1]))
                norm(2 * L)
                g = moe(L, g)
                dve.wait_ge(S["comb_ps"], g * NE + E0)
                norm(2 * L + 1)

        @block.gpsimd
        def _(pool):
            pool.dma_start(x[:], a["x"][0].rearrange("(t p) d -> p t d", p=P)).then_inc(S["x_in"], 16)
            pool.dma_start(w_rt[:, :, :], a["router_w"].rearrange("(p k) e -> p k e", k=KT)).then_inc(S["rt_in"], 16)
            pool.dma_start(rt_bias[:, :], a["router_bias"].rearrange("(o e) -> o e", o=1).to_broadcast([P, NE])).then_inc(S["rt_in"], 16)
            pool.dma_start(sinks[:, :], a["swa_sinks"].to_broadcast([P, AH])).then_inc(S["rt_in"], 16)
            pool.memset(par_rows[:, :, 1, :], 0.0).then_inc(S["pool_step"], 1)
            pool.memset(ident[:, :], 0.0).then_inc(S["consts"], 1)
            pool.memset(ones[:, :], 1.0).then_inc(S["consts"], 1)
            pool.memset(triu[:, :], 1.0).then_inc(S["consts"], 1)
            pool.wait_ge(S["consts"], 3)
            pool.affine_select(out=ident[:, :], in_=ident[:, :], compare_op=ALU.not_equal, fill=1.0, base=0,
                               pattern=[[-1, P]], channel_multiplier=1).then_inc(S["consts"], 1)
            pool.affine_select(out=triu[:, :], in_=triu[:, :], compare_op=ALU.is_ge, fill=0.0, base=0,
                               pattern=[[1, T]], channel_multiplier=-1).then_inc(S["consts"], 1)
            pool.iota(iota_c[:, :], pattern=[[0, 2], [1, CAP]], base=0, channel_multiplier=0, allow_small_or_imprecise_dtypes=True).then_inc(S["consts"], 1)
            pool.iota(rank[:, :], pattern=[[-1, NE]], base=NE, channel_multiplier=0, allow_small_or_imprecise_dtypes=True).then_inc(S["consts"], 1)

            def gains(n):
                if n > 0:
                    pool.wait_ge(S["ln_done"], TT * n)
                g, b = ("ln_mix_g", "ln_mix_b") if n % 2 == 0 else ("ln_ffn_g", "ln_ffn_b")
                for i, w in enumerate((g, b)):
                    pool.dma_start(ln_gb[:, i, :], a[w][n // 2:n // 2 + 1, :].to_broadcast([P, D])).then_inc(S["lngb_in"], 16)

            def ssd(L):
                j = occ[L]
                for h in range(NH):
                    pool.wait_ge(S["dec_sb"], j * NH + h + 1)
                    pool.wait_ge(S["cb_sb"], NG * (j + 1))
                    if h >= 2:
                        pool.wait_ge(S["y_ps"], j * NH + h - 1)
                    pool.tensor_tensor(mm_[:, h % 2, :], dec[:, h % 2, :], cbm[:, h // HPG, :], ALU.mult)\
                        .then_inc(S["m_sb"], 1)

            def mask(rows, b, cols, at):
                pool.memset(bias[rows, b, cols], NEG).then_inc(S["bias_sb"], 1)
                pool.wait_ge(S["bias_sb"], at)

            def swa():
                pool.wait_ge(S["ln_done"], TT * 2)
                pool.iota(lg[:, 0, 0:P], pattern=[[-1, P]], base=0, channel_multiplier=1, allow_small_or_imprecise_dtypes=True)
                pool.iota(lg[:, 0, P:SC], pattern=[[-1, T]], base=P, channel_multiplier=1, allow_small_or_imprecise_dtypes=True).then_inc(S["pool_step"], 1)
                pool.wait_ge(S["pool_step"], 2)
                pool.tensor_scalar(lg[:, 1, :], lg[:, 0, :], 0.0, -2.0, ALU.max, ALU.mult).then_inc(S["pool_step"], 1)
                pool.wait_ge(S["pool_step"], 3)
                pool.tensor_tensor(bias[:, 0, :], lg[:, 0, :], lg[:, 1, :], ALU.add).then_inc(S["pool_step"], 1)
                pool.wait_ge(S["pool_step"], 4)
                mask(slice(0, CH), 0, slice(CH, P), 1)
                mask(slice(0, CH), 0, slice(P + 3 * CH, SC), 2)
                mask(slice(0, P), 0, slice(P, P + CH), 3)
                mask(slice(CH, P), 0, slice(P + CH, P + 2 * CH), 4)

            def ca():
                pool.wait_ge(S["ln_done"], TT * 4)
                pool.dma_start(rel[0:AH, :], a["ca_rel_bias"][0]).then_inc(S["rel_in"], 16)
                for b in range(2):
                    mask(slice(0, CH), b, slice(CH, P), 5 + 2 * b)
                    mask(slice(0, CH), b, slice(P + 3 * CH, SC), 6 + 2 * b)
                pool.wait_ge(S["rev_sb"], 1)
                pool.dma_start(rev_dram, revx[0:AH, :].unsqueeze(1).to_broadcast([AH, CH, 384])).then_inc(S["rev_out"], 16)
                pool.wait_ge(S["rev_out"], 16)
                for h in range(AH):
                    if h >= 2:
                        pool.wait_ge(S["max_sb"], AH + h - 1)
                    b = h % 2

                    def toeplitz(q0, width, col):
                        src = bass.AP(rev_dram.tensor, h * CH * 384 + 255 - q0, [[383, CH], [1, width]])
                        pool.dma_start(bias[q0 % P:q0 % P + CH, b, col:col + width], src)\
                            .then_inc(S[f"bias_in{b}"], 16)

                    toeplitz(0, CH, 0)
                    toeplitz(CH, P, 0)
                    toeplitz(P, 3 * CH, P)
                    toeplitz(3 * CH, T, P)

            def moe(L, g):
                pool.wait_ge(S["nwin_sb"], L + 1)
                g1 = pool.snap(g + pool.value_load(nwin[0:1, 0:1], min_val=1, max_val=T // CAP))
                with pool.Fori(g, g1) as gw:
                    with pool.Fori(0, NE // BODY) as i:
                        for b in range(BODY):
                            pool.wait_ge(S["down_hi"], gw * NE + i * BODY + (E0 + b + 1))
                            pool.tensor_tensor(w_lo[2][:, :], ring[:, (b * UPE + 2) % RING, :], w_hi[2][:, :].bitcast(F32),
                                               ALU.subtract).then_inc(S["down_lo"], 1)
                return g1

            pool.nop().then_inc(S["down_lo"], E0)
            g = 0
            gains(0)
            for L in range(DEPTH):
                if KINDS[L] == SSD:
                    ssd(L)
                elif KINDS[L] == SWA:
                    swa()
                else:
                    ca()
                gains(2 * L + 1)
                g = moe(L, g)
                if L < DEPTH - 1:
                    gains(2 * L + 2)


_INS = ["x", "ssd_w_in", "ssd_conv_w", "ssd_conv_b", "ssd_dt_bias", "ssd_a_log", "ssd_d_skip", "ssd_norm_w", "ssd_w_out",
        "swa_w_in", "swa_sinks", "swa_w_out", "ca_w_in", "ca_rel_bias", "ca_w_out", "router_w", "router_bias",
        "moe_w_gate", "moe_w_up", "moe_w_down", "ln_mix_g", "ln_mix_b", "ln_ffn_g", "ln_ffn_b"]


def kernel(**inputs):
    import numpy as _np
    import concourse.bacc as _bacc
    from concourse import mybir as _mybir
    from concourse.bass_utils import run_bass_kernel_spmd as _run

    nc = _bacc.Bacc("TRN2", target_bir_lowering=False, num_devices=1)
    arrays, aps = {}, {}
    for name in _INS:
        arr = _np.ascontiguousarray(inputs[name])
        arrays[f"in_{name}"] = arr
        aps[name] = nc.dram_tensor(f"in_{name}", arr.shape, _mybir.dt.from_np(arr.dtype), kind="ExternalInput").ap()
    out = nc.dram_tensor("out", (T, D), _mybir.dt.float32, kind="ExternalOutput").ap()
    trunk(nc, aps, out)
    r = _run(nc, [arrays], core_ids=[0])
    return r.results[0]["out"].reshape(1, T, D)
```

```python
from contextlib import ExitStack

import concourse.bass as bass
from concourse import mybir

F32 = mybir.dt.float32
BF16 = mybir.dt.bfloat16
F32R = mybir.dt.float32r
I32 = mybir.dt.int32
ALU = mybir.AluOpType
ACT = mybir.ActivationFunctionType
AX = mybir.AxisListType

P = 128
D = 1024
T = 256
TT = T // P
KT = D // P
DEPTH = 4
CH = 64
ALPHA = (2.0 * DEPTH) ** 0.25
EPS = 1e-5
DI = 2 * D
NH = 32
HB = 3
NG = 4
HPG = NH // NG
XBC = DI + 2 * NG * 128
CT_X = DI // P
CT_BC = XBC // P
CONV = 4
AH = 16
DH = 64
KVH = 4
REL_CLIP = 128
N_REL = CH - 1 + REL_CLIP + 1
NEG = -1.0e30
NE = 16
FF = D // 4
FT = FF // P
UW = 2048
RING = 6
LB = 4
UPE = 3
BODY = 4
SLOT_BANKS = (2, 3, 1)
PEEL = 2
CAP = CH
PAIR = 2
E0 = 2
FILLS = 4 * NE // PAIR
XDT_AT = 8 * 259 + 4 * T + (CT_BC + CT_X) * T
ARENA = 24900
SC = P + T

SSD, SWA, CA = 0, 1, 2
KINDS = [i % 3 for i in range(DEPTH)]
N_IN = {SSD: (DI + XBC) // 256, SWA: 6, CA: 12}
N_SPLIT = {SSD: N_IN[SSD], SWA: 5, CA: 8}
N_OUT = {SSD: 8, SWA: 4, CA: 4}
UNIT0 = []
PROJ0 = []
_u = _p = 0
for _k in KINDS:
    UNIT0.append(_u)
    PROJ0.append(_p)
    _u += N_IN[_k] + N_OUT[_k]
    _p += N_IN[_k]


def trunk(nc, a, out):
    ctx = ExitStack()
    with ctx:
        def sb(name, shape, dt=F32):
            return ctx.enter_context(nc.sbuf_tensor(name, shape, dt))

        def sem(name):
            return ctx.enter_context(nc.semaphore(name))

        ring = sb("ring", [P, RING, UW])
        x = sb("x", [P, TT, D])
        ln_gb = sb("ln_gb", [P, 2, D])
        ident = sb("ident", [P, P])
        ones = sb("ones", [P, P])
        triu = sb("triu", [P, T])
        rank = sb("rank", [P, NE])
        par = sb("par", [P, 2, 176])
        d_rows = sb("d_rows", [CT_X, 2, 2])
        w_dt = sb("w_dt", [P, 2, KT, NH])
        dtb = sb("dtb", [1, 2, NH])
        a_row = sb("a_row", [1, 2, NH])
        a_bc = sb("a_bc", [P, 2, NH])
        w_rt = sb("w_rt", [P, KT, NE])
        rt_bias = sb("rt_bias", [P, NE])
        sinks = sb("sinks", [P, AH])
        st = sb("st", [P, TT, 2, 6])
        mv = sb("mv", [P, TT, 2])
        rs = sb("rs", [P, TT])
        iota_c = sb("iota_c", [P, 2 * CAP])
        ident_r = sb("ident_r", [P, P], F32R)
        pick = sb("pick", [2 * NH, NH], F32R)
        ones_r = sb("ones_r", [P, P], F32R)
        triu_r = sb("triu_r", [P, P], F32R)
        zero = sb("zero", [1, 512], F32R)
        nwin = sb("nwin", [1, 1], I32)

        mix_ctx = ExitStack()
        with nc.sbuf_tensor("lhs_parts", [P, LB, 2, T], F32R) as lhs_parts:
            pass
        xT = mix_ctx.enter_context(nc.sbuf_tensor("xT", [P, KT, T], F32))
        with nc.sbuf_tensor("below_parts", [P, XDT_AT], F32), nc.sbuf_tensor("xt_parts", [P, 2, KT, T], F32R) as xt_parts:
            pass
        arena = mix_ctx.enter_context(nc.sbuf_tensor("arena", [P, ARENA], F32))
        acT = mix_ctx.enter_context(nc.sbuf_tensor("acT", [2 * NH, SC], F32R))
        tile_hi = mix_ctx.enter_context(nc.sbuf_tensor("tile_hi", [P, 2, D], F32R))
        tile_lo = mix_ctx.enter_context(nc.sbuf_tensor("tile_lo", [P, 2, D], F32R))
        mix_ctx.close()
        moe_ctx = ExitStack()

        def mb(name, shape, dt=F32):
            return moe_ctx.enter_context(nc.sbuf_tensor(name, shape, dt))

        slot_tok = mb("slot_tok", [P, NE, T], BF16)
        x_hi = mb("x_hi", [P, TT, D], F32R)
        x_lo = mb("x_lo", [P, TT, D], F32R)
        w_hi = [mb(f"{n}_hi", [P, UW], F32R) for n in ("gate", "up")]
        w_lo = [mb(f"{n}_lo", [P, UW], F32R) for n in ("gate", "up")]
        w_hi.append(mb("down_hi", [P, UW], F32R))
        w_lo.append(mb("down_lo", [P, UW], F32R))
        xg = mb("xg", [P, 2, KT, PAIR, 2 * CAP], F32R)
        disp = mb("disp", [P, TT, NE, 2 * CAP], F32R)
        gates = mb("gates", [P, TT, NE, 2], F32R)
        hi_lo_h = mb("hi_lo_h", [P, FT, 2, CAP], F32R)
        sel = mb("sel", [P, 2, T], F32R)
        fold = mb("fold", [CAP, 512])
        gu = mb("gu", [CAP, 512])
        sil = mb("sil", [CAP, FF])
        hbuf = mb("hbuf", [CAP, FF])
        gate_slot = mb("gate_slot", [P, NE])
        posm = mb("posm", [P, TT, NE])
        chosen = mb("chosen", [P, TT, NE], F32R)
        rt = mb("rt", [P, 20, TT, NE])
        y_hi = mb("y_hi", [P, 2, D], F32R)
        y_lo = mb("y_lo", [P, 2, D], F32R)
        moe_ctx.close()
        top = [0]

        def take(n, reset=None):
            if reset is not None:
                top[0] = reset
            top[0] += n
            assert top[0] <= ARENA
            return arena[:, top[0] - n:top[0]]

        xbc = take(8 * 259, 0).rearrange("p (c t) -> p c t", t=259)
        cacc = take(4 * T).rearrange("p (c t) -> p c t", t=T)
        cv = take(CT_BC * T).rearrange("p (c t) -> p c t", t=T)
        sz = take(CT_X * T).rearrange("p (c t) -> p c t", t=T)
        xdt = take(TT * DI)
        assert top[0] == XDT_AT + TT * DI
        xdt = xdt.rearrange("p (a c) -> p a c", a=TT)
        cbm = take(NG * SC)
        par_rows = cbm[:, 0:4 * P].rearrange("p (j n c) -> p j n c", j=2, n=2)
        cbm = cbm.rearrange("p (g c) -> p g c", g=NG)
        seg = take(HB * SC).rearrange("p (g c) -> p g c", g=HB)
        dec = take(HB * SC).rearrange("p (g c) -> p g c", g=HB)
        mm_ = take(HB * SC).rearrange("p (g c) -> p g c", g=HB)
        dts = take(8 * TT * NH).rearrange("p (n c) -> p n c", n=8)
        gsum = take(NG * T, 0).rearrange("p (g t) -> p g t", g=NG)
        ytmp = take(2 * T).rearrange("p (g t) -> p g t", g=2)
        sq = take(4 * T).rearrange("p (g t) -> p g t", g=4)
        assert top[0] <= 8 * 259 + 4 * T
        qT = take(8 * T, 0).rearrange("p (c t) -> p c t", t=T)
        kT = take(8 * T).rearrange("p (c t) -> p c t", t=T)
        v = take(TT * D).rearrange("p (a c) -> p a c", a=TT)
        oT = take(8 * T).rearrange("p (c t) -> p c t", t=T)
        bias = take(2 * SC).rearrange("p (g c) -> p g c", g=2)
        lg = take(2 * SC).rearrange("p (g c) -> p g c", g=2)
        pT = take(2 * SC).rearrange("p (g c) -> p g c", g=2)
        hst = take(2 * 16).rearrange("p (g c) -> p g c", g=2)
        revx = take(384)
        rel = take(N_REL)
        assert top[0] <= XDT_AT
        ps = [ctx.enter_context(nc.psum_tensor(f"ps{i}", [P, 512], F32)) for i in range(8)]
        rev_dram = nc.dram_tensor("rev_dram", (AH, CH, 384), F32, kind="Internal").ap()

        loaded = [sem(f"loaded{s}") for s in range(RING)]
        loaded_moe = [sem(f"loaded_moe{s}") for s in range(RING)]
        S = {n: sem(n) for n in (
            "consts", "par_in", "w_dt_in", "par_rows_d", "par_ps", "par_sb", "a_exp", "a_ps", "a_sb", "rt_in", "x_in",
            "xt_ps", "xt_sb", "v_ready", "xt_hi", "xt_lo", "proj_free", "lngb_in", "tile_used", "tile_hi", "tile_lo", "lhs_hi", "lhs_lo", "pos_ps", "nwin_sb", "disp_sb", "xhi_sb", "xlo_sb", "pro_ps", "fill_ps", "fill_sb", "tok_a", "tok_v", "gates_ps", "gates_hl", "gs_sb", "win_done", "posm_sb", "zeroed",
            "gate_used", "up_used", "ht_ps", "yp_ps", "comb_ps", "gate_hi", "down_hi", "fold_sb", "sil_sb", "hth_sb", "yhi_sb", "sel_sb", "sel_tok",
            "up_hi", "gate_lo", "up_lo", "sum_sb", "h_sb", "htl_sb", "ylo_sb", "down_lo", "res_done", 
            "ln_stats", "ln_root", "ln_rs", "ln_done", "dve_step",
            "dt_ps", "dt_abs", "dt_exp", "dt_u", "dt_ln", "dt_sb", "cum_ps", "cum_sb", "conv_acc", "conv_done",
            "cb_ps", "cb_sb", "xs_ps", "xdt_sb", "bc_ps", "seg_sb", "dec_sb", "m_sb", "y_ps", "y2_sb", "sq_sb",
            "ss_ps", "ss_sb", "ss_root", "yn_sb",
            "bias_sb", "rel_in", "rev_sb", "rev_out", "bias_in0", "bias_in1", "s_ps", "max_sb", "exp_sb", "p_sb", "pt_ps", "pt_sb", "o_ps", "o_sb",
            "rt_ps", "rt_exp", "store", "pool_step")}

        def par_cw(j, tile, k):
            return par[:, j, k * CT_BC + tile:k * CT_BC + tile + 1]

        def par_d(j, t):
            return par[:, j, 96 + t:97 + t]

        def par_cb(j, tile):
            return par[:, j, 96 + 32 + tile:97 + 32 + tile]

        def par_nw(j, t):
            return par[:, j, 96 + 64 + t:97 + 64 + t]

        occ = {0: 0, 3: 1}
        att = {1: 0, 2: 1}
        order = [("xbc", n) for n in (8, 9, 10, 11, 0, 1, 2, 3, 4, 5, 6, 7)] + [("z", n) for n in range(8)]

        def tile0(L):
            return 2 * sum(N_SPLIT[k] + N_OUT[k] for k in KINDS[:L])

        def out0(L):
            return tile0(L) + 2 * N_SPLIT[KINDS[L]]

        def lhs0(L):
            return 2 * sum(N_OUT[k] for k in KINDS[:L])

        def projected(L, n):
            if n < N_SPLIT[KINDS[L]]:
                return S["tile_used"], tile0(L) + 2 * n + 2
            return S["v_ready"], sum(N_IN[k] - N_SPLIT[k] for k in KINDS[:L]) + n - N_SPLIT[KINDS[L]] + 1

        def used(u):
            L = max(n for n in range(DEPTH) if UNIT0[n] <= u)
            n = u - UNIT0[L]
            if n < N_IN[KINDS[L]]:
                return (S["tile_lo"], tile0(L) + 2 * n + 2) if n < N_SPLIT[KINDS[L]] else projected(L, n)
            return S["tile_lo"], out0(L) + 2 * (n - N_IN[KINDS[L]]) + 2

        def slot(u):
            L = max(n for n in range(DEPTH) if UNIT0[n] <= u)
            return (u - UNIT0[L]) % RING

        def landed(u):
            return sum(slot(n) == slot(u) for n in range(u + 1))

        def landed_moe(gw, o, e, n):
            return (gw * NE + o) * (16 * UPE // RING) + 16 * ((e * UPE + n) // RING + 1)

        def tile_of(L, i):
            kind = KINDS[L]
            n_in = 2 * N_SPLIT[kind]
            u = UNIT0[L] + (i // 2 if i < n_in else N_IN[kind] + (i - n_in) // 2)
            w = ring[:, slot(u), :]
            if i < n_in:
                w = w.rearrange("p (k n) -> p k n", k=KT)[:, :, (i % 2) * P:(i % 2) * P + P]
                hi, lo = (t[:, i % 2, :].rearrange("p (k n) -> p k n", k=KT) for t in (tile_hi, tile_lo))
            else:
                w = w[:, (i % 2) * D:(i % 2) * D + D]
                hi, lo = (t[:, i % 2, :] for t in (tile_hi, tile_lo))
            return u, w, hi, lo

        def down_half(t, half):
            return t.rearrange("p (f n) -> p f n", f=FT)[:, :, half * 512:half * 512 + 512]

        lo_sems = (("gate_lo", 2), ("up_lo", 2), ("down_lo", 2))

        block = ctx.enter_context(nc.Block())

        @block.sync
        def _(sp):
            def put(u, src, g):
                L = max(n for n in range(DEPTH) if UNIT0[n] <= u)
                n = u - UNIT0[L]
                if n >= RING:
                    sp.wait_ge(*used(u - RING))
                elif L > 0:
                    name, per = lo_sems[n % UPE]
                    sp.wait_ge(S[name], (g * NE + (E0 - 1 + n // UPE)) * per)
                dst = ring[:, slot(u), :].rearrange("p (a b) -> p a b", a=src.shape[1])
                if u == 1:
                    sp.wait_ge(S["x_in"], 16)
                sp.dma_start(dst, src).then_inc(loaded[slot(u)], 16)

            def relative_bias():
                sp.wait_ge(S["rev_out"], 16)
                sp.wait_ge(S["bias_sb"], 8)
                for h in range(AH):
                    if h >= 2:
                        sp.wait_ge(S["max_sb"], AH + h - 1)
                    b = h % 2
                    for q0, width, col in ((0, CH, 0), (CH, P, 0), (P, 3 * CH, P), (3 * CH, T, P)):
                        src = bass.AP(rev_dram.tensor, h * CH * 384 + 255 - q0, [[383, CH], [1, width]])
                        sp.dma_start(bias[q0 % P:q0 % P + CH, b, col:col + width], src).then_inc(S[f"bias_in{b}"], 16)

            def w_in_unit(w, c):
                return w.rearrange("(p k) n -> p k n", k=KT)[:, :, c:c + 256]

            def w_out_unit(w, n):
                return w[256 * n:256 * n + 256, :].rearrange("(r p) n -> p r n", r=2)

            g = 0
            for L in range(DEPTH):
                kind = KINDS[L]
                u = UNIT0[L]
                if kind == SSD:
                    j = occ[L]
                    for n, (what, i) in enumerate(order):
                        c = 256 * i + (DI if what == "xbc" else 0)
                        put(u + n, w_in_unit(a["ssd_w_in"][j], c), g)
                    wo = a["ssd_w_out"][j]
                elif kind == SWA:
                    for n in range(N_IN[SWA]):
                        put(u + n, w_in_unit(a["swa_w_in"][0], 256 * n), g)
                    wo = a["swa_w_out"][0]
                else:
                    for n in range(N_IN[CA]):
                        put(u + n, w_in_unit(a["ca_w_in"][0], 256 * n), g)
                    wo = a["ca_w_out"][0]
                u += N_IN[kind]
                for n in range(N_OUT[kind]):
                    put(u + n, w_out_unit(wo, n), g)
                if kind == CA:
                    relative_bias()
                gate_v = a["moe_w_gate"][L].rearrange("e (p k) f -> e p (k f)", k=KT)
                up_v = a["moe_w_up"][L].rearrange("e (p k) f -> e p (k f)", k=KT)
                down_v = a["moe_w_down"][L].rearrange("e (r p) n -> e p r n", r=FT)
                last = UNIT0[L] + N_IN[kind] + N_OUT[kind]

                views = (gate_v, up_v, down_v)

                def expert(gw, o, e, n):
                    k = e * UPE + n
                    if k < RING:
                        sp.wait_ge(*used(max(u for u in range(last - RING, last) if slot(u) == k)))
                    name, per = lo_sems[n]
                    sp.wait_ge(S[name], (gw * NE + o + (E0 + e - RING // UPE + 1)) * per)
                    dst = ring[:, k % RING, :]
                    if n == 2:
                        dst = dst.rearrange("p (r n) -> p r n", r=FT)
                    sp.dma_start(dst, views[n][o + e]).then_inc(loaded_moe[k % RING], 16)

                def step(gw, o, e):
                    if e < NE:
                        expert(gw, o, e, 0)
                    if e >= 1:
                        expert(gw, o, e - 1, 2)
                    if e < NE:
                        expert(gw, o, e, 1)

                def experts(gw):
                    for e in range(PEEL):
                        step(gw, 0, e)
                    with sp.Fori(0, (NE - 2 * PEEL) // BODY) as i:
                        o = i * BODY
                        for e in range(PEEL, PEEL + BODY):
                            step(gw, o, e)
                    for e in range(NE - PEEL, NE + 1):
                        step(gw, 0, e)

                experts(g)
                sp.wait_ge(S["nwin_sb"], L + 1)
                g1 = sp.snap(g + sp.value_load(nwin[0:1, 0:1], min_val=1, max_val=T // CAP))
                with sp.If(g1 > g + 1):
                    with sp.Fori(g + 1, g1) as gw:
                        experts(gw)
                g = g1
            sp.wait_ge(S["ln_done"], 2 * DEPTH * TT)
            sp.dma_start(out.rearrange("(a p) d -> p a d", p=P), x[:]).then_inc(S["store"], 16)
            sp.wait_ge(S["store"], 16)

        @block.tensor
        def _(pe):
            def unit_wait(u):
                pe.wait_ge(loaded[slot(u)], 16 * landed(u))

            def unit(u, r):
                return ring[:, slot(u), :].rearrange("p (a b) -> p a b", a=r)

            def turn_x(n):
                for tt in range(TT):
                    if n == 0:
                        pe.wait_ge(S["x_in"], 16)
                        pe.wait_ge(S["consts"], 7)
                    else:
                        pe.wait_ge(S["ln_done"], TT * (n - 1) + tt + 1)
                    for k in range(KT):
                        c = (k % 2) * T + tt * P
                        t = pe.transpose(ps[k // 2][:, c:c + P], x[:, tt, k:D:KT], ident[:])
                        if tt == TT - 1 and k % 2 == 1:
                            t.then_inc(S["xt_ps"], 1)

            def project_in(L, n):
                pg = PROJ0[L] + n
                if pg >= 4:
                    pe.wait_ge(S["proj_free"], pg - 3)
                for c in range(2):
                    pe.wait_ge(S["tile_lo"], tile0(L) + 2 * n + c + 1)
                    for k in range(KT):
                        for m, (w, part) in enumerate(((tile_hi, 0), (tile_lo, 0), (tile_hi, 1))):
                            t = pe.matmul(ps[pg % 4][:, c * T:c * T + T], w[:, c, k * P:k * P + P], xt_parts[:, part, k, :],
                                          start=k == 0 and m == 0, stop=k == KT - 1 and m == 2)
                    t.then_inc(S["tile_used"], 1)

            def project_out(L, n_ct, ready):
                for ct in range(n_ct):
                    ready(ct)
                    pe.wait_ge(S["lhs_lo"], lhs0(L) + ct + 1)
                    pe.wait_ge(S["tile_lo"], out0(L) + ct + 1)
                    for tt in range(TT):
                        tok = slice(tt * P, tt * P + P)
                        for half in range(2):
                            c = slice(half * 512, half * 512 + 512)
                            for n, (part, w) in enumerate(((0, tile_hi), (0, tile_lo), (1, tile_hi))):
                                t = pe.matmul(ps[4 + 2 * tt + half][:, :], lhs_parts[:, ct % LB, part, tok], w[:, ct % 2, c],
                                              start=ct == 0 and n == 0, stop=ct == n_ct - 1 and n == 2)
                    t.then_inc(S["tile_used"], 1)

            def parameters():
                pe.wait_ge(S["par_in"], 16 * 8)
                pe.wait_ge(S["par_rows_d"], 2)
                for j in range(2):
                    pe.transpose(ps[7][:, 176 * j:176 * j + 96], par_rows[0:96, j, 0, :], ident[0:96, 0:96])
                    t = pe.transpose(ps[7][:, 176 * j + 96:176 * j + 176], par_rows[0:80, j, 1, :], ident[0:80, 0:80])
                t.then_inc(S["par_ps"], 1)
                pe.wait_ge(S["a_exp"], 1)
                pe.matmul(ps[6][:, 0:2 * NH], ones[0:1, :], a_row[0:1, :, :].rearrange("p a b -> p (a b)"),
                          start=True, stop=True).then_inc(S["a_ps"], 1)

            def xt_wait(n):
                pe.wait_ge(S["xt_sb"], 4 * (n + 1))

            def ssd(L):
                j = occ[L]
                pg0 = PROJ0[L]
                u0 = UNIT0[L]
                xt_wait(2 * L)
                if L == 0:
                    pe.wait_ge(S["w_dt_in"], 16 * 3)
                for tt in range(TT):
                    o = ps[4][:, tt * NH:tt * NH + NH]
                    for k in range(KT):
                        pe.matmul(o, xT[:, k, tt * P:tt * P + P], w_dt[:, j, k, :], start=k == 0, stop=False)
                    t = pe.matmul(o, ones[0:1, :], dtb[0:1, j, :], start=False, stop=True)
                t.then_inc(S["dt_ps"], 1)
                pe.wait_ge(S["xt_lo"], 4 * (L + 1))
                for n in range(4):
                    project_in(L, n)
                    if L == 0 and n == 0:
                        parameters()
                pe.wait_ge(S["dt_sb"], 2 * (j + 1))
                da = dts[:, 1, :].rearrange("p (a h) -> p a h", a=TT)
                pe.matmul(ps[5][:, 0:NH], triu[:, 0:P], da[:, 0, :], start=True, stop=True)
                pe.matmul(ps[5][:, NH:2 * NH], ones[:, :], da[:, 0, :], start=True, stop=False)
                pe.matmul(ps[5][:, NH:2 * NH], triu[:, 0:P], da[:, 1, :], start=False, stop=True)
                pe.matmul(ps[6][0:NH, 0:T], da[:, 0, :], triu[:, :], start=True, stop=False)
                pe.matmul(ps[6][0:NH, P:T], da[:, 1, :], triu[:, 0:P], start=False, stop=True)\
                    .then_inc(S["cum_ps"], 1)
                for n in range(4, 12):
                    project_in(L, n)
                pe.wait_ge(S["conv_done"], j * CT_BC + 8)
                pe.wait_ge(S["cum_sb"], 2 * (j + 1))
                for g in range(NG):
                    bt, c_t = cv[:, CT_X + g, :], cv[:, CT_X + NG + g, :]
                    pe.matmul(ps[4 + g][:, 0:T], bt[:, 0:P], c_t[:, :], start=True, stop=True)
                    pe.matmul(ps[4 + g][:, T:SC], bt[:, P:T], c_t[:, P:T], start=True, stop=True)\
                        .then_inc(S["cb_ps"], 1)
                for n in range(12, 20):
                    project_in(L, n)
                pe.wait_ge(S["conv_done"], j * CT_BC + 24)
                for q in range(8):
                    tt, c4 = q % 2, q // 2
                    if q < 4:
                        pe.wait_ge(S["cb_sb"], NG * j + q + 1)
                    else:
                        pe.wait_ge(S["xdt_sb"], 8 * j + q - 3)
                    for c in range(4):
                        t = pe.transpose(ps[4 + q % 4][:, c * P:c * P + P], cv[:, 4 * c4 + c, tt * P:tt * P + P], ident[:])
                    t.then_inc(S["xs_ps"], 1)

                def bc(h):
                    if h == 0:
                        pe.wait_ge(S["proj_free"], pg0 + 20)
                    if h >= 3:
                        pe.wait_ge(S["seg_sb"], 2 * (j * NH + h - 2))
                    pe.matmul(ps[h % 3][:, 0:SC], pick[:, h:h + 1].to_broadcast([2 * NH, P]), acT[:, :],
                              start=True, stop=True).then_inc(S["bc_ps"], 1)

                def yh(h):
                    b = 4 + (h // 4) % 4
                    if h == 0:
                        pe.wait_ge(S["xdt_sb"], 8 * (j + 1))
                    if h % 4 == 0 and h >= 16:
                        pe.wait_ge(S["y2_sb"], j * CT_X + 2 * (h // 4 - 3))
                    pe.wait_ge(S["m_sb"], j * NH + h + 1)
                    lo = DH * (h % 2)
                    c = T * ((h % 4) // 2)
                    o = ps[b][lo:lo + DH, :]
                    pe.matmul(o[:, c:c + T], xdt[:, 0, h * DH:h * DH + DH], mm_[:, h % HB, 0:T], start=True, stop=False)
                    t = pe.matmul(o[:, c + P:c + T], xdt[:, 1, h * DH:h * DH + DH], mm_[:, h % HB, T:SC],
                                  start=False, stop=True)
                    t.then_inc(S["y_ps"], 1)

                def sumsq(g):
                    if g >= 1:
                        pe.wait_ge(S["ss_sb"], j * NG + g)
                    for c in range(4):
                        pe.wait_ge(S["sq_sb"], j * CT_X + 4 * g + c + 1)
                        t = pe.matmul(ps[3][:, (g % 2) * T:(g % 2) * T + T], ones[:, :], sq[:, c, :],
                                      start=c == 0, stop=c == 3)
                    t.then_inc(S["ss_ps"], 1)

                for h in range(3):
                    bc(h)
                for h in range(NH):
                    if h + 3 < NH:
                        bc(h + 3)
                    yh(h)
                    if h % 8 == 4 and h >= 8:
                        sumsq(h // 8 - 1)

                def ready(ct):
                    if ct == 0:
                        pe.wait_ge(S["y2_sb"], CT_X * (j + 1))
                    if ct == 1:
                        sumsq(NG - 1)

                project_out(L, CT_X, ready)

            def attention(L):
                m = att[L]
                kind = KINDS[L]
                pg0, u0 = PROJ0[L], UNIT0[L]
                xt_wait(2 * L)
                pe.wait_ge(S["xt_lo"], 4 * (L + 1))
                nqk = N_SPLIT[kind]
                for n in range(nqk):
                    project_in(L, n)
                for n in range(nqk, N_IN[kind]):
                    pg = pg0 + n
                    unit_wait(u0 + n)
                    pe.wait_ge(S["proj_free"], pg - 3)
                    w = unit(u0 + n, KT)
                    for tt in range(TT):
                        for k in range(KT):
                            t = pe.matmul(ps[pg % 4][:, tt * T:tt * T + T], xT[:, k, tt * P:tt * P + P], w[:, k, :],
                                          start=k == 0, stop=k == KT - 1)
                    t.then_inc(S["v_ready"], 1)
                pe.wait_ge(S["proj_free"], pg0 + N_IN[kind])

                def heads(h):
                    kvh = h // (AH // KVH) if kind == SWA else h
                    lo = DH * (h % 2)
                    kc = kvh if kind == SWA else h // 2
                    return lo, kvh, kc

                def scores(h):
                    lo, kvh, kc = heads(h)
                    b = h % 2
                    if h >= 2:
                        pe.wait_ge(S["max_sb"], AH * m + h - 1)
                    q = qT[lo:lo + DH, h // 2, :]
                    k = kT[lo:lo + DH, kc, :]
                    pe.matmul(ps[b][:, 0:P], q[:, 0:P], k[:, 0:P], start=True, stop=True)
                    pe.matmul(ps[b][:, P:SC], q[:, P:T], k[:, :], start=True, stop=True).then_inc(S["s_ps"], 1)

                def turn_p(h):
                    b = 2 + h % 2
                    pe.wait_ge(S["p_sb"], AH * m + h + 1)
                    if h >= 2:
                        pe.wait_ge(S["pt_sb"], AH * m + h - 1)
                    pe.transpose(ps[b][:, 0:P], lg[:, h % 2, 0:P], ident[:])
                    pe.transpose(ps[b][:, P:2 * P], lg[:, h % 2, P:2 * P], ident[:])
                    pe.transpose(ps[b][:, 2 * P:SC], lg[:, h % 2, 2 * P:SC], ident[:]).then_inc(S["pt_ps"], 1)

                def pv(h):
                    lo, kvh, kc = heads(h)
                    b = 4 + (h // 4) % 4
                    pe.wait_ge(S["pt_sb"], AH * m + h + 1)
                    c = T * ((h % 4) // 2)
                    o = ps[b][lo:lo + DH, :]
                    pe.matmul(o[:, c:c + T], v[:, 0, kvh * DH:kvh * DH + DH], pT[:, h % 2, 0:T], start=True, stop=False)
                    pe.matmul(o[:, c + P:c + T], v[:, 1, kvh * DH:kvh * DH + DH], pT[:, h % 2, T:SC],
                              start=False, stop=True).then_inc(S["o_ps"], 1)

                scores(0)
                scores(1)
                for h in range(AH):
                    turn_p(h)
                    if h + 2 < AH:
                        scores(h + 2)
                    pv(h)
                pe.wait_ge(S["o_sb"], 4 * (m + 1))
                project_out(L, 8, lambda ct: None)

            def moe(L, g):
                xt_wait(2 * L + 1)
                if L == 0:
                    pe.wait_ge(S["rt_in"], 16 * 3)
                for tt in range(TT):
                    for k in range(KT):
                        t = pe.matmul(ps[4][:, tt * NE:tt * NE + NE], xT[:, k, tt * P:tt * P + P], w_rt[:, k, :],
                                      start=k == 0, stop=k == KT - 1)
                t.then_inc(S["rt_ps"], 1)
                if L == 0:
                    pe.wait_ge(S["zeroed"], 6)
                pe.wait_ge(S["sel_sb"], L + 1)
                pe.matmul(ps[5][:, 0:NE], triu_r[:, :], chosen[:, 0, :], start=True, stop=True)
                pe.matmul(ps[5][:, NE:2 * NE], ones_r[:, :], chosen[:, 0, :], start=True, stop=False)
                pe.matmul(ps[5][:, NE:2 * NE], triu_r[:, :], chosen[:, 1, :], start=False, stop=True)
                pe.matmul(ps[5][:, 2 * NE:3 * NE], ones_r[:, :], chosen[:, 0, :], start=True, stop=False)
                pe.matmul(ps[5][:, 2 * NE:3 * NE], ones_r[:, :], chosen[:, 1, :], start=False, stop=True)\
                    .then_inc(S["pos_ps"], 1)
                pe.wait_ge(S["nwin_sb"], L + 1)
                for bank in range(4, 8):
                    pe.matmul(ps[bank][:, :], zero[0:1, 0:P], zero[0:1, :], start=True, stop=False,
                              skip_group_check=True)
                g1 = pe.snap(g + pe.value_load(nwin[0:1, 0:1], min_val=1, max_val=T // CAP))
                pe.wait_ge(S["xlo_sb"], L + 1)

                def gather(bank, kp, pair):
                    for k in (2 * kp, 2 * kp + 1):
                        o = ps[bank][:, (k % 2) * T:(k % 2) * T + T].rearrange("p (e m c) -> p e m c", e=PAIR, m=2)
                        for part, src in enumerate((x_hi, x_lo)):
                            for tt in range(TT):
                                t = pe.matmul(o[:, :, part, :], src[:, tt, k:D:KT], disp[:, tt, pair, 0:CAP],
                                              start=tt == 0, stop=tt == TT - 1)
                    t.then_inc(S["fill_ps"], 1)

                def gate_up(gw, o, e):
                    E = gw * NE + o + (E0 + e)
                    pe.wait_ge(S["fill_sb"], gw * FILLS + o * 2 + (3 + 4 * (e // PAIR)))
                    pe.wait_ge(S["htl_sb"], E)
                    for n, (hi_ready, lo_ready, done) in enumerate((("gate_hi", "gate_lo", "gate_used"),
                                                                    ("up_hi", "up_lo", "up_used"))):
                        for k in range(KT):
                            if k % (KT // 2) == 0:
                                pe.wait_ge(S[hi_ready], 2 * E + (k // (KT // 2) + 1))
                                pe.wait_ge(S[lo_ready], 2 * E + (k // (KT // 2) + 1))
                            if n == 0 and k == KT - 2:
                                pe.wait_ge(S["fill_sb"], gw * FILLS + o * 2 + (4 + 4 * (e // PAIR)))
                            for m, w in enumerate((w_hi[n], w_lo[n])):
                                t = pe.matmul(ps[0][:, n * FF:n * FF + FF], xg[:, (e // PAIR) % 2, k, e % PAIR, :],
                                              w[:, k * FF:k * FF + FF],
                                              start=k == 0 and m == 0, stop=k == KT - 1 and m == 1)
                            if k % (KT // 2) == KT // 2 - 1:
                                t.then_inc(S[done], 1)

                def turn_h(gw, o, e):
                    pe.wait_ge(S["consts"], 7)
                    pe.wait_ge(S["h_sb"], gw * NE + o + (E0 + e))
                    for f in range(FT):
                        t = pe.transpose(ps[0][:, f * CAP:f * CAP + CAP], hbuf[:, f * P:f * P + P], ident[0:CAP, 0:CAP])
                    t.then_inc(S["ht_ps"], 1)

                def down(gw, o, e):
                    E = gw * NE + o + (E0 + e)
                    pe.wait_ge(S["htl_sb"], E + 1)
                    pe.wait_ge(S["ylo_sb"], 2 * E)
                    for half in range(2):
                        pe.wait_ge(S["down_hi"], 2 * E + half + 1)
                        pe.wait_ge(S["down_lo"], 2 * E + half + 1)
                        for f in range(FT):
                            for m, w in enumerate((w_hi[2], w_lo[2])):
                                c = f * D + half * 512
                                t = pe.matmul(ps[1 + half][:, :], hi_lo_h[:, f, :, :].rearrange("p m c -> p (m c)"), w[:, c:c + 512],
                                              start=f == 0 and m == 0, stop=f == FT - 1 and m == 1)
                        t.then_inc(S["yp_ps"], 1)

                def combine(gw, o, e):
                    E = gw * NE + o + (E0 + e)
                    pe.wait_ge(S["sel_tok"], E + 1)
                    for half in range(2):
                        pe.wait_ge(S["ylo_sb"], 2 * E + half + 1)
                        for tt in range(TT):
                            for y in (y_hi, y_lo):
                                t = pe.matmul(ps[4 + 2 * tt + half][:, :], sel[:, e % 2, tt * P:tt * P + P],
                                              y[:, e % 2, half * 512:half * 512 + 512], start=False, stop=False,
                                              skip_group_check=True)
                    t.then_inc(S["comb_ps"], 1)

                def slots(gw):
                    pe.wait_ge(S["gates_hl"], L + 1)
                    pe.wait_ge(S["disp_sb"], gw * 2 + 2)
                    for e in range(NE):
                        for tt in range(TT):
                            t = pe.matmul(ps[1][:, 2 * e:2 * e + 2], disp[:, tt, e, :], gates[:, tt, e, :],
                                          start=tt == 0, stop=tt == TT - 1)
                    t.then_inc(S["gates_ps"], 1)
                    for q in range(NE // 2):
                        if q >= 3:
                            pe.wait_ge(S["tok_v" if (q - 3) % 2 else "tok_a"], gw * 4 + ((q - 3) // 2 + 1))
                        elif q == 2:
                            pe.wait_ge(S["gs_sb"], gw + 1)
                        for r in range(2):
                            for tt in range(TT):
                                t = pe.matmul(ps[SLOT_BANKS[q % 3]][:, r * T + tt * P:r * T + tt * P + P], disp[:, tt, 2 * q + r, :],
                                              ident_r[:, :], start=True, stop=True)
                        t.then_inc(S["pro_ps"], 1)
                    pe.wait_ge(S["tok_a"], gw * 4 + 4)
                    pe.wait_ge(S["tok_v"], gw * 4 + 4)

                def step(gw, o, e):
                    if e < NE:
                        gate_up(gw, o, e)
                    if e == 0:
                        slots(gw)
                    if 1 <= e <= NE:
                        down(gw, o, e - 1)
                    for r in range(2):
                        if e < NE - PAIR:
                            n = 2 * (e % PAIR) + r
                            pair = bass.ds(o + (e // PAIR + 1) * PAIR, PAIR)
                            pe.wait_ge(S["fill_sb"], gw * FILLS + o * 2 + (4 + 4 * (e // PAIR) + n))
                            gather(3, n, pair)
                        if r == 0:
                            if e < NE:
                                turn_h(gw, o, e)
                            if e >= 2:
                                combine(gw, o, e - 2)

                with pe.Fori(g, g1) as gw:
                    pe.wait_ge(S["disp_sb"], gw * 2 + 1)
                    for kp in range(4):
                        gather(kp, kp, slice(0, PAIR))
                    for e in range(PEEL):
                        step(gw, 0, e)
                    with pe.Fori(0, (NE - 2 * PEEL) // BODY) as i:
                        o = i * BODY
                        for e in range(PEEL, PEEL + BODY):
                            step(gw, o, e)
                    for e in range(NE - PEEL, NE + 2):
                        step(gw, 0, e)
                return g1

            pe.wait_ge(S["consts"], 7)
            for name, n in (("gate_used", 2), ("up_used", 2), ("ht_ps", 1), ("yp_ps", 2), ("comb_ps", 1)):
                pe.nop().then_inc(S[name], E0 * n)
            turn_x(0)
            g = 0
            for L in range(DEPTH):
                if KINDS[L] == SSD:
                    ssd(L)
                else:
                    attention(L)
                turn_x(2 * L + 1)
                g = moe(L, g)
                if L < DEPTH - 1:
                    turn_x(2 * L + 2)

        @block.scalar
        def _(act):
            for j in range(2):
                act.dma_start(w_dt[:, j, :, :], a["ssd_w_in"][j].rearrange("(p k) n -> p k n", k=KT)[:, :, DI + XBC:DI + XBC + NH]).then_inc(S["w_dt_in"], 16)
            act.dma_start(dtb[0:1, :, :], a["ssd_dt_bias"].rearrange("(o j) h -> o j h", o=1)).then_inc(S["w_dt_in"], 16)
            act.wait_ge(S["pool_step"], 1)
            for j in range(2):
                act.dma_start(par_rows[0:96, j, 0, :], a["ssd_conv_w"][j].rearrange("k (c p) -> (k c) p", p=P)).then_inc(S["par_in"], 16)
                act.dma_start(par_rows[32:56, j, 1, :], a["ssd_conv_b"][j].rearrange("(c p) -> c p", p=P)).then_inc(S["par_in"], 16)
                act.dma_start(par_rows[64:80, j, 1, :], a["ssd_norm_w"][j].rearrange("(c p) -> c p", p=P)).then_inc(S["par_in"], 16)
            act.dma_start(d_rows[:, :, :], a["ssd_d_skip"].rearrange("j (c r) -> c j r", r=2)).then_inc(S["par_in"], 16)
            act.dma_start(a_row[0:1, :, :], a["ssd_a_log"].rearrange("(o j) h -> o j h", o=1)).then_inc(S["par_in"], 16)

            def xt_evac(n):
                for kp in range(4):
                    act.wait_ge(S["xt_ps"], 4 * n + kp + 1)
                    x_t = ps[kp][:, :].rearrange("p (a t) -> p a t", a=2)
                    act.activation(xT[:, 2 * kp:2 * kp + 2, :], x_t, ACT.Copy).then_inc(S["xt_sb"], 1)
                    if n % 2 == 0:
                        act.activation(xt_parts[:, 0, 2 * kp:2 * kp + 2, :], x_t, ACT.Copy).then_inc(S["xt_hi"], 1)

            def tile_high(L, i):
                u, w, hi, _ = tile_of(L, i)
                act.wait_ge(loaded[slot(u)], 16 * landed(u))
                if tile0(L) + i >= 2:
                    act.wait_ge(S["tile_used"], tile0(L) + i - 1)
                act.activation(hi, w, ACT.Copy).then_inc(S["tile_hi"], 1)

            def lhs_high(L, lhs, ct, ready, at):
                act.wait_ge(S[ready], at)
                if ct >= LB:
                    act.wait_ge(S["tile_used"], out0(L) + ct - LB + 1)
                act.activation(lhs_parts[:, ct % LB, 0, :], lhs[:, ct, :], ACT.Copy).then_inc(S["lhs_hi"], 1)

            def norm(n):
                for tt in range(TT):
                    act.wait_ge(S["ln_stats"], TT * n + tt + 1)
                    act.activation(rs[:, tt:tt + 1], mv[:, tt, 1:2], ACT.Sqrt).then_inc(S["ln_root"], 1)

            def ssd(L):
                j = occ[L]
                pg0 = PROJ0[L]

                def silu_conv(n):
                    t0 = 2 * order[n][1]
                    act.wait_ge(S["conv_acc"], j * 12 + n + 1)
                    for c in range(2):
                        act.activation(cv[:, t0 + c, :], cacc[:, 2 * (n % 2) + c, :], ACT.Silu, bias=par_cb(j, t0 + c))\
                            .then_inc(S["conv_done"], 1)

                def softplus_exp():
                    act.wait_ge(S["dt_abs"], 2 * j + 2)
                    act.activation(dts[:, 2, :], dts[:, 3, :], ACT.Exp).then_inc(S["dt_exp"], 1)

                def softplus_ln():
                    act.wait_ge(S["dt_u"], j + 1)
                    act.activation(dts[:, 5, :], dts[:, 4, :], ACT.Ln).then_inc(S["dt_ln"], 1)

                tile_high(L, 0)
                tile_high(L, 1)
                softplus_exp()
                softplus_ln()
                for n in range(12):
                    tile_high(L, 2 * n + 2)
                    if n >= 2:
                        silu_conv(n - 2)
                    tile_high(L, 2 * n + 3)
                    act.wait_ge(*projected(L, n))
                    if n >= 4:
                        act.wait_ge(S["conv_acc"], j * 12 + n - 3)
                    s = 2 * (n % 4)
                    act.activation(xbc[:, s:s + 2, 3:259], ps[(pg0 + n) % 4][:, :].rearrange("p (a t) -> p a t", a=2),
                                   ACT.Copy).then_inc(S["proj_free"], 1)
                for n in range(12, 20):
                    tile_high(L, 2 * n + 2)
                    if n <= 13:
                        silu_conv(n - 2)
                    tile_high(L, 2 * n + 3)
                    act.wait_ge(*projected(L, n))
                    t0 = 2 * order[n][1]
                    act.activation(sz[:, t0:t0 + 2, :], ps[(pg0 + n) % 4][:, :].rearrange("p (a t) -> p a t", a=2),
                                   ACT.Silu).then_inc(S["proj_free"], 1)
                for h in range(NH):
                    act.wait_ge(S["seg_sb"], 2 * (j * NH + h + 1))
                    if h >= HB:
                        act.wait_ge(S["m_sb"], j * NH + h - HB + 1)
                    act.activation(dec[:, h % HB, :], seg[:, h % HB, :], ACT.Exp).then_inc(S["dec_sb"], 1)
                    if h % 4 == 2 and h >= 4:
                        square(j, h // 4 - 1)
                for g in range(NG - 1):
                    root(j, g)
                square(j, 7)
                for ct in range(3):
                    lhs_high(L, sz, ct, "yn_sb", j * CT_X + ct + 1)
                for ct in range(CT_X):
                    if ct + 2 < CT_X:
                        tile_high(L, 2 * N_SPLIT[KINDS[L]] + ct + 2)
                    if ct + 3 < CT_X:
                        lhs_high(L, sz, ct + 3, "yn_sb", j * CT_X + ct + 4)
                    if ct == 3:
                        root(j, NG - 1)

            def root(j, g):
                act.wait_ge(S["ss_sb"], NG * j + g + 1)
                act.activation(gsum[:, g, :], gsum[:, g, :], ACT.Sqrt).then_inc(S["ss_root"], 1)

            def square(j, q):
                for c in (2 * q, 2 * q + 1):
                    act.wait_ge(S["y2_sb"], j * CT_X + c + 1)
                    if c >= 4:
                        act.wait_ge(S["ss_ps"], j * NG + c // 4)
                    act.activation(sq[:, c % 4, :], sz[:, c, :], ACT.Square).then_inc(S["sq_sb"], 1)

            def attention(L):
                m = att[L]
                kind = KINDS[L]
                pg0 = PROJ0[L]
                scale = float(DH) ** -0.5
                if kind == SWA:
                    act.wait_ge(S["rt_in"], 16 * 3)
                tile_high(L, 0)
                tile_high(L, 1)
                for n in range(4):
                    tile_high(L, 2 * n + 2)
                    tile_high(L, 2 * n + 3)
                    act.wait_ge(*projected(L, n))
                    act.activation(qT[:, 2 * n:2 * n + 2, :], ps[(pg0 + n) % 4][:, :].rearrange("p (a t) -> p a t", a=2),
                                   ACT.Copy, scale=scale).then_inc(S["proj_free"], 1)
                if kind == SWA:
                    tile_high(L, 10)
                    tile_high(L, 11)
                    act.wait_ge(*projected(L, 4))
                    bank = ps[(pg0 + 4) % 4]
                    for g in range(KVH):
                        src = bank[DH * (g % 2):DH * (g % 2) + DH, (g // 2) * T:(g // 2) * T + T]
                        for half in range(2):
                            ins = act.activation(kT[DH * half:DH * half + DH, g, :], src, ACT.Copy)
                            if g == KVH - 1 and half == 1:
                                ins.then_inc(S["proj_free"], 1)
                    nv = 5
                else:
                    for n in range(4, 8):
                        tile_high(L, 2 * n + 2)
                        tile_high(L, 2 * n + 3)
                        act.wait_ge(*projected(L, n))
                        act.activation(kT[:, 2 * n - 8:2 * n - 6, :],
                                       ps[(pg0 + n) % 4][:, :].rearrange("p (a t) -> p a t", a=2),
                                       ACT.Copy).then_inc(S["proj_free"], 1)
                    nv = 8
                for n in range(nv, N_IN[kind]):
                    act.wait_ge(*projected(L, n))
                    c = 256 * (n - nv)
                    act.activation(v[:, :, c:c + 256], ps[(pg0 + n) % 4][:, :].rearrange("p (a t) -> p a t", a=2),
                                   ACT.Copy).then_inc(S["proj_free"], 1)
                for h in range(AH):
                    act.wait_ge(S["max_sb"], AH * m + h + 1)
                    b = h % 2
                    act.activation(lg[:, b, 0:P], lg[:, b, 0:P], ACT.Exp, bias=hst[:, b, 0:1],
                                   accum_out=hst[:, b, 2:3])
                    if kind == SWA:
                        act.activation(hst[:, b, 4:6], hst[:, b, 0:2], ACT.Exp, bias=sinks[:, h:h + 1])
                    act.activation(lg[:, b, P:SC], lg[:, b, P:SC], ACT.Exp, bias=hst[:, b, 1:2],
                                   accum_out=hst[:, b, 3:4]).then_inc(S["exp_sb"], 1)
                    act.wait_ge(S["pt_ps"], AH * m + h + 1)
                    if h >= 2:
                        act.wait_ge(S["o_ps"], AH * m + h - 1)
                    act.activation(pT[:, b, :], ps[2 + b][:, 0:SC], ACT.Copy).then_inc(S["pt_sb"], 1)
                    if h % 4 == 3:
                        act.wait_ge(S["o_ps"], AH * m + h + 1)
                        c = h // 4
                        act.activation(oT[:, 2 * c:2 * c + 2, :], ps[4 + c][:, :].rearrange("p (a t) -> p a t", a=2),
                                       ACT.Copy).then_inc(S["o_sb"], 1)
                for ct in range(3):
                    lhs_high(L, oT, ct, "o_sb", 4 * m + ct // 2 + 1)
                for ct in range(8):
                    if ct + 2 < 8:
                        tile_high(L, 2 * N_SPLIT[KINDS[L]] + ct + 2)
                    if ct + 3 < 8:
                        lhs_high(L, oT, ct + 3, "o_sb", 4 * m + (ct + 3) // 2 + 1)

            def gate_high(gw, o, e):
                act.wait_ge(loaded_moe[e * UPE % RING], landed_moe(gw, o, e, 0))
                for s in range(2):
                    c = slice(s * UW // 2, (s + 1) * UW // 2)
                    act.wait_ge(S["gate_used"], (gw * NE + o) * 2 + (2 * (E0 + e) + s - 1))
                    act.activation(w_hi[0][:, c], ring[:, e * UPE % RING, c], ACT.Copy).then_inc(S["gate_hi"], 1)

            def down_high(gw, o, e, half):
                act.wait_ge(loaded_moe[(e * UPE + 2) % RING], landed_moe(gw, o, e, 2))
                act.wait_ge(S["yp_ps"], (gw * NE + o) * 2 + (2 * (E0 + e) + half - 1))
                act.activation(down_half(w_hi[2][:, :], half), down_half(ring[:, (e * UPE + 2) % RING, :], half), ACT.Copy)\
                    .then_inc(S["down_hi"], 1)

            def moe(L, g):
                act.activation(x_hi[:, :, :], x[:, :, :], ACT.Copy).then_inc(S["xhi_sb"], 1)
                act.wait_ge(S["rt_ps"], L + 1)
                act.activation(rt[:, 1, :, :], ps[4][:, 0:TT * NE].rearrange("p (a e) -> p a e", a=TT), ACT.Exp,
                               scale=-1.0).then_inc(S["rt_exp"], 1)
                act.wait_ge(S["nwin_sb"], L + 1)
                g1 = act.snap(g + act.value_load(nwin[0:1, 0:1], min_val=1, max_val=T // CAP))

                def fill_evac(gw, o, n, buf, kp, bank):
                    act.wait_ge(S["fill_ps"], gw * FILLS + o * 2 + (n + 1))
                    act.activation(xg[:, buf, 2 * kp:2 * kp + 2, :, :].rearrange("p k e c -> p (k e c)"),
                                   ps[bank][:, :], ACT.Copy).then_inc(S["fill_sb"], 1)

                def step(gw, o, e):
                    E = gw * NE + o + (E0 + e)
                    if e + 1 < NE:
                        gate_high(gw, o, e + 1)
                    if e < NE:
                        act.wait_ge(S["up_used"], 2 * E + 2)
                        act.activation(fold[:, :], ps[0][CAP:P, :], ACT.Copy).then_inc(S["fold_sb"], 1)
                    if 1 <= e <= NE:
                        act.wait_ge(S["comb_ps"], E - 2)
                        if e == 1:
                            act.wait_ge(S["tok_a"], gw * 4 + 4)
                            act.wait_ge(S["tok_v"], gw * 4 + 4)
                        act.activation(sel[:, (e - 1) % 2, :].unsqueeze(1), slot_tok[:, bass.ds(o + (e - 1), 1), :], ACT.Copy)\
                            .then_inc(S["sel_tok"], 1)
                    for half in range(2):
                        if 1 <= e <= NE:
                            c = slice(half * 512, half * 512 + 512)
                            act.wait_ge(S["yp_ps"], 2 * E + (half - 1))
                            act.activation(y_hi[:, (e - 1) % 2, c], ps[1 + half][:, :], ACT.Copy).then_inc(S["yhi_sb"], 1)
                        if half == 0 and e < NE:
                            act.wait_ge(S["sum_sb"], E + 1)
                            act.activation(sil[:, :], gu[:, 0:FF], ACT.Silu).then_inc(S["sil_sb"], 1)
                        if half == 0 and e == 0:
                            for q in range(0, NE // 2, 2):
                                act.wait_ge(S["pro_ps"], gw * (NE // 2) + (q + 1))
                                act.activation(slot_tok[:, 2 * q:2 * q + 2, :],
                                               ps[SLOT_BANKS[q % 3]][:, :].rearrange("p (e t) -> p e t", e=2), ACT.Copy)\
                                    .then_inc(S["tok_a"], 1)
                    for r in range(2):
                        if e < NE:
                            down_high(gw, o, e, r)
                        if e < NE - PAIR:
                            fill_evac(gw, o, 4 + 2 * e + r, (e // PAIR + 1) % 2, 2 * (e % PAIR) + r, 3)
                        if r == 0 and e < NE:
                            act.wait_ge(S["ht_ps"], E + 1)
                            act.activation(hi_lo_h[:, :, 0, :], ps[0][:, 0:FT * CAP].rearrange("p (f c) -> p f c", f=FT),
                                           ACT.Copy).then_inc(S["hth_sb"], 1)

                with act.Fori(g, g1) as gw:
                    with act.If(gw > g):
                        gate_high(gw, 0, 0)
                    for kp in range(4):
                        fill_evac(gw, 0, kp, 0, kp, kp)
                    for e in range(PEEL):
                        step(gw, 0, e)
                    with act.Fori(0, (NE - 2 * PEEL) // BODY) as i:
                        o = i * BODY
                        for e in range(PEEL, PEEL + BODY):
                            step(gw, o, e)
                    for e in range(NE - PEEL, NE + 1):
                        step(gw, 0, e)
                return g1

            for name, n in (("gate_hi", 2), ("down_hi", 2), ("fold_sb", 1), ("sil_sb", 1), ("hth_sb", 1), ("yhi_sb", 2),
                            ("sel_tok", 1)):
                act.nop().then_inc(S[name], E0 * n)
            xt_evac(0)
            act.wait_ge(S["par_in"], 16 * 8)
            act.activation(a_row[0:1, :, :], a_row[0:1, :, :], ACT.Exp).then_inc(S["a_exp"], 1)
            g = 0
            for L in range(DEPTH):
                if KINDS[L] == SSD:
                    ssd(L)
                else:
                    attention(L)
                norm(2 * L)
                gate_high(g, 0, 0)
                xt_evac(2 * L + 1)
                g = moe(L, g)
                norm(2 * L + 1)
                if L < DEPTH - 1:
                    xt_evac(2 * L + 2)

        @block.vector
        def _(dve):
            steps = [0]

            def link(ins):
                steps[0] += 1
                ins.then_inc(S["dve_step"], 1)
                dve.wait_ge(S["dve_step"], steps[0])

            dve.wait_ge(S["consts"], 7)
            for to, of in ((ident_r, ident[:, :]), (ones_r, ones[:, :]), (triu_r, triu[:, 0:P])):
                dve.tensor_copy(to[:, :], of).then_inc(S["zeroed"], 1)
            for n in range(2):
                dve.tensor_copy(pick[n * NH:n * NH + NH, :], ident[0:NH, 0:NH]).then_inc(S["zeroed"], 1)
            dve.memset(zero[:, :].bitcast(F32), 0.0).then_inc(S["zeroed"], 1)
            dve.wait_ge(S["par_in"], 16 * 8)
            dve.wait_ge(S["pool_step"], 1)
            for j in range(2):
                dve.tensor_copy(par_rows[0:CT_X, j, 1, :].rearrange("c (r q) -> c r q", r=2),
                                d_rows[:, j, :].unsqueeze(2).to_broadcast([CT_X, 2, DH])).then_inc(S["par_rows_d"], 1)

            def xt_low(L):
                for kp in range(4):
                    k = slice(2 * kp, 2 * kp + 2)
                    dve.wait_ge(S["xt_hi"], 4 * L + kp + 1)
                    dve.tensor_tensor(xt_parts[:, 1, k, :], xT[:, k, :], xt_parts[:, 0, k, :].bitcast(F32), ALU.subtract)\
                        .then_inc(S["xt_lo"], 1)

            def tile_low(L, i):
                _, w, hi, lo = tile_of(L, i)
                dve.wait_ge(S["tile_hi"], tile0(L) + i + 1)
                dve.tensor_tensor(lo, w, hi.bitcast(F32), ALU.subtract).then_inc(S["tile_lo"], 1)

            def lhs_low(L, lhs, ct):
                dve.wait_ge(S["lhs_hi"], lhs0(L) + ct + 1)
                dve.tensor_tensor(lhs_parts[:, ct % LB, 1, :], lhs[:, ct, :], lhs_parts[:, ct % LB, 0, :].bitcast(F32),
                                  ALU.subtract).then_inc(S["lhs_lo"], 1)

            def norm(n):
                if n == 0:
                    dve.wait_ge(S["x_in"], 16)

                def residual(tt):
                    for half in range(2):
                        c = slice(half * 512, half * 512 + 512)
                        dve.scalar_tensor_tensor(x[:, tt, c], x[:, tt, c], ALPHA, ps[4 + 2 * tt + half][:, :],
                                                 ALU.mult, ALU.add).then_inc(S["res_done"], 1)

                def statistics(tt):
                    for half in range(2):
                        c = slice(half * 512, half * 512 + 512)
                        dve.wait_ge(S["res_done"], 4 * n + 2 * tt + half + 1)
                        ins = dve.bn_stats(st[:, tt, half, :], x[:, tt, c])
                    link(ins)
                    link(dve.bn_aggr(mv[:, tt, :], st[:, tt, :, :]))
                    dve.tensor_scalar(mv[:, tt, 1:2], mv[:, tt, 1:2], EPS, None, ALU.add).then_inc(S["ln_stats"], 1)

                def scale(tt):
                    dve.wait_ge(S["ln_root"], TT * n + tt + 1)
                    dve.reciprocal(rs[:, tt:tt + 1], rs[:, tt:tt + 1]).then_inc(S["ln_rs"], 1)
                    dve.wait_ge(S["lngb_in"], 32 * (n + 1))
                    link(dve.scalar_tensor_tensor(x[:, tt, :], x[:, tt, :], mv[:, tt, 0:1], ln_gb[:, 0, :],
                                                  ALU.subtract, ALU.mult))
                    dve.wait_ge(S["ln_rs"], TT * n + tt + 1)
                    dve.scalar_tensor_tensor(x[:, tt, :], x[:, tt, :], rs[:, tt:tt + 1], ln_gb[:, 1, :],
                                             ALU.mult, ALU.add).then_inc(S["ln_done"], 1)

                for part in (residual, statistics, scale):
                    for tt in range(TT):
                        part(tt)

            def ssd(L):
                j = occ[L]
                link(dve.memset(xbc[:, :, 0:3], 0.0))
                xt_low(L)
                tile_low(L, 0)
                tile_low(L, 1)
                if L == 0:
                    dve.wait_ge(S["par_ps"], 1)
                    dve.tensor_copy(par[:, :, :].rearrange("p j c -> p (j c)"), ps[7][:, 0:2 * 176]).then_inc(S["par_sb"], 1)
                    dve.wait_ge(S["a_ps"], 1)
                    dve.tensor_copy(a_bc[:, :, :].rearrange("p a b -> p (a b)"), ps[6][:, 0:2 * NH]).then_inc(S["a_sb"], 1)
                    dve.wait_ge(S["par_sb"], 1)
                    dve.wait_ge(S["a_sb"], 1)
                dve.wait_ge(S["dt_ps"], j + 1)
                pre = ps[4][:, 0:TT * NH]
                dve.tensor_scalar(dts[:, 6, :], pre, 0.0, None, ALU.max).then_inc(S["dt_abs"], 1)
                dve.wait_ge(S["dt_abs"], 2 * j + 1)
                dve.scalar_tensor_tensor(dts[:, 3, :], dts[:, 6, :], -2.0, pre, ALU.mult, ALU.add).then_inc(S["dt_abs"], 1)
                dve.wait_ge(S["dt_exp"], j + 1)
                dve.tensor_scalar(dts[:, 4, :], dts[:, 2, :], 1.0, None, ALU.add).then_inc(S["dt_u"], 1)
                dve.wait_ge(S["dt_u"], j + 1)
                link(dve.scalar_tensor_tensor(dts[:, 7, :], dts[:, 4, :], 1.0, dts[:, 2, :], ALU.subtract, ALU.subtract))
                link(dve.reciprocal(dts[:, 2, :], dts[:, 4, :]))
                link(dve.tensor_tensor(dts[:, 7, :], dts[:, 7, :], dts[:, 2, :], ALU.mult))
                link(dve.tensor_tensor(dts[:, 6, :], dts[:, 6, :], dts[:, 7, :], ALU.subtract))
                dve.wait_ge(S["dt_ln"], j + 1)
                dve.tensor_tensor(dts[:, 0, :], dts[:, 6, :], dts[:, 5, :], ALU.add).then_inc(S["dt_sb"], 1)
                dve.wait_ge(S["dt_sb"], 2 * j + 1)
                dve.scalar_tensor_tensor(dts[:, 1, :].rearrange("p (a h) -> p a h", a=TT),
                                         dts[:, 0, :].rearrange("p (a h) -> p a h", a=TT), -1.0,
                                         a_bc[:, j, :].unsqueeze(1).to_broadcast([P, TT, NH]), ALU.mult, ALU.mult)\
                    .then_inc(S["dt_sb"], 1)

                def conv(n, taps):
                    if 0 in taps:
                        dve.wait_ge(S["proj_free"], PROJ0[L] + n + 1)
                        if n >= 2:
                            dve.wait_ge(S["conv_done"], j * CT_BC + 2 * (n - 1))
                    t0 = 2 * order[n][1]
                    for k in taps:
                        for c in range(2):
                            src = xbc[:, 2 * (n % 4) + c, k:k + T]
                            dst = cacc[:, 2 * (n % 2) + c, :]
                            w = par_cw(j, t0 + c, k)
                            if k == 0:
                                ins = dve.tensor_scalar(dst, src, w, None, ALU.mult)
                            else:
                                ins = dve.scalar_tensor_tensor(dst, src, w, dst, ALU.mult, ALU.add)
                            if k == CONV - 1 and c == 1:
                                ins.then_inc(S["conv_acc"], 1)
                            elif c == 1:
                                link(ins)
                for n in range(20):
                    tile_low(L, 2 * n + 2)
                    if 1 <= n <= 12:
                        conv(n - 1, (0, 1))
                    tile_low(L, 2 * n + 3)
                    if 1 <= n <= 12:
                        conv(n - 1, (2, 3))
                    if n == 5:
                        dve.wait_ge(S["cum_ps"], j + 1)
                        dve.tensor_copy(dts[:, 7, :], ps[5][:, 0:TT * NH]).then_inc(S["cum_sb"], 1)
                        for lo_c, hi_c, src in ((0, T, 0), (T, SC, P)):
                            dve.tensor_copy(acT[0:NH, lo_c:hi_c], ps[6][0:NH, src:T])
                            link(dve.tensor_copy(acT[NH:2 * NH, lo_c:hi_c], ps[6][0:NH, src:T]))
                        for lo_c, hi_c, src in ((0, T, 0), (T, SC, P)):
                            ins = dve.tensor_tensor(acT[NH:2 * NH, lo_c:hi_c], ps[6][0:NH, src:T], acT[NH:2 * NH, lo_c:hi_c].bitcast(F32),
                                                    ALU.subtract)
                        ins.then_inc(S["cum_sb"], 1)
                    if n == 13:
                        for g in range(NG):
                            dve.wait_ge(S["cb_ps"], NG * j + g + 1)
                            dve.tensor_tensor(cbm[:, g, 0:T], ps[4 + g][:, 0:T], triu[:, :], ALU.mult)
                            dve.tensor_tensor(cbm[:, g, T:SC], ps[4 + g][:, T:SC], triu[:, 0:P], ALU.mult).then_inc(S["cb_sb"], 1)
                dt_v = dts[:, 0, :].rearrange("p (a h) -> p a h", a=TT)
                for q in range(8):
                    tt, c4 = q % 2, q // 2
                    dve.wait_ge(S["xs_ps"], 8 * j + q + 1)
                    dve.tensor_tensor(xdt[:, tt, 512 * c4:512 * c4 + 512].rearrange("p (h c) -> p h c", c=DH),
                                      ps[4 + q % 4][:, :].rearrange("p (h c) -> p h c", c=DH),
                                      dt_v[:, tt, 8 * c4:8 * c4 + 8].unsqueeze(2).to_broadcast([P, 8, DH]), ALU.mult)\
                        .then_inc(S["xdt_sb"], 1)

                def gating(c):
                    dve.wait_ge(S["y_ps"], j * NH + 4 * (c // 2) + 4)
                    link(dve.scalar_tensor_tensor(ytmp[:, c % 2, :], cv[:, c, :], par_d(j, c),
                                                  ps[4 + (c // 2) % 4][:, (c % 2) * T:(c % 2) * T + T], ALU.mult, ALU.add))
                    dve.tensor_tensor(sz[:, c, :], ytmp[:, c % 2, :], sz[:, c, :], ALU.mult).then_inc(S["y2_sb"], 1)

                def mean_square(g):
                    dve.wait_ge(S["ss_ps"], NG * j + g + 1)
                    dve.tensor_scalar(gsum[:, g, :], ps[3][:, (g % 2) * T:(g % 2) * T + T], 1.0 / (DI // NG), EPS,
                                      ALU.mult, ALU.add).then_inc(S["ss_sb"], 1)

                def group_root(g):
                    dve.wait_ge(S["ss_root"], NG * j + g + 1)
                    link(dve.reciprocal(gsum[:, g, :], gsum[:, g, :]))

                def group_norm(c):
                    dve.scalar_tensor_tensor(sz[:, c, :], sz[:, c, :], par_nw(j, c), gsum[:, c // 4, :],
                                             ALU.mult, ALU.mult).then_inc(S["yn_sb"], 1)

                acs = dts[:, 7, :].rearrange("p (a h) -> p a h", a=TT)
                dve.wait_ge(S["cum_sb"], 2 * (j + 1))
                for h in range(NH):
                    dve.wait_ge(S["bc_ps"], j * NH + h + 1)
                    if h >= HB:
                        dve.wait_ge(S["dec_sb"], j * NH + h - HB + 1)
                    dve.tensor_scalar(seg[:, h % HB, 0:T], ps[h % 3][:, 0:T], acs[:, 0, h:h + 1], 0.0,
                                      ALU.subtract, ALU.min).then_inc(S["seg_sb"], 1)
                    dve.tensor_scalar(seg[:, h % HB, T:SC], ps[h % 3][:, T:SC], acs[:, 1, h:h + 1], 0.0,
                                      ALU.subtract, ALU.min).then_inc(S["seg_sb"], 1)
                    if h % 4 == 1 and h >= 4:
                        gating(2 * (h // 4) - 2)
                        gating(2 * (h // 4) - 1)
                    if h in (15, 23, 31):
                        mean_square(h // 8 - 1)
                gating(14)
                gating(15)
                group_root(0)
                for ct in range(4):
                    group_norm(ct)
                for ct in range(3):
                    lhs_low(L, sz, ct)
                for ct in range(CT_X):
                    if ct + 2 < CT_X:
                        tile_low(L, 2 * N_SPLIT[KINDS[L]] + ct + 2)
                    if ct + 3 < CT_X:
                        lhs_low(L, sz, ct + 3)
                    if ct == 2:
                        mean_square(NG - 1)
                    if ct + 4 < CT_X:
                        if ct % 4 == 0:
                            group_root(ct // 4 + 1)
                        group_norm(ct + 4)

            def attention(L):
                m = att[L]
                kind = KINDS[L]
                if kind == CA:
                    dve.wait_ge(S["rel_in"], 16)
                    dve.tensor_copy(revx[0:AH, 0:127], rel[0:AH, N_REL - 1:N_REL].to_broadcast([AH, 127]))
                    dve.tensor_copy(revx[0:AH, 127:127 + N_REL], rel[0:AH, ::-1])
                    dve.tensor_copy(revx[0:AH, 127 + N_REL:384], rel[0:AH, 0:1].to_broadcast([AH, 384 - 127 - N_REL]))\
                        .then_inc(S["rev_sb"], 1)
                xt_low(L)
                for i in range(2 * N_SPLIT[kind] + 2):
                    tile_low(L, i)
                for h in range(AH):
                    b = h % 2
                    dve.wait_ge(S["s_ps"], AH * m + h + 1)
                    if kind == SWA:
                        dve.wait_ge(S["bias_sb"], 4)
                        slope = 2.0 ** (-8.0 * (h + 1) / AH)
                        bsrc, mul = bias[:, 0, :], slope
                    else:
                        dve.wait_ge(S[f"bias_in{b}"], 16 * 4 * (h // 2 + 1))
                        bsrc, mul = bias[:, b, :], 1.0
                    if kind == CA and h == 0:
                        dve.wait_ge(S["bias_sb"], 8)
                    if h >= 2:
                        dve.wait_ge(S["pt_ps"], AH * m + h - 1)
                    link(dve.scalar_tensor_tensor(lg[:, b, :], bsrc, mul, ps[b][:, 0:SC], ALU.mult, ALU.add))
                    dve.tensor_reduce(hst[:, b, 6:7], lg[:, b, 0:P], AX.X, ALU.max)
                    link(dve.tensor_reduce(hst[:, b, 7:8], lg[:, b, P:SC], AX.X, ALU.max))
                    if kind == SWA:
                        dve.tensor_scalar(hst[:, b, 0:2], hst[:, b, 6:8], sinks[:, h:h + 1], -1.0, ALU.max, ALU.mult)\
                            .then_inc(S["max_sb"], 1)
                    else:
                        dve.tensor_scalar(hst[:, b, 0:2], hst[:, b, 6:8], -1.0, None, ALU.mult).then_inc(S["max_sb"], 1)
                    dve.wait_ge(S["exp_sb"], AH * m + h + 1)
                    if kind == SWA:
                        link(dve.tensor_tensor(hst[:, b, 2:4], hst[:, b, 2:4], hst[:, b, 4:6], ALU.add))
                    link(dve.reciprocal(hst[:, b, 8:10], hst[:, b, 2:4]))
                    dve.tensor_scalar(lg[:, b, 0:P], lg[:, b, 0:P], hst[:, b, 8:9], None, ALU.mult)
                    dve.tensor_scalar(lg[:, b, P:SC], lg[:, b, P:SC], hst[:, b, 9:10], None, ALU.mult)\
                        .then_inc(S["p_sb"], 1)
                for ct in range(3):
                    lhs_low(L, oT, ct)
                for ct in range(8):
                    if ct + 2 < 8:
                        tile_low(L, 2 * N_SPLIT[KINDS[L]] + ct + 2)
                    if ct + 3 < 8:
                        lhs_low(L, oT, ct + 3)

            def low(gw, o, e, n):
                for s in range(2):
                    c = slice(s * UW // 2, (s + 1) * UW // 2)
                    dve.wait_ge(S[("gate_hi", "up_hi")[n]], (gw * NE + o) * 2 + (2 * (E0 + e) + s + 1))
                    dve.tensor_tensor(w_lo[n][:, c], ring[:, (e * UPE + n) % RING, c], w_hi[n][:, c].bitcast(F32),
                                      ALU.subtract).then_inc(S[("gate_lo", "up_lo")[n]], 1)

            def up_high(gw, o, e):
                dve.wait_ge(loaded_moe[(e * UPE + 1) % RING], landed_moe(gw, o, e, 1))
                for s in range(2):
                    c = slice(s * UW // 2, (s + 1) * UW // 2)
                    dve.wait_ge(S["up_used"], (gw * NE + o) * 2 + (2 * (E0 + e) + s - 1))
                    dve.tensor_copy(w_hi[1][:, c], ring[:, (e * UPE + 1) % RING, c]).then_inc(S["up_hi"], 1)

            def moe(L, g):
                R = lambda n: rt[:, n, :, :]
                small = lambda n, w: rt[:, n, :, :].rearrange("p a e -> p (a e)")[:, 0:TT * w].rearrange("p (a e) -> p a e", e=w)
                low(g, 0, 0, 0)
                up_high(g, 0, 0)
                low(g, 0, 0, 1)
                dve.wait_ge(S["xhi_sb"], L + 1)
                dve.tensor_tensor(x_lo[:, :, :], x[:, :, :], x_hi[:, :, :].bitcast(F32), ALU.subtract).then_inc(S["xlo_sb"], 1)
                dve.wait_ge(S["rt_exp"], L + 1)
                link(dve.tensor_scalar(R(1), R(1), 1.0, None, ALU.add))
                link(dve.reciprocal(R(2), R(1)))
                if L == 0:
                    dve.wait_ge(S["rt_in"], 16 * 3)
                link(dve.tensor_tensor(R(3), R(2), rt_bias[:, :].unsqueeze(1).to_broadcast([P, TT, NE]), ALU.add))
                g4 = rt[:, 3, :, :].rearrange("p a (g e) -> p (a g) e", e=4)
                pairs = rt[:, 4:7, :, :].rearrange("p n a e -> p (n a e)")[:, 0:48].rearrange("p (g e) -> p g e", e=6)
                dve.tensor_tensor(pairs[:, :, 0:2], g4[:, :, 0:2], g4[:, :, 2:4], ALU.add)
                dve.tensor_tensor(pairs[:, :, 2:4], g4[:, :, 0:2], g4[:, :, 3:1:-1], ALU.add)
                link(dve.tensor_tensor(pairs[:, :, 4:6], g4[:, :, 0:4:2], g4[:, :, 1:4:2], ALU.add))
                gs = small(7, 4)
                link(dve.tensor_reduce(gs.rearrange("p a g -> p (a g)"), pairs, AX.X, ALU.max))
                m1 = rt[:, 8, 0, :]

                def one_hot(dst, src, w, tmp, c):
                    rk = rank[:, NE - w:NE].unsqueeze(1).to_broadcast([P, TT, w])
                    link(dve.tensor_reduce(m1[:, c:c + TT], src, AX.X, ALU.max))
                    link(dve.tensor_tensor(dst, src, m1[:, c:c + TT].unsqueeze(2).to_broadcast([P, TT, w]), ALU.is_equal))
                    link(dve.tensor_tensor(tmp, dst, rk, ALU.mult))
                    link(dve.tensor_reduce(m1[:, c + TT:c + 2 * TT], tmp, AX.X, ALU.max))
                    link(dve.tensor_tensor(dst, tmp, m1[:, c + TT:c + 2 * TT].unsqueeze(2).to_broadcast([P, TT, w]), ALU.is_equal))

                best = small(9, 4)
                one_hot(best, gs, 4, small(10, 4), 0)
                link(dve.tensor_scalar(small(11, 4), best, 1.0, -NEG, ALU.subtract, ALU.mult))
                selm = R(12)
                link(dve.tensor_tensor(selm.rearrange("p a (g e) -> p (a g) e", e=4), g4,
                                       small(11, 4).rearrange("p a g -> p (a g)").unsqueeze(2).to_broadcast([P, TT * 4, 4]), ALU.add))
                one_hot(R(13), selm, NE, R(14), 4)
                link(dve.scalar_tensor_tensor(R(15), R(13), 4.0 * NEG, selm, ALU.mult, ALU.add))
                one_hot(R(16), R(15), NE, R(14), 8)
                dve.tensor_tensor(chosen[:, :, :], R(13), R(16), ALU.add).then_inc(S["sel_sb"], 1)
                dve.wait_ge(S["sel_sb"], L + 1)
                link(dve.tensor_tensor(R(17), chosen[:, :, :].bitcast(F32), R(2), ALU.mult))
                link(dve.tensor_reduce(m1[:, 12:12 + TT], R(17), AX.X, ALU.add))
                link(dve.reciprocal(m1[:, 14:14 + TT], m1[:, 12:12 + TT]))
                link(dve.tensor_tensor(R(0), R(17), m1[:, 14:14 + TT].unsqueeze(2).to_broadcast([P, TT, NE]), ALU.mult))
                link(dve.tensor_copy(gates[:, :, :, 0], R(0)))
                dve.tensor_tensor(gates[:, :, :, 1], R(0), gates[:, :, :, 0].bitcast(F32), ALU.subtract).then_inc(S["gates_hl"], 1)
                dve.wait_ge(S["pos_ps"], L + 1)
                link(dve.tensor_tensor(posm[:, :, :], ps[5][:, 0:TT * NE].rearrange("p (a e) -> p a e", a=TT),
                                       chosen[:, :, :].bitcast(F32), ALU.mult))
                link(dve.tensor_reduce(m1[0:1, 12:13], ps[5][0:1, 2 * NE:3 * NE], AX.X, ALU.max))
                dve.tensor_scalar(posm[:, :, :], posm[:, :, :], -1.0, None, ALU.add).then_inc(S["posm_sb"], 1)
                link(dve.tensor_scalar(m1[0:1, 13:14], m1[0:1, 12:13], CAP + 0.5, 1.0, ALU.is_gt, ALU.add))
                for n in range(2, T // CAP):
                    link(dve.scalar_tensor_tensor(m1[0:1, 13:14], m1[0:1, 12:13], n * CAP + 0.5, m1[0:1, 13:14],
                                                  ALU.is_gt, ALU.add))
                dve.tensor_copy(nwin[0:1, 0:1], m1[0:1, 13:14]).then_inc(S["nwin_sb"], 1)
                dve.wait_ge(S["nwin_sb"], L + 1)
                dve.wait_ge(S["posm_sb"], L + 1)
                g1 = dve.snap(g + dve.value_load(nwin[0:1, 0:1], min_val=1, max_val=T // CAP))

                def y_low(gw, o, e, half):
                    E = gw * NE + o + (E0 + e)
                    c = slice(half * 512, half * 512 + 512)
                    dve.wait_ge(S["yhi_sb"], 2 * E + half + 1)
                    dve.tensor_tensor(y_lo[:, e % 2, c], ps[1 + half][:, :], y_hi[:, e % 2, c].bitcast(F32), ALU.subtract)\
                        .then_inc(S["ylo_sb"], 1)

                def step(gw, o, e):
                    E = gw * NE + o + (E0 + e)
                    if e + 1 < NE:
                        low(gw, o, e + 1, 0)
                    if e < NE:
                        dve.wait_ge(S["fold_sb"], E + 1)
                        dve.tensor_tensor(gu[:, :], ps[0][0:CAP, :], fold[:, :], ALU.add).then_inc(S["sum_sb"], 1)
                    if e == 0:
                        dve.wait_ge(S["gates_ps"], gw + 1)
                        dve.tensor_reduce(gate_slot[:, :], ps[1][:, 0:2 * NE].rearrange("p (e m) -> p e m", m=2), AX.X, ALU.add)\
                            .then_inc(S["gs_sb"], 1)
                        dve.wait_ge(S["gs_sb"], gw + 1)
                    if e >= 1:
                        y_low(gw, o, e - 1, 0)
                    if e < NE:
                        dve.wait_ge(S["sil_sb"], E + 1)
                        dve.scalar_tensor_tensor(hbuf[:, :], sil[:, :], gate_slot[0:CAP, bass.ds(o + e, 1)],
                                                 gu[:, FF:2 * FF], ALU.mult, ALU.mult).then_inc(S["h_sb"], 1)
                    if e == 0:
                        for q in range(1, NE // 2, 2):
                            dve.wait_ge(S["pro_ps"], gw * (NE // 2) + (q + 1))
                            dve.tensor_copy(slot_tok[:, 2 * q:2 * q + 2, :],
                                            ps[SLOT_BANKS[q % 3]][:, :].rearrange("p (e t) -> p e t", e=2)).then_inc(S["tok_v"], 1)
                    if e >= 1:
                        y_low(gw, o, e - 1, 1)
                    if e + 1 < NE:
                        up_high(gw, o, e + 1)
                    if e < NE:
                        dve.wait_ge(S["hth_sb"], E + 1)
                        dve.tensor_tensor(hi_lo_h[:, :, 1, :], ps[0][:, 0:FT * CAP].rearrange("p (f c) -> p f c", f=FT),
                                          hi_lo_h[:, :, 0, :].bitcast(F32), ALU.subtract).then_inc(S["htl_sb"], 1)
                    if e + 1 < NE:
                        low(gw, o, e + 1, 1)

                def one_hot_slots(experts):
                    n = experts.stop - experts.start
                    dve.tensor_tensor(disp[:, :, experts, :],
                                      posm[:, :, experts].unsqueeze(3).to_broadcast([P, TT, n, 2 * CAP]),
                                      iota_c[:, :].unsqueeze(1).unsqueeze(1).to_broadcast([P, TT, n, 2 * CAP]), ALU.is_equal)\
                        .then_inc(S["disp_sb"], 1)

                with dve.Fori(g, g1) as gw:
                    dve.wait_ge(S["comb_ps"], gw * NE + E0)
                    one_hot_slots(slice(0, PAIR))
                    one_hot_slots(slice(PAIR, NE))
                    with dve.If(gw > g):
                        low(gw, 0, 0, 0)
                        up_high(gw, 0, 0)
                        low(gw, 0, 0, 1)
                    dve.wait_ge(S["disp_sb"], gw * 2 + 2)
                    dve.tensor_scalar(posm[:, :, :], posm[:, :, :], -float(CAP), None, ALU.add).then_inc(S["win_done"], 1)
                    dve.wait_ge(S["win_done"], gw + 1)
                    for e in range(PEEL):
                        step(gw, 0, e)
                    with dve.Fori(0, (NE - 2 * PEEL) // BODY) as i:
                        o = i * BODY
                        for e in range(PEEL, PEEL + BODY):
                            step(gw, o, e)
                    for e in range(NE - PEEL, NE + 1):
                        step(gw, 0, e)
                return g1

            for name, n in (("up_hi", 2), ("gate_lo", 2), ("up_lo", 2), ("sum_sb", 1), ("htl_sb", 1), ("ylo_sb", 2)):
                dve.nop().then_inc(S[name], E0 * n)
            dve.nop().then_inc(S["h_sb"], E0 - 1)
            g = 0
            for L in range(DEPTH):
                if KINDS[L] == SSD:
                    ssd(L)
                else:
                    attention(L)
                dve.wait_ge(S["tile_used"], tile0(L + 1))
                norm(2 * L)
                g = moe(L, g)
                dve.wait_ge(S["comb_ps"], g * NE + E0)
                norm(2 * L + 1)

        @block.gpsimd
        def _(pool):
            pool.dma_start(x[:], a["x"][0].rearrange("(t p) d -> p t d", p=P)).then_inc(S["x_in"], 16)
            pool.dma_start(w_rt[:, :, :], a["router_w"].rearrange("(p k) e -> p k e", k=KT)).then_inc(S["rt_in"], 16)
            pool.dma_start(rt_bias[:, :], a["router_bias"].rearrange("(o e) -> o e", o=1).to_broadcast([P, NE])).then_inc(S["rt_in"], 16)
            pool.dma_start(sinks[:, :], a["swa_sinks"].to_broadcast([P, AH])).then_inc(S["rt_in"], 16)
            pool.memset(par_rows[:, :, 1, :], 0.0).then_inc(S["pool_step"], 1)
            pool.memset(ident[:, :], 0.0).then_inc(S["consts"], 1)
            pool.memset(ones[:, :], 1.0).then_inc(S["consts"], 1)
            pool.memset(triu[:, :], 1.0).then_inc(S["consts"], 1)
            pool.wait_ge(S["consts"], 3)
            pool.affine_select(out=ident[:, :], in_=ident[:, :], compare_op=ALU.not_equal, fill=1.0, base=0,
                               pattern=[[-1, P]], channel_multiplier=1).then_inc(S["consts"], 1)
            pool.affine_select(out=triu[:, :], in_=triu[:, :], compare_op=ALU.is_ge, fill=0.0, base=0,
                               pattern=[[1, T]], channel_multiplier=-1).then_inc(S["consts"], 1)
            pool.iota(iota_c[:, :], pattern=[[0, 2], [1, CAP]], base=0, channel_multiplier=0, allow_small_or_imprecise_dtypes=True).then_inc(S["consts"], 1)
            pool.iota(rank[:, :], pattern=[[-1, NE]], base=NE, channel_multiplier=0, allow_small_or_imprecise_dtypes=True).then_inc(S["consts"], 1)

            def gains(n):
                if n > 0:
                    pool.wait_ge(S["ln_done"], TT * n)
                g, b = ("ln_mix_g", "ln_mix_b") if n % 2 == 0 else ("ln_ffn_g", "ln_ffn_b")
                for i, w in enumerate((g, b)):
                    pool.dma_start(ln_gb[:, i, :], a[w][n // 2:n // 2 + 1, :].to_broadcast([P, D])).then_inc(S["lngb_in"], 16)

            def ssd(L):
                j = occ[L]
                for h in range(NH):
                    pool.wait_ge(S["dec_sb"], j * NH + h + 1)
                    pool.wait_ge(S["cb_sb"], NG * (j + 1))
                    if h >= HB:
                        pool.wait_ge(S["y_ps"], j * NH + h - HB + 1)
                    pool.tensor_tensor(mm_[:, h % HB, :], dec[:, h % HB, :], cbm[:, h // HPG, :], ALU.mult)\
                        .then_inc(S["m_sb"], 1)

            def mask(rows, b, cols, at):
                pool.memset(bias[rows, b, cols], NEG).then_inc(S["bias_sb"], 1)
                pool.wait_ge(S["bias_sb"], at)

            def swa():
                pool.wait_ge(S["ln_done"], TT * 2)
                pool.iota(lg[:, 0, 0:P], pattern=[[-1, P]], base=0, channel_multiplier=1, allow_small_or_imprecise_dtypes=True)
                pool.iota(lg[:, 0, P:SC], pattern=[[-1, T]], base=P, channel_multiplier=1, allow_small_or_imprecise_dtypes=True).then_inc(S["pool_step"], 1)
                pool.wait_ge(S["pool_step"], 2)
                pool.tensor_scalar(lg[:, 1, :], lg[:, 0, :], 0.0, -2.0, ALU.max, ALU.mult).then_inc(S["pool_step"], 1)
                pool.wait_ge(S["pool_step"], 3)
                pool.tensor_tensor(bias[:, 0, :], lg[:, 0, :], lg[:, 1, :], ALU.add).then_inc(S["pool_step"], 1)
                pool.wait_ge(S["pool_step"], 4)
                mask(slice(0, CH), 0, slice(CH, P), 1)
                mask(slice(0, CH), 0, slice(P + 3 * CH, SC), 2)
                mask(slice(0, P), 0, slice(P, P + CH), 3)
                mask(slice(CH, P), 0, slice(P + CH, P + 2 * CH), 4)

            def ca():
                pool.wait_ge(S["ln_done"], TT * 4)
                pool.dma_start(rel[0:AH, :], a["ca_rel_bias"][0]).then_inc(S["rel_in"], 16)
                for b in range(2):
                    mask(slice(0, CH), b, slice(CH, P), 5 + 2 * b)
                    mask(slice(0, CH), b, slice(P + 3 * CH, SC), 6 + 2 * b)
                pool.wait_ge(S["rev_sb"], 1)
                pool.dma_start(rev_dram, revx[0:AH, :].unsqueeze(1).to_broadcast([AH, CH, 384])).then_inc(S["rev_out"], 16)

            def moe(L, g):
                pool.wait_ge(S["nwin_sb"], L + 1)
                g1 = pool.snap(g + pool.value_load(nwin[0:1, 0:1], min_val=1, max_val=T // CAP))
                with pool.Fori(g, g1) as gw:
                    with pool.Fori(0, NE // BODY) as i:
                        for b in range(BODY):
                            for half in range(2):
                                pool.wait_ge(S["down_hi"], (gw * NE + i * BODY) * 2 + (2 * (E0 + b) + half + 1))
                                w, hi, lo = (down_half(t, half)
                                             for t in (ring[:, (b * UPE + 2) % RING, :], w_hi[2][:, :], w_lo[2][:, :]))
                                pool.tensor_tensor(lo, w, hi.bitcast(F32), ALU.subtract).then_inc(S["down_lo"], 1)
                return g1

            pool.nop().then_inc(S["down_lo"], 2 * E0)
            g = 0
            gains(0)
            for L in range(DEPTH):
                if KINDS[L] == SSD:
                    ssd(L)
                elif KINDS[L] == SWA:
                    swa()
                else:
                    ca()
                gains(2 * L + 1)
                g = moe(L, g)
                if L < DEPTH - 1:
                    gains(2 * L + 2)


_INS = ["x", "ssd_w_in", "ssd_conv_w", "ssd_conv_b", "ssd_dt_bias", "ssd_a_log", "ssd_d_skip", "ssd_norm_w", "ssd_w_out",
        "swa_w_in", "swa_sinks", "swa_w_out", "ca_w_in", "ca_rel_bias", "ca_w_out", "router_w", "router_bias",
        "moe_w_gate", "moe_w_up", "moe_w_down", "ln_mix_g", "ln_mix_b", "ln_ffn_g", "ln_ffn_b"]


def kernel(**inputs):
    import numpy as _np
    import concourse.bacc as _bacc
    from concourse import mybir as _mybir
    from concourse.bass_utils import run_bass_kernel_spmd as _run

    nc = _bacc.Bacc("TRN2", target_bir_lowering=False, num_devices=1)
    arrays, aps = {}, {}
    for name in _INS:
        arr = _np.ascontiguousarray(inputs[name])
        arrays[f"in_{name}"] = arr
        aps[name] = nc.dram_tensor(f"in_{name}", arr.shape, _mybir.dt.from_np(arr.dtype), kind="ExternalInput").ap()
    out = nc.dram_tensor("out", (T, D), _mybir.dt.float32, kind="ExternalOutput").ap()
    trunk(nc, aps, out)
    r = _run(nc, [arrays], core_ids=[0])
    return r.results[0]["out"].reshape(1, T, D)
```
